# Optimizing a Trainium2 kernel written in Bass

```python
import math
import jax
import jax.numpy as jnp
from jax import lax
import numpy as np

D_MODEL = 1024
BATCH = 1
SEQ = 512
DEPTH = 2

GRID_W = 64
CTX_LEN = 256
N_MIXERS = 4
N_MOD = 9
EPS = 1e-6
ROPE_BASE = 10000.0
Q_BLOCK = 128
NEG_INF = -1e30
D_FF = 2816
POOL_WINDOWS = (2, 4, 8, 16)
POOL_GROUPS = len(POOL_WINDOWS)
POOL_G = D_MODEL // POOL_GROUPS
DIFF_HEADS = 8
DIFF_DH = D_MODEL // (2 * DIFF_HEADS)
MLA_HEADS = 16
MLA_Q_RANK = 384
MLA_KV_RANK = 256
MLA_NOPE = 64
MLA_ROPE = 32
MLA_V = D_MODEL // MLA_HEADS
NA_HEADS = 16
NA_DH = D_MODEL // NA_HEADS
NA_KH = 8
NA_KW = 16

kernel_name = 'hybrid_interleaved_dit_ctx_prefix'

def n_layers_of(m):
    return len(range(m, DEPTH, N_MIXERS))

def rms_norm(x, g):
    xf = x.astype(jnp.float32)
    y = xf * lax.rsqrt(jnp.mean(xf * xf, axis=-1, keepdims=True) + EPS)
    return y.astype(x.dtype) * g

def modulate(x, g, shift, scale):
    return rms_norm(x, g) * (1 + scale) + shift

def swiglu(h, w_in, w_out):
    gate, up = jnp.split(h @ w_in, 2, axis=-1)
    return (jax.nn.silu(gate) * up) @ w_out

def ffn_half_step(xs, md, k, g, w_in, w_out):
    h = modulate(xs, g, md[3 * k], md[3 * k + 1])
    return xs + 0.5 * md[3 * k + 2] * swiglu(h, w_in, w_out)

def axial_rope(n_tok, dim, dtype):
    nf = dim // 4
    inv = ROPE_BASE ** (-jnp.arange(nf, dtype=jnp.float32) / nf)
    t = jnp.arange(n_tok, dtype=jnp.int32)
    pos = jnp.stack([t // GRID_W, t % GRID_W], axis=-1).astype(jnp.float32)
    ang = jnp.broadcast_to(pos[:, :, None, None] * inv, (n_tok, 2, 2, nf)).reshape(n_tok, dim)
    return jnp.cos(ang).astype(dtype), jnp.sin(ang).astype(dtype)

def apply_rope(x, cos, sin):
    n, dim = cos.shape
    nf = dim // 4
    xs = x.reshape(x.shape[:-1] + (2, 2, nf))
    rot = jnp.stack([-xs[..., 1, :], xs[..., 0, :]], axis=-2).reshape(x.shape)
    bshape = (n,) + (1,) * (x.ndim - 3) + (dim,)
    return x * cos.reshape(bshape) + rot * sin.reshape(bshape)

def over_query_blocks(fn, q):
    b, s = q.shape[:2]
    nb = s // Q_BLOCK
    qb = jnp.moveaxis(q.reshape((b, nb, Q_BLOCK) + q.shape[2:]), 1, 0)
    out = lax.map(fn, qb)
    return jnp.moveaxis(out, 0, 1).reshape((b, s) + out.shape[3:])

def softmax_attend(q, k, v, scale):
    s = jnp.einsum('bqhd,bkhd->bhqk', q, k).astype(jnp.float32) * scale
    p = jax.nn.softmax(s, axis=-1).astype(v.dtype)
    return jnp.einsum('bhqk,bkhe->bqhe', p, v)

def pool_mix(h, w, b, scale):
    bsz, n, _ = h.shape
    hf = h.astype(jnp.float32).reshape(bsz, n, POOL_GROUPS, POOL_G)
    cs = jnp.concatenate([jnp.zeros_like(hf[:, :1]), jnp.cumsum(hf, axis=1)], axis=1)
    t = jnp.arange(n)[:, None]
    win = jnp.array(POOL_WINDOWS, dtype=jnp.int32)[None, :]
    lo = jnp.clip(t - win // 2, 0, n)
    hi = jnp.clip(t - win // 2 + win, 0, n)
    grp = jnp.arange(POOL_GROUPS)[None, :]
    mean = (cs[:, hi, grp] - cs[:, lo, grp]) / (hi - lo).astype(jnp.float32)[None, :, :, None]
    d = (mean - hf).astype(h.dtype)
    y = jnp.einsum('bngi,gio->bngo', d, w) + b
    return y.reshape(h.shape) * scale

def diff_project(h, w_qkv, qk_g):
    b, n, _ = h.shape
    qkv = (h @ w_qkv).reshape(b, n, 3, DIFF_HEADS, 2, DIFF_DH)
    q = rms_norm(qkv[:, :, 0], qk_g[0])
    k = rms_norm(qkv[:, :, 1], qk_g[1])
    v = qkv[:, :, 2].reshape(b, n, DIFF_HEADS, 2 * DIFF_DH)
    return q, k, v

def diff_attend(q, k, v, lam):
    s = jnp.einsum('bqhcd,bkhcd->bhcqk', q, k).astype(jnp.float32) * (DIFF_DH ** -0.5)
    p = jax.nn.softmax(s, axis=-1)
    a = (p[:, :, 0] - lam * p[:, :, 1]).astype(v.dtype)
    return jnp.einsum('bhqk,bkhe->bqhe', a, v)

def diff_mixer(hl, hc, w_qkv, qk_g, lam_p, sub_g, w_o, lam_init, want_ctx):
    ql, kl, vl = diff_project(hl, w_qkv, qk_g)
    qc, kc, vc = diff_project(hc, w_qkv, qk_g)
    cos, sin = axial_rope(hl.shape[1], DIFF_DH, hl.dtype)
    ql, kl = apply_rope(ql, cos, sin), apply_rope(kl, cos, sin)
    lp = lam_p.astype(jnp.float32)
    lam = jnp.exp(jnp.sum(lp[0] * lp[1])) - jnp.exp(jnp.sum(lp[2] * lp[3])) + lam_init
    k_all = jnp.concatenate([kl, kc], axis=1)
    v_all = jnp.concatenate([vl, vc], axis=1)

    def finish(o):
        o = rms_norm(o, sub_g) * (1.0 - lam_init)
        return o.reshape(o.shape[0], o.shape[1], D_MODEL) @ w_o

    yl = finish(over_query_blocks(lambda qb: diff_attend(qb, k_all, v_all, lam), ql))
    yc = finish(diff_attend(qc, kc, vc, lam)) if want_ctx else None
    return yl, yc

def mla_project(h, w_dq, q_g, w_uq, w_dkv, kv_g, w_ukv, qk_g):
    b, n, _ = h.shape
    q = (rms_norm(h @ w_dq, q_g) @ w_uq).reshape(b, n, MLA_HEADS, MLA_NOPE + MLA_ROPE)
    q = jnp.concatenate([rms_norm(q[..., :MLA_NOPE], qk_g[0, :MLA_NOPE]),
                         rms_norm(q[..., MLA_NOPE:], qk_g[0, MLA_NOPE:])], axis=-1)
    ckv, k_pe = jnp.split(h @ w_dkv, [MLA_KV_RANK], axis=-1)
    kv = (rms_norm(ckv, kv_g) @ w_ukv).reshape(b, n, MLA_HEADS, MLA_NOPE + MLA_V)
    k_nope = rms_norm(kv[..., :MLA_NOPE], qk_g[1, :MLA_NOPE])
    k_pe = rms_norm(k_pe, qk_g[1, MLA_NOPE:])
    return q, k_nope, k_pe, kv[..., MLA_NOPE:]

def mla_attend(q, k_nope, k_pe, v):
    s = (jnp.einsum('bqhd,bkhd->bhqk', q[..., :MLA_NOPE], k_nope)
         + jnp.einsum('bqhr,bkr->bhqk', q[..., MLA_NOPE:], k_pe)).astype(jnp.float32)
    p = jax.nn.softmax(s * ((MLA_NOPE + MLA_ROPE) ** -0.5), axis=-1).astype(v.dtype)
    return jnp.einsum('bhqk,bkhe->bqhe', p, v)

def mla_mixer(hl, hc, w_dq, q_g, w_uq, w_dkv, kv_g, w_ukv, qk_g, w_o, want_ctx):
    ql, kl_nope, kl_pe, vl = mla_project(hl, w_dq, q_g, w_uq, w_dkv, kv_g, w_ukv, qk_g)
    qc, kc_nope, kc_pe, vc = mla_project(hc, w_dq, q_g, w_uq, w_dkv, kv_g, w_ukv, qk_g)
    cos, sin = axial_rope(hl.shape[1], MLA_ROPE, hl.dtype)
    ql = jnp.concatenate([ql[..., :MLA_NOPE], apply_rope(ql[..., MLA_NOPE:], cos, sin)], axis=-1)
    kl_pe = apply_rope(kl_pe, cos, sin)
    k_nope = jnp.concatenate([kl_nope, kc_nope], axis=1)
    k_pe = jnp.concatenate([kl_pe, kc_pe], axis=1)
    v = jnp.concatenate([vl, vc], axis=1)
    b, n = hl.shape[:2]
    ol = over_query_blocks(lambda qb: mla_attend(qb, k_nope, k_pe, v), ql)
    yl = ol.reshape(b, n, MLA_HEADS * MLA_V) @ w_o
    yc = None
    if want_ctx:
        yc = mla_attend(qc, kc_nope, kc_pe, vc).reshape(b, hc.shape[1], MLA_HEADS * MLA_V) @ w_o
    return yl, yc

def na_project(h, w_qkv, qk_g):
    b, n, _ = h.shape
    qkv = (h @ w_qkv).reshape(b, n, 3, NA_HEADS, NA_DH)
    return rms_norm(qkv[:, :, 0], qk_g[0]), rms_norm(qkv[:, :, 1], qk_g[1]), qkv[:, :, 2]

def na_mixer(hl, hc, w_qkv, qk_g, rpb, w_o, want_ctx):
    ql, kl, vl = na_project(hl, w_qkv, qk_g)
    qc, kc, vc = na_project(hc, w_qkv, qk_g)
    b, n = hl.shape[:2]
    rows = n // GRID_W
    kh = min(NA_KH, rows)
    scale = NA_DH ** -0.5
    qg = ql.reshape(b, rows, GRID_W, NA_HEADS, NA_DH)
    kg = kl.reshape(b, rows, GRID_W, NA_HEADS, NA_DH)
    vg = vl.reshape(b, rows, GRID_W, NA_HEADS, NA_DH)
    col = jnp.arange(GRID_W)
    col_start = jnp.clip(col - NA_KW // 2, 0, GRID_W - NA_KW)
    col_mask = (col[None, :] >= col_start[:, None]) & (col[None, :] < col_start[:, None] + NA_KW)
    col_idx = jnp.clip(col[None, :] - col[:, None] + NA_KW - 1, 0, 2 * NA_KW - 2)

    def row_block(r):
        rs = jnp.clip(r - kh // 2, 0, rows - kh)
        q_r = lax.dynamic_index_in_dim(qg, r, axis=1, keepdims=False)
        k_r = lax.dynamic_slice_in_dim(kg, rs, kh, axis=1)
        v_r = lax.dynamic_slice_in_dim(vg, rs, kh, axis=1).reshape(b, kh * GRID_W, NA_HEADS, NA_DH)
        s_loc = jnp.einsum('bqhd,bikhd->bhqik', q_r, k_r).astype(jnp.float32) * scale
        row_idx = rs + jnp.arange(kh) - r + NA_KH - 1
        bias = rpb[:, row_idx[None, :, None], col_idx[:, None, :]]
        s_loc = jnp.where(col_mask[:, None, :], s_loc + bias.astype(jnp.float32), NEG_INF)
        s_loc = s_loc.reshape(b, NA_HEADS, GRID_W, kh * GRID_W)
        s_ctx = jnp.einsum('bqhd,bkhd->bhqk', q_r, kc).astype(jnp.float32) * scale
        p = jax.nn.softmax(jnp.concatenate([s_loc, s_ctx], axis=-1), axis=-1).astype(vl.dtype)
        return (jnp.einsum('bhqk,bkhe->bqhe', p[..., :kh * GRID_W], v_r)
                + jnp.einsum('bhqk,bkhe->bqhe', p[..., kh * GRID_W:], vc))

    out = lax.map(row_block, jnp.arange(rows, dtype=jnp.int32))
    yl = jnp.moveaxis(out, 0, 1).reshape(b, n, D_MODEL) @ w_o
    yc = None
    if want_ctx:
        yc = softmax_attend(qc, kc, vc, scale).reshape(b, hc.shape[1], D_MODEL) @ w_o
    return yl, yc

def setup_inputs(seed: int = 0) -> dict:
    key = jax.random.key(seed)
    ks = iter(jax.random.split(key, 40))
    D = D_MODEL

    def nrm(shape, s):
        return jax.random.normal(next(ks), shape, jnp.float32) * s

    def gain(shape):
        return 1.0 + nrm(shape, 0.05)

    nA, nB, nC, nD = (n_layers_of(m) for m in range(N_MIXERS))
    return {
        'x': nrm((BATCH, SEQ, D), 1.0),
        'c': nrm((BATCH, D), 1.0),
        'ctx': nrm((BATCH, CTX_LEN, D), 1.0),
        'c_ctx': nrm((D,), 1.0),
        'ada_w': nrm((DEPTH, D, N_MOD * D), 0.5 * D ** -0.5),
        'ada_b': nrm((DEPTH, N_MOD * D), 0.02),
        'norm_g': gain((DEPTH, 3, D)),
        'ffn_w_in': nrm((DEPTH, 2, D, 2 * D_FF), D ** -0.5),
        'ffn_w_out': nrm((DEPTH, 2, D_FF, D), D_FF ** -0.5),
        'pool_w': nrm((nA, POOL_GROUPS, POOL_G, POOL_G), POOL_G ** -0.5),
        'pool_b': nrm((nA, POOL_GROUPS, POOL_G), 0.02),
        'pool_scale': gain((nA, D)),
        'diff_w_qkv': nrm((nB, D, 3 * D), D ** -0.5),
        'diff_qk_g': gain((nB, 2, DIFF_DH)),
        'diff_lambda': nrm((nB, 4, DIFF_DH), 0.1),
        'diff_sub_g': gain((nB, 2 * DIFF_DH)),
        'diff_w_o': nrm((nB, D, D), D ** -0.5),
        'mla_w_dq': nrm((nC, D, MLA_Q_RANK), D ** -0.5),
        'mla_q_g': gain((nC, MLA_Q_RANK)),
        'mla_w_uq': nrm((nC, MLA_Q_RANK, MLA_HEADS * (MLA_NOPE + MLA_ROPE)), MLA_Q_RANK ** -0.5),
        'mla_w_dkv': nrm((nC, D, MLA_KV_RANK + MLA_ROPE), D ** -0.5),
        'mla_kv_g': gain((nC, MLA_KV_RANK)),
        'mla_w_ukv': nrm((nC, MLA_KV_RANK, MLA_HEADS * (MLA_NOPE + MLA_V)), MLA_KV_RANK ** -0.5),
        'mla_qk_g': gain((nC, 2, MLA_NOPE + MLA_ROPE)),
        'mla_w_o': nrm((nC, MLA_HEADS * MLA_V, D), (MLA_HEADS * MLA_V) ** -0.5),
        'na_w_qkv': nrm((nD, D, 3 * D), D ** -0.5),
        'na_qk_g': gain((nD, 2, NA_DH)),
        'na_rpb': nrm((nD, NA_HEADS, 2 * NA_KH - 1, 2 * NA_KW - 1), 0.5),
        'na_w_o': nrm((nD, D, D), D ** -0.5),
    }

def reference(x, c, ctx, c_ctx, ada_w, ada_b, norm_g, ffn_w_in, ffn_w_out,
              pool_w, pool_b, pool_scale,
              diff_w_qkv, diff_qk_g, diff_lambda, diff_sub_g, diff_w_o,
              mla_w_dq, mla_q_g, mla_w_uq, mla_w_dkv, mla_kv_g, mla_w_ukv, mla_qk_g, mla_w_o,
              na_w_qkv, na_qk_g, na_rpb, na_w_o):
    xl, xc = x, ctx
    for i in range(DEPTH):
        m, j = i % N_MIXERS, i // N_MIXERS
        want_ctx = i != DEPTH - 1
        ctx_needed = want_ctx or m != 0
        mod_l = jnp.moveaxis((jax.nn.silu(c) @ ada_w[i] + ada_b[i]).reshape(-1, N_MOD, 1, D_MODEL), 1, 0)
        xl = ffn_half_step(xl, mod_l, 0, norm_g[i, 0], ffn_w_in[i, 0], ffn_w_out[i, 0])
        hl = modulate(xl, norm_g[i, 1], mod_l[3], mod_l[4])
        hc = None
        if ctx_needed:
            mod_c = (jax.nn.silu(c_ctx) @ ada_w[i] + ada_b[i]).reshape(N_MOD, 1, D_MODEL)
            xc = ffn_half_step(xc, mod_c, 0, norm_g[i, 0], ffn_w_in[i, 0], ffn_w_out[i, 0])
            hc = modulate(xc, norm_g[i, 1], mod_c[3], mod_c[4])
        if m == 0:
            yl = pool_mix(hl, pool_w[j], pool_b[j], pool_scale[j])
            yc = pool_mix(hc, pool_w[j], pool_b[j], pool_scale[j]) if want_ctx else None
        elif m == 1:
            yl, yc = diff_mixer(hl, hc, diff_w_qkv[j], diff_qk_g[j], diff_lambda[j], diff_sub_g[j],
                                diff_w_o[j], 0.8 - 0.6 * math.exp(-0.3 * i), want_ctx)
        elif m == 2:
            yl, yc = mla_mixer(hl, hc, mla_w_dq[j], mla_q_g[j], mla_w_uq[j], mla_w_dkv[j], mla_kv_g[j],
                               mla_w_ukv[j], mla_qk_g[j], mla_w_o[j], want_ctx)
        else:
            yl, yc = na_mixer(hl, hc, na_w_qkv[j], na_qk_g[j], na_rpb[j], na_w_o[j], want_ctx)
        xl = xl + mod_l[5] * yl
        xl = ffn_half_step(xl, mod_l, 2, norm_g[i, 2], ffn_w_in[i, 1], ffn_w_out[i, 1])
        if want_ctx:
            xc = xc + mod_c[5] * yc
            xc = ffn_half_step(xc, mod_c, 2, norm_g[i, 2], ffn_w_in[i, 1], ffn_w_out[i, 1])
    return xl


_drawn_inputs = setup_inputs


def setup_inputs(seed=0):
    import zlib

    import numpy as np

    out = dict(_drawn_inputs(seed))
    spreads = {}
    factors = {'pool_b': 8.0,
     'pool_scale': 3.896,
     'diff_qk_g': 7.379,
     'diff_lambda': 3.151,
     'diff_sub_g': 5.537}
    for name, (base, spread) in spreads.items():
        noise = np.random.default_rng([zlib.crc32(name.encode()), seed]).standard_normal(out[name].shape)
        drawn = base * np.exp(spread * noise) if base else spread * noise
        out[name] = jnp.asarray(drawn.astype(out[name].dtype))
    for name, factor in factors.items():
        out[name] = (out[name] * factor).astype(out[name].dtype)
    return out
```

```python
from contextlib import ExitStack

import numpy as np

import concourse.bass as bass
from concourse import mybir

F32 = mybir.dt.float32
F32R = mybir.dt.float32r
ALU = mybir.AluOpType
ACT = mybir.ActivationFunctionType
AX = mybir.AxisListType

P = 128
D = 1024
DC = D // P
NL, NX = 512, 256
NT = NL + NX
GRID_W = 64
D_FF = 2816
FC = D_FF // P
PARTS = 2
FP = FC // PARTS
OUT_PAIRS = DC // 2
PART_PAIRS = FP + OUT_PAIRS
FFN_PAIRS = PARTS * PART_PAIRS
N_MOD = 9
MODC = N_MOD * DC
EPS = 1e-6
WINDOWS = (2, 4, 8, 16)
PAD = max(WINDOWS) // 2
HEADS = 8
DH = D // (2 * HEADS)
DV = 2 * DH
TT = NT // P
QT = NL // P
LAM_INIT = 0.8 - 0.6 * float(np.exp(-0.3 * 1))

PAIR_FFN = (0, FFN_PAIRS + 4, 2 * FFN_PAIRS + 4, 3 * FFN_PAIRS + 8)
PAIR_POOL = FFN_PAIRS
PAIR_WO = 3 * FFN_PAIRS + 4
PAIRS = 4 * FFN_PAIRS + 8

C_ADA_B, C_NORM_G, C_POOL_S, C_COND, C_CTX = 0, 72, 96, 104, 112
C_POOL_B, C_SUB_G = 96, 104
PAR_ROWS = (120, 105)

ADA_COLS = 512
ADA_UNITS = N_MOD * D // ADA_COLS
ADA_CH = ADA_COLS // P


def build(nc, x, ctx_in, c, c_ctx, ada_w, ada_b, norm_g, w_in, w_out, pool_w, pool_b, pool_scale,
          w_qkv, qk_g, lam_p, sub_g, w_o, rope, edge, ident_in, out, debug=None):
    stack = ExitStack()
    with stack:
        def sb(name, shape, dt=F32, on=stack):
            return on.enter_context(nc.sbuf_tensor(name, shape, dt))

        def sem(name):
            return stack.enter_context(nc.semaphore(name))

        xT = sb("xT", [P, DC, NT])
        h_hi = sb("h_hi", [P, DC, NT], F32R)
        h_lo = sb("h_lo", [P, DC, NT], F32R)
        KMAX = 12
        w_raw = sb("w_raw", [P, 2, KMAX * P])
        w_hi = sb("w_hi", [P, 2, KMAX * P], F32R)
        w_lo = sb("w_lo", [P, 2, KMAX * P], F32R)
        ident = sb("ident", [P, P])
        ones = sb("ones", [P, P])
        epsc = sb("epsc", [P, 1])
        par = sb("par", [P, 2, P])
        cs = sb("cs", [P, 2 * DC])
        mod = sb("mod", [P, 2, MODC])
        amul = sb("amul", [P, 3, 2, DC])
        gate = sb("gate", [P, 3, 2, DC])
        pscl = sb("pscl", [P, 2, DC])
        pbia = sb("pbia", [P, 2, DC])
        rope_sb = sb("rope_sb", [P, QT, 2, DH])
        gqk = sb("gqk", [P, 4, DH])
        lam_sb = sb("lam_sb", [P, 4, DH])
        lam_s = sb("lam_s", [P, 4])
        nlam = sb("nlam", [P, 1])
        subg = sb("subg", [P, 1])
        eps4 = sb("eps4", [P, 4])
        nhalf = sb("nhalf", [P, 4])
        ss = sb("ss", [P, 2, 4])
        rr = sb("rr", [P, 2, 4])
        mx = sb("mx", [P, 2])
        nm = sb("nm", [P, 2, 2])
        zz = sb("zz", [P, 2, 2])
        rz = sb("rz", [P, 2])
        edge_sb = sb("edge_sb", [P, len(WINDOWS), 4, PAD])

        ffn = ExitStack()
        a_hi = sb("a_hi", [P, FP, NT], F32R, ffn)
        a_lo = sb("a_lo", [P, FP, NT], F32R, ffn)
        ffn.close()
        a_hi_f32 = a_hi[:].bitcast(F32)
        setup = ExitStack()
        xstage = sb("xstage", [P, TT, D], F32, setup)
        pstage = sb("pstage", [P, 2, P], F32, setup)
        ada_raw = sb("ada_raw", [P, 2, DC, ADA_COLS], F32, setup)
        setup.close()
        pool = ExitStack()
        LINE = PAD + NL + PAD + NX + PAD
        hp = sb("hp", [P, DC, LINE], F32, pool)
        win = sb("win", [P, 2, LINE], F32, pool)
        pt = sb("pt", [P, 2, NT], F32, pool)
        pool.close()
        attn = ExitStack()
        oT = sb("oT", [P, HEADS, NL], F32, attn)
        aT_hi = sb("aT_hi", [P, TT, NL], F32R, attn)
        aT_lo = sb("aT_lo", [P, TT, NL], F32R, attn)
        vs_hi = sb("vs_hi", [P, TT, DV], F32R, attn)
        e = sb("e", [P, 2, 2, NT], F32, attn)
        qT_hi = sb("qT_hi", [P, NL], F32R, attn)
        qT_lo = sb("qT_lo", [P, NL], F32R, attn)
        kT_hi = sb("kT_hi", [P, NT], F32R, attn)
        kT_lo = sb("kT_lo", [P, NT], F32R, attn)
        vs_lo = sb("vs_lo", [P, TT, DV], F32R, attn)
        qkv = sb("qkv", [P, TT, 3 * DV], F32, attn)
        a = sb("a", [P, NT], F32, attn)
        qk_sq = sb("qk_sq", [P, 2, 2 * DV], F32, attn)
        qk_c = sb("qk_c", [P, 2 * DV], F32, attn)
        qk_s = sb("qk_s", [P, 2 * DV], F32, attn)
        attn.close()
        over = ExitStack()
        stack.enter_context(over)
        a_hold = sb("a_hold", [P, 2 * FP * NT], F32, over)
        sil = sb("sil", [P, NT])
        prod = sb("prod", [P, NT])
        sq = sb("sq", [P, 2, NT])
        rs = sb("rs", [P, NT])
        xn = sb("xn", [P, 2, NT])
        hf = prod
        attn_hold = sb("attn_hold", [P, P], F32)

        pu = stack.enter_context(nc.psum_tensor("pu", [P, 4, 512], F32))
        pv = stack.enter_context(nc.psum_tensor("pv", [P, 4, 512], F32))

        def ps(ch, s):
            return pu[:, ch, 0:NL] if s == 0 else pu[:, 2 + ch, 0:NX]

        SEG = (slice(0, NL), slice(NL, NT))

        in_x = sem("in_x")
        in_par = sem("in_par")
        par_z = sem("par_z")
        par_t = sem("par_t")
        par_ready = sem("par_ready")
        cs_ready = sem("cs_ready")
        xt_done = sem("xt_done")
        x_ready = sem("x_ready")
        ada_in = [sem(f"ada_in{i}") for i in range(2)]
        ada_done = sem("ada_done")
        ada_out = sem("ada_out")
        mod_ready = sem("mod_ready")
        mod_step = sem("mod_step")
        raw_ready = [sem(f"raw_ready{i}") for i in range(2)]
        hi_ready = [sem(f"hi_ready{i}") for i in range(2)]
        split_ready = [sem(f"split_ready{i}") for i in range(2)]
        unit_done = [sem(f"unit_done{i}") for i in range(2)]
        psum_used = [sem(f"psum_used{i}") for i in range(2)]
        acthi_ready = sem("acthi_ready")
        act_ready = sem("act_ready")
        sq_ready = sem("sq_ready")
        sq_used = sem("sq_used")
        sd_ready = sem("sd_ready")
        rs_ready = sem("rs_ready")
        xn_ready = sem("xn_ready")
        hf_ready = sem("hf_ready")
        hhi_ready = sem("hhi_ready")
        h_ready = sem("h_ready")
        pad_ready = sem("pad_ready")
        win_step = sem("win_step")
        d_ready = sem("d_ready")
        pt_ready = sem("pt_ready")
        const_ready = sem("const_ready")
        ot_done = sem("ot_done")
        o_ready = [sem(f"o_ready{i}") for i in range(2)]
        out_done = sem("out_done")

        aw_ready = sem("aw_ready")
        aw_hi = sem("aw_hi")
        aw_split = sem("aw_split")
        qkv_done = sem("qkv_done")
        qkv_out = sem("qkv_out")
        qsq_ready = sem("qsq_ready")
        ss_ready = sem("ss_ready")
        rr_ready = sem("rr_ready")
        rr_step = sem("rr_step")
        qk_step = sem("qk_step")
        qk_ready = sem("qk_ready")
        tq_done = sem("tq_done")
        tq_hi = sem("tq_hi")
        tq_split = sem("tq_split")
        v_hi = sem("v_hi")
        v_split = sem("v_split")
        s_done = sem("s_done")
        nm_ready = sem("nm_ready")
        exp_done = sem("exp_done")
        mix_step = sem("mix_step")
        a_ready = sem("a_ready")
        ta_done = sem("ta_done")
        ta_hi = sem("ta_hi")
        ta_split = sem("ta_split")
        pv_done = sem("pv_done")
        oT_ready = sem("oT_ready")
        lam_step = sem("lam_step")
        osq_ready = sem("osq_ready")
        ovar_done = sem("ovar_done")
        osd_ready = sem("osd_ready")
        orc_ready = sem("orc_ready")
        on_ready = sem("on_ready")
        onh_ready = sem("onh_ready")
        on_split = sem("on_split")

        aw = [t[:].rearrange("p a b -> p (a b)").rearrange("p (k c) -> p k c", k=DC) for t in (w_raw, w_hi, w_lo)]
        HK = NT // 2

        def scores(c):
            return pu[:, 2 * c:2 * c + 2, 0:HK]

        N_PAR = 17
        TQ = (("q", 0, QT), ("k", 0, QT), ("k", QT, TT))

        def wslot(t, ch, k):
            return t[:, ch, 0:k * P].rearrange("p (k c) -> p k c", k=k)

        NORM_LAYER = (0, 0, 0, 1, 1, 1)
        NORM_K = (0, 1, 2, 0, 1, 2)
        NORM_PREV = (None, PAIR_FFN[0] + FFN_PAIRS, PAIR_POOL + 4, PAIR_FFN[1] + FFN_PAIRS,
                     PAIR_FFN[2] + FFN_PAIRS, PAIR_WO + 4)
        NORM_N = (NT, NT, NT, NT, NT, NL)
        FFN_N = (NT, NT, NT, NL)

        block = stack.enter_context(nc.Block())

        @block.sync
        def _(sp):
            xr = x.rearrange("b (t p) d -> p (b t) d", p=P)
            cr = ctx_in.rearrange("b (t p) d -> p (b t) d", p=P)
            sp.wait_ge(par_z, 1)
            def rows(t, r, a):
                n = a.shape[0]
                sp.dma_start(pstage[r:r + n, t, :], a).then_inc(in_par, 16)
            for L in range(2):
                rows(L, C_ADA_B, ada_b[L].rearrange("(r q) -> r q", q=P))
                rows(L, C_NORM_G, norm_g[L].rearrange("k (r q) -> (k r) q", q=P))
            rows(0, C_POOL_S, pool_scale.rearrange("a (r q) -> (a r) q", q=P))
            rows(0, C_COND, c.rearrange("a (r q) -> (a r) q", q=P))
            rows(0, C_CTX, c_ctx.rearrange("(r q) -> r q", q=P))
            rows(1, C_POOL_B, pool_b.rearrange("a g (r q) -> (a g r) q", q=P))
            rows(1, C_SUB_G, sub_g)
            sp.dma_start(ident[:], ident_in).then_inc(in_par, 16)
            sp.dma_start(edge_sb[:], edge.rearrange("g s e -> (g s e)").partition_broadcast(P)
                         .rearrange("p (g s e) -> p g s e", g=len(WINDOWS), s=4)).then_inc(in_par, 16)
            sp.dma_start(rope_sb[:], rope.rearrange("t p a d -> p t a d")).then_inc(in_par, 16)
            for i in range(4):
                sp.dma_start(gqk[:, i, :], qk_g[0, i // 2].partition_broadcast(P)).then_inc(in_par, 16)
            sp.dma_start(lam_sb[:], lam_p[0].rearrange("a d -> (a d)").partition_broadcast(P)
                         .rearrange("p (a d) -> p a d", a=4)).then_inc(in_par, 16)
            sp.dma_start(xstage[:, 0:QT, :], xr).then_inc(in_x, 16)
            sp.dma_start(xstage[:, QT:TT, :], cr).then_inc(in_x, 16)

            def load_ada(L):
                src = ada_w[L].rearrange("(k p) (u n) -> p k u n", p=P, n=ADA_COLS)
                with sp.Fori(0, ADA_UNITS // 2) as i:
                    for b in range(2):
                        sp.wait_ge(ada_done, 2 + L * ADA_UNITS + 2 * i + b - 1)
                        sp.dma_start(ada_raw[:, b], src[:, :, 2 * i + b, :]).then_inc(ada_in[b], 16)

            def load_unit(ch, pair, dst, src):
                sp.wait_ge(split_ready[ch], pair + 1)
                sp.dma_start(dst, src).then_inc(raw_ready[ch], 16)

            def load_ffn(n):
                wi = w_in[n // 2, n % 2].rearrange("(k p) (u n) -> p k u n", p=P, n=P)
                wo = w_out[n // 2, n % 2].rearrange("(q k p) (m n) -> p q k m n", p=P, q=PARTS, n=P)
                with sp.Fori(0, PARTS) as q:
                    with sp.Fori(0, FP) as f:
                        for ch in range(2):
                            load_unit(ch, PAIR_FFN[n] + q * PART_PAIRS + f, wslot(w_raw, ch, DC),
                                      wi[:, :, ch * FC + q * FP + f, :])
                    with sp.Fori(0, OUT_PAIRS) as m:
                        for ch in range(2):
                            load_unit(ch, PAIR_FFN[n] + q * PART_PAIRS + FP + m, wslot(w_raw, ch, FP),
                                      wo[:, q, :, 2 * m + ch, :])

            load_ada(0)
            load_ffn(0)
            for g in range(4):
                for ch in range(2):
                    load_unit(ch, PAIR_POOL + g, wslot(w_raw, ch, 2),
                              pool_w[0, g].rearrange("(k p) (o n) -> p k o n", p=P, n=P)[:, :, ch, :])
            load_ffn(1)
            sp.wait_ge(unit_done[1], PAIR_FFN[1] + FFN_PAIRS + 1)
            load_ada(1)
            load_ffn(2)
            for ch in range(2):
                sp.wait_ge(split_ready[ch], PAIR_WO + 1)
            wq = w_qkv[0].rearrange("(k p) (j h c) -> p k j h c", p=P, j=3, h=HEADS)
            for h in range(HEADS):
                if h:
                    sp.wait_ge(aw_split, h)
                for j in range(3):
                    sp.dma_start(aw[0][:, :, j * DV:(j + 1) * DV], wq[:, :, j, h, :]).then_inc(aw_ready, 16)
            sp.wait_ge(aw_split, HEADS)
            for m in range(4):
                for ch in range(2):
                    load_unit(ch, PAIR_WO + m, wslot(w_raw, ch, DC),
                              w_o[0].rearrange("(k p) (m n) -> p k m n", p=P, n=P)[:, :, 2 * m + ch, :])
            load_ffn(3)
            for t in range(QT):
                for b in range(2):
                    sp.wait_ge(o_ready[b], t + 1)
                sp.dma_start(out.rearrange("b (t p) d -> p (b t) d", p=P)[:, t], xstage[:, t, :]).then_inc(out_done, 16)
            sp.wait_ge(out_done, 16 * QT)

        @block.gpsimd
        def _(gp):
            nc.gpsimd.memset(pstage[:], 0.0).then_inc(par_z, 1)
            nc.gpsimd.memset(ones[:], 1.0).then_inc(const_ready, 1)
            nc.gpsimd.memset(epsc[:], EPS).then_inc(const_ready, 1)
            nc.gpsimd.memset(eps4[:], EPS).then_inc(const_ready, 1)
            nc.gpsimd.memset(nhalf[:], -0.5).then_inc(const_ready, 1)
            gp.wait_ge(unit_done[1], PAIR_POOL + 1)
            nc.gpsimd.memset(hp[:, :, 0:PAD], 0.0)
            nc.gpsimd.memset(hp[:, :, PAD + NL:2 * PAD + NL], 0.0)
            nc.gpsimd.memset(hp[:, :, LINE - PAD:LINE], 0.0).then_inc(pad_ready, 1)

            def inv_rms(h, base):
                for t in range(TT):
                    n = base + TT * h + t
                    g = slice(0, 4) if t < QT else slice(2, 4)
                    gp.wait_ge(ss_ready, n + 1)
                    nc.gpsimd.tensor_tensor(ss[:, t % 2, g], ss[:, t % 2, g], eps4[:, g], ALU.add).then_inc(rr_step, 1)
                    gp.wait_ge(rr_step, n + 1)
                    nc.gpsimd.tensor_tensor(rr[:, t % 2, g], ss[:, t % 2, g], nhalf[:, g], ALU.pow).then_inc(rr_ready, 1)
            gp.wait_ge(const_ready, 4)
            with gp.Fori(0, HEADS) as h:
                inv_rms(h, 0)

        @block.scalar
        def _(act):
            def split_hi(ch, pair, k):
                act.wait_ge(raw_ready[ch], 16 * (pair + 1))
                act.wait_ge(unit_done[ch], pair + 1)
                act.activation(w_hi[:, ch, 0:k * P], w_raw[:, ch, 0:k * P], ACT.Copy).then_inc(hi_ready[ch], 1)

            def silu_pair(pair, count, f, n, nxt):
                act.wait_ge(unit_done[0], pair + 2)
                for s in range(2 if n == NT else 1):
                    i = act.activation(sil[:, SEG[s]], ps(0, s), ACT.Silu)
                i.then_inc(psum_used[0], 1)
                for ch in range(2):
                    split_hi(ch, pair + 1, nxt)
                act.wait_ge(psum_used[1], pair + 2)
                act.activation(a_hi[:, f, 0:n], prod[:, 0:n], ACT.Copy).then_inc(acthi_ready, 1)

            def ffn_act(k, nxt):
                n = FFN_N[k]
                for q in range(PARTS):
                    b = PAIR_FFN[k] + q * PART_PAIRS
                    with act.Fori(0, FP - 1) as f:
                        silu_pair(b + f, 0, f, n, DC)
                    silu_pair(b + FP - 1, 0, FP - 1, n, FP)
                    with act.Fori(0, OUT_PAIRS - 1) as m:
                        for ch in range(2):
                            split_hi(ch, b + FP + m + 1, FP)
                    for ch in range(2):
                        if q < PARTS - 1 or nxt:
                            split_hi(ch, b + PART_PAIRS, DC if q < PARTS - 1 else nxt)

            def norm_act(i):
                L, k, n = NORM_LAYER[i], NORM_K[i], NORM_N[i]
                segs = 2 if n == NT else 1
                if i == 0:
                    act.wait_ge(x_ready, DC)
                else:
                    for ch in range(2):
                        act.wait_ge(psum_used[ch], NORM_PREV[i] + 1)
                for j in range(DC):
                    if j >= 2:
                        act.wait_ge(sq_used, DC * i + j - 1)
                    elif i:
                        act.wait_ge(sq_used, DC * i)
                    act.activation(sq[:, j % 2, 0:n], xT[:, j, 0:n], ACT.Square).then_inc(sq_ready, 1)
                act.wait_ge(sq_used, DC * (i + 1))
                for s in range(segs):
                    j = act.activation(rs[:, SEG[s]], (pv[:, 0, 0:NL], pv[:, 1, 0:NX])[s], ACT.Sqrt,
                                       scale=1.0 / D, bias=epsc[:])
                j.then_inc(sd_ready, 1)
                act.wait_ge(mod_ready, L + 1)
                for j in range(DC):
                    act.wait_ge(xn_ready, DC * i + j + 1)
                    if k == 1 and L == 0:
                        if j == 0:
                            act.wait_ge(pad_ready, 1)
                        for s, at in ((0, PAD), (1, 2 * PAD + NL)):
                            last = act.activation(hp[:, j, at:at + (NL, NX)[s]], xn[:, j % 2, SEG[s]], ACT.Identity,
                                                  scale=amul[:, k, s, j:j + 1], bias=mod[:, s, 3 * k * DC + j:3 * k * DC + j + 1])
                        last.then_inc(hf_ready, 1)
                        act.wait_ge(d_ready, j + 1)
                    else:
                        if j:
                            act.wait_ge(h_ready, DC * i + j)
                        for s in range(segs):
                            last = act.activation(hf[:, SEG[s]], xn[:, j % 2, SEG[s]], ACT.Identity,
                                                  scale=amul[:, k, s, j:j + 1], bias=mod[:, s, 3 * k * DC + j:3 * k * DC + j + 1])
                        last.then_inc(hf_ready, 1)
                        act.wait_ge(hf_ready, DC * i + j + 1)
                    act.activation(h_hi[:, j, 0:n], hf[:, 0:n], ACT.Copy).then_inc(hhi_ready, 1)

            def project_act(h, t):
                n = TT * h + t
                act.wait_ge(qkv_done, n + 1)
                if not (isinstance(h, int) and h == 0):
                    act.wait_ge(tq_done, 3 * h)
                    act.wait_ge(v_split, h)
                at = 0 if t < QT else DV
                act.activation(qkv[:, t, at:], pv[:, t % 2, at:3 * DV], ACT.Copy).then_inc(qkv_out, 1)
                act.wait_ge(qkv_out, n + 1)
                if n is not None and not (isinstance(h, int) and h == 0 and t < 2):
                    act.wait_ge(ss_ready, n - 1)
                act.activation(qk_sq[:, t % 2, at:2 * DV], qkv[:, t, at:2 * DV], ACT.Square,
                               scale=DH ** -0.5).then_inc(qsq_ready, 1)

            def exp_act(g, i):
                n = QT * g + i
                act.wait_ge(a_ready, n + 1)
                for c in range(2):
                    act.wait_ge(nm_ready, 2 * n + c + 1)
                    act.activation(e[:, i % 2, c, :].rearrange("p (b k) -> p b k", b=2), scores(c), ACT.Exp,
                                   scale=DH ** -0.5, bias=nm[:, i % 2, c:c + 1],
                                   accum_out=zz[:, i % 2, c:c + 1]).then_inc(exp_done, 1)

            def weights_hi(g, i):
                for b in range(2):
                    act.wait_ge(ta_done, 2 * (QT * g + i) + b + 2)
                    act.activation(aT_hi[:, 3 * b:3 * b + 3, i * P:(i + 1) * P],
                                   pv[:, 2 + b, 0:3 * P].rearrange("p (k q) -> p k q", k=3), ACT.Copy).then_inc(ta_hi, 1)

            def head_w_hi(h):
                act.wait_ge(aw_ready, 48 * (h + 1))
                act.activation(aw[1], aw[0], ACT.Copy).then_inc(aw_hi, 1)

            def attn_act(h, do_a, do_b):
                g = h - 1
                for s in range(TT):
                    if do_a:
                        project_act(h, s)
                    if do_b and 1 <= s <= QT:
                        weights_hi(g, s - 1)
                    if do_b and s < QT:
                        exp_act(g, s)
                if do_a:
                    if not (isinstance(h, int) and h == HEADS - 1):
                        act.wait_ge(qkv_done, TT * (h + 1))
                        head_w_hi(h + 1)
                if do_b:
                    act.wait_ge(pv_done, g + 1)
                    act.activation(oT[:, bass.ds(g, 1), :].rearrange("p o q -> p (o q)"), pu[:, 0, :], ACT.Copy).then_inc(oT_ready, 1)
                if do_a:
                    for b, (w, t0, t1) in enumerate(TQ):
                        act.wait_ge(tq_done, 3 * h + b + 1)
                        dst = qT_hi if w == "q" else kT_hi
                        act.activation(dst[:, t0 * P:t1 * P], pv[:, 2 + b % 2, 0:(t1 - t0) * P], ACT.Copy).then_inc(tq_hi, 1)
                    act.activation(vs_hi[:], qkv[:, :, 2 * DV:], ACT.Copy).then_inc(v_hi, 1)

            act.sem_inc(exp_done, 4)
            act.sem_inc(oT_ready, 1)
            act.wait_ge(par_ready, 1)
            act.activation(cs[:], par[:, 0, C_COND:C_COND + 2 * DC], ACT.Silu).then_inc(cs_ready, 1)
            act.wait_ge(const_ready, 4)
            for ch in range(2):
                split_hi(ch, 0, DC)
            norm_act(0)
            ffn_act(0, 2)
            norm_act(1)
            for g in range(4):
                for ch in range(2):
                    split_hi(ch, PAIR_POOL + g + 1, 2 if g < 3 else DC)
                for ch in range(2):
                    act.wait_ge(unit_done[ch], PAIR_POOL + g + 2)
                    if g or ch:
                        act.wait_ge(pt_ready, 2 * g + ch)
                    m = 2 * g + ch
                    for s in range(2):
                        last = act.activation(pt[:, 0, SEG[s]], ps(ch, s), ACT.Identity,
                                              scale=pscl[:, s, m:m + 1], bias=pbia[:, s, m:m + 1])
                    last.then_inc(psum_used[ch], 1)
            act.wait_ge(pt_ready, 2 * 4)
            norm_act(2)
            ffn_act(1, None)
            for ch in range(2):
                split_hi(ch, PAIR_FFN[2], DC)
            norm_act(3)
            ffn_act(2, None)
            act.wait_ge(lam_step, 2)
            act.activation(lam_s[:, 2:4], lam_s[:, 0:2], ACT.Exp).then_inc(lam_step, 1)
            norm_act(4)
            for ch in range(2):
                act.wait_ge(unit_done[ch], PAIR_WO + 1)
            head_w_hi(0)
            attn_act(0, True, False)
            with act.Fori(1, HEADS - 1) as h:
                attn_act(h, True, True)
            attn_act(HEADS - 1, True, True)
            attn_act(HEADS, False, True)
            for h in range(HEADS):
                act.wait_ge(oT_ready, h + 2)
                if h >= 2:
                    act.wait_ge(ovar_done, h - 1)
                act.activation(e[:, h % 2, 0, 0:NL], oT[:, h, :], ACT.Square).then_inc(osq_ready, 1)
            for ch in range(2):
                split_hi(ch, PAIR_WO, DC)
            for h in range(HEADS):
                act.wait_ge(ovar_done, h + 1)
                if h >= 2:
                    act.wait_ge(on_ready, h - 1)
                act.activation(e[:, h % 2, 1, 0:NL], (pu, pv)[h // 4][:, h % 4, :], ACT.Sqrt, scale=1.0 / DV,
                               bias=epsc[:]).then_inc(osd_ready, 1)
                if h:
                    act.wait_ge(on_ready, h)
                    act.activation(h_hi[:, h - 1, 0:NL], oT[:, h - 1, :], ACT.Copy).then_inc(onh_ready, 1)
            act.wait_ge(on_ready, HEADS)
            act.activation(h_hi[:, HEADS - 1, 0:NL], oT[:, HEADS - 1, :], ACT.Copy).then_inc(onh_ready, 1)
            for m in range(OUT_PAIRS):
                for ch in range(2):
                    split_hi(ch, PAIR_WO + m + 1, DC)
            norm_act(5)
            ffn_act(3, None)
            for t in range(QT):
                act.wait_ge(ot_done, 2 * t + 2)
                act.activation(xstage[:, t, 512:1024], pv[:, 2 * (t % 2) + 1, :], ACT.Copy).then_inc(o_ready[1], 1)

        @block.tensor
        def _(pe):
            def unit(ch, pair, k, rhs_hi, rhs_lo, n, acts=None):
                pe.wait_ge(split_ready[ch], pair + 2)
                pe.wait_ge(psum_used[ch], pair + 1)
                hi, lo = wslot(w_hi, ch, k), wslot(w_lo, ch, k)
                if acts is not None:
                    pe.wait_ge(act_ready, acts)
                for j in range(k):
                    if acts is not None and j == k - 1:
                        pe.wait_ge(act_ready, acts + 1)
                    for a, (w, r) in enumerate(((hi, rhs_hi), (hi, rhs_lo), (lo, rhs_hi))):
                        for s in range(2 if n == NT else 1):
                            last = pe.matmul(ps(ch, s), w[:, j, :], r(j)[:, SEG[s]],
                                             start=(j == 0 and a == 0), stop=(j == k - 1 and a == 2))
                last.then_inc(unit_done[ch], 1)

            def ffn_pe(k):
                n = FFN_N[k]
                with pe.Fori(0, PARTS) as q:
                    b = PAIR_FFN[k] + q * PART_PAIRS
                    with pe.Fori(0, FP) as f:
                        for ch in range(2):
                            unit(ch, b + f, DC, lambda j: h_hi[:, j], lambda j: h_lo[:, j], n)
                    with pe.Fori(0, OUT_PAIRS) as m:
                        for ch in range(2):
                            unit(ch, b + FP + m, FP, lambda j: a_hi[:, j], lambda j: a_lo[:, j], n,
                                 acts=k * FC + q * FP + FP)

            def norm_pe(i):
                n = NORM_N[i]
                for j in range(DC):
                    pe.wait_ge(sq_ready, DC * i + j + 1)
                    for s in range(2 if n == NT else 1):
                        last = pe.matmul((pv[:, 0, 0:NL], pv[:, 1, 0:NX])[s], ones[:], sq[:, j % 2, SEG[s]],
                                         start=(j == 0), stop=(j == DC - 1))
                    last.then_inc(sq_used, 1)
                pe.wait_ge(h_ready, DC * (i + 1))

            def ada_pe(L):
                with pe.Fori(0, ADA_UNITS // 2) as i:
                    for b in range(2):
                        pe.wait_ge(ada_in[b], 16 * (L * ADA_UNITS // 2 + i + 1))
                        pe.wait_ge(ada_out, 2 + L * ADA_UNITS + 2 * i + b - 1)
                        for m in range(ADA_CH):
                            for j in range(DC):
                                last = pe.matmul(pv[:, 2 + b, 2 * m:2 * m + 2], ada_raw[:, b, j, m * P:(m + 1) * P],
                                                 cs[:, j::DC], start=(j == 0), stop=(j == DC - 1))
                        last.then_inc(ada_done, 1)

            def project(h, t):
                at = 0 if t < QT else DV
                if t == 0:
                    pe.wait_ge(aw_split, h + 1)
                if not (isinstance(h, int) and h == 0 and t < 2):
                    pe.wait_ge(qkv_out, TT * h + t - 1)
                for j in range(DC):
                    for i, (x_, w_) in enumerate(((h_hi, 1), (h_hi, 2), (h_lo, 1))):
                        last = pe.matmul(pv[:, t % 2, at:3 * DV], x_[:, j, t * P:(t + 1) * P], aw[w_][:, j, at:],
                                         start=(j == 0 and i == 0), stop=(j == DC - 1 and i == 2))
                last.then_inc(qkv_done, 1)

            def score(g, i):
                for c in range(2):
                    pe.wait_ge(exp_done, 2 * (QT * g + i) + c + 3)
                    if i == 0:
                        pe.wait_ge(oT_ready, g + 1)
                    if i == 0:
                        pe.wait_ge(tq_split, 3 * (g + 1))
                    d = slice(c * DH, (c + 1) * DH)
                    for b in range(2):
                        ks = slice(b * HK, (b + 1) * HK)
                        for n, (q_, k_) in enumerate(((qT_hi, kT_hi), (qT_hi, kT_lo), (qT_lo, kT_hi))):
                            last = pe.matmul(pu[:, 2 * c + b, 0:HK], q_[d, i * P:(i + 1) * P], k_[d, ks],
                                             start=(n == 0), stop=(n == 2))
                    last.then_inc(s_done, 1)

            def turn_weights(g, i):
                pe.wait_ge(a_ready, QT * g + i + 3)
                for b in range(2):
                    pe.wait_ge(ta_split, 2 * (QT * g + i) + b + 1)
                    for k in range(3):
                        last = pe.transpose(pv[:, 2 + b, k * P:(k + 1) * P], a[:, (3 * b + k) * P:(3 * b + k + 1) * P], ident[:])
                    last.then_inc(ta_done, 1)

            def values(g):
                pe.wait_ge(ta_split, 2 * QT * (g + 1) + 2)
                pe.wait_ge(v_split, g + 1)
                pe.wait_ge(exp_done, 2 * QT * (g + 1) + 4)
                for k in range(TT):
                    for n, (v_, a_) in enumerate(((vs_hi, aT_hi), (vs_hi, aT_lo), (vs_lo, aT_hi))):
                        last = pe.matmul(pu[:, 0, :], v_[:, k, :], a_[:, k, :], start=(k == 0 and n == 0),
                                         stop=(k == TT - 1 and n == 2))
                last.then_inc(pv_done, 1)

            def turn_qk(h):
                for b, (w, t0, t1) in enumerate(TQ):
                    pe.wait_ge(qk_ready, TT * h + t1)
                    if b == 2:
                        pe.wait_ge(tq_split, 3 * h + 1)
                    for t in range(t0, t1):
                        c0 = 0 if w == "q" else DV
                        last = pe.transpose(pv[:, 2 + b % 2, (t - t0) * P:(t - t0 + 1) * P], qkv[:, t, c0:c0 + DV], ident[:])
                    last.then_inc(tq_done, 1)

            def attn_pe(h, do_a, do_b):
                g = h - 1
                for s in range(TT):
                    if do_a:
                        project(h, s)
                    if do_b and s < QT:
                        score(g, s)
                    if do_b and 1 <= s <= QT:
                        turn_weights(g, s - 1)
                if do_b:
                    values(g)
                if do_a:
                    turn_qk(h)

            for ch in range(2):
                pe.sem_inc(unit_done[ch], 1)
                pe.sem_inc(ada_done, 1)
            pe.sem_inc(ta_done, 1)
            pe.wait_ge(in_par, N_PAR * 16)
            for t in range(2):
                last = pe.transpose(pv[:, 0, t * P:(t + 1) * P], pstage[:, t, :], ident[:])
            last.then_inc(par_t, 1)
            pe.wait_ge(in_x, 32)
            for j in range(DC):
                if j >= 2:
                    pe.wait_ge(x_ready, j - 1)
                for t in range(TT):
                    o = ps(j % 2, 0)[:, t * P:(t + 1) * P] if t < QT else ps(j % 2, 1)[:, (t - QT) * P:(t - QT + 1) * P]
                    last = pe.transpose(o, xstage[:, t, j * P:(j + 1) * P], ident[:])
                last.then_inc(xt_done, 1)
            pe.wait_ge(x_ready, DC)
            pe.wait_ge(cs_ready, 1)
            ada_pe(0)
            norm_pe(0)
            ffn_pe(0)
            norm_pe(1)
            for g in range(4):
                for ch in range(2):
                    unit(ch, PAIR_POOL + g, 2, lambda j: h_hi[:, 2 * g + j], lambda j: h_lo[:, 2 * g + j], NT)
            norm_pe(2)
            ffn_pe(1)
            ada_pe(1)
            norm_pe(3)
            ffn_pe(2)
            norm_pe(4)
            attn_pe(0, True, False)
            with pe.Fori(1, HEADS) as h:
                attn_pe(h, True, True)
            attn_pe(HEADS, False, True)
            pe.wait_ge(oT_ready, HEADS + 1)
            for h in range(HEADS):
                pe.wait_ge(osq_ready, h + 1)
                pe.matmul((pu, pv)[h // 4][:, h % 4, :], ones[:], e[:, h % 2, 0, 0:NL], start=True,
                          stop=True).then_inc(ovar_done, 1)
            pe.wait_ge(osd_ready, HEADS)
            pe.wait_ge(on_split, HEADS)
            for m in range(OUT_PAIRS):
                for ch in range(2):
                    unit(ch, PAIR_WO + m, DC, lambda j: h_hi[:, j], lambda j: h_lo[:, j], NL)
            norm_pe(5)
            ffn_pe(3)
            for ch in range(2):
                pe.wait_ge(psum_used[ch], PAIRS + 1)
            for t in range(QT):
                for b in range(2):
                    if t >= 2:
                        pe.wait_ge(o_ready[b], t - 1)
                    for j in range(4):
                        last = pe.transpose(pv[:, 2 * (t % 2) + b, j * P:(j + 1) * P], xT[:, 4 * b + j, t * P:(t + 1) * P], ident[:])
                    last.then_inc(ot_done, 1)

        @block.vector
        def _(dve):
            def split_lo(ch, pair, k):
                dve.wait_ge(hi_ready[ch], pair + 1)
                dve.tensor_tensor(w_lo[:, ch, 0:k * P], w_raw[:, ch, 0:k * P], w_hi[:, ch, 0:k * P].bitcast(F32),
                                  ALU.subtract).then_inc(split_ready[ch], 1)

            def mul_pair(k, pair, count, f, n, nxt):
                split_lo(0, pair + 1, nxt)
                dve.wait_ge(unit_done[1], pair + 2)
                dve.wait_ge(psum_used[0], pair + 2)
                dve.wait_ge(act_ready, count + 1)
                for s in range(2 if n == NT else 1):
                    last = dve.tensor_tensor(prod[:, SEG[s]], ps(1, s), sil[:, SEG[s]], ALU.mult)
                last.then_inc(psum_used[1], 1)
                split_lo(1, pair + 1, nxt)
                dve.wait_ge(acthi_ready, count + 1)
                dve.tensor_tensor(a_lo[:, f, 0:n], prod[:, 0:n], a_hi_f32[:, f, 0:n],
                                  ALU.subtract).then_inc(act_ready, 1)

            def add_out(ch, pair, m, gk, n):
                dve.wait_ge(unit_done[ch], pair + 2)
                for s in range(2 if n == NT else 1):
                    last = dve.scalar_tensor_tensor(xT[:, m, SEG[s]], ps(ch, s), gate[:, gk, s, m],
                                                    xT[:, m, SEG[s]], ALU.mult, ALU.add)
                last.then_inc(psum_used[ch], 1)

            def ffn_dve(k, nxt):
                n, gk = FFN_N[k], 2 * (k % 2)
                for q in range(PARTS):
                    b = PAIR_FFN[k] + q * PART_PAIRS
                    a = k * FC + q * FP
                    with dve.Fori(0, FP - 1) as f:
                        mul_pair(k, b + f, a + f, f, n, DC)
                    mul_pair(k, b + FP - 1, a + FP - 1, FP - 1, n, FP)
                    with dve.Fori(0, OUT_PAIRS - 1) as m:
                        for ch in range(2):
                            add_out(ch, b + FP + m, bass.ds(2 * m + ch, 1), gk, n)
                            split_lo(ch, b + FP + m + 1, FP)
                    for ch in range(2):
                        add_out(ch, b + PART_PAIRS - 1, slice(DC - 2 + ch, DC - 1 + ch), gk, n)
                        if q < PARTS - 1 or nxt:
                            split_lo(ch, b + PART_PAIRS, DC if q < PARTS - 1 else nxt)

            def norm_dve(i):
                L, k, n = NORM_LAYER[i], NORM_K[i], NORM_N[i]
                dve.wait_ge(sd_ready, i + 1)
                dve.reciprocal(rs[:, 0:n], rs[:, 0:n]).then_inc(rs_ready, 1)
                dve.wait_ge(rs_ready, i + 1)

                def scale(j):
                    if j >= 2:
                        dve.wait_ge(hf_ready, DC * i + j - 1)
                    dve.tensor_tensor(xn[:, j % 2, 0:n], xT[:, j, 0:n], rs[:, 0:n], ALU.mult).then_inc(xn_ready, 1)
                scale(0)
                for j in range(DC):
                    if j + 1 < DC:
                        scale(j + 1)
                    if k == 1 and L == 0:
                        pool_chunk(j)
                    dve.wait_ge(hhi_ready, DC * i + j + 1)
                    dve.tensor_tensor(h_lo[:, j, 0:n], hf[:, 0:n], h_hi[:, j, 0:n].bitcast(F32),
                                      ALU.subtract).then_inc(h_ready, 1)

            steps = [0]

            def pool_chunk(j):
                g = j // 2
                w = WINDOWS[g]
                dve.wait_ge(hf_ready, DC + j + 1)

                def step(i):
                    steps[0] += 1
                    i.then_inc(win_step, 1)
                    dve.wait_ge(win_step, steps[0])
                src, size, length, b = hp[:, j, :], 1, LINE, 0
                while size < w:
                    length -= size
                    step(dve.tensor_tensor(win[:, b, 0:length], src[:, 0:length], src[:, size:size + length], ALU.add))
                    src, b, size = win[:, b, :], 1 - b, 2 * size
                lat, ctx = PAD - w // 2, 2 * PAD + NL - w // 2
                for e, at in enumerate((lat, lat + NL - PAD, ctx, ctx + NX - PAD)):
                    last = dve.tensor_tensor(src[:, at:at + PAD], src[:, at:at + PAD], edge_sb[:, g, e, :], ALU.mult)
                step(last)
                for s, at, to in ((0, lat, PAD), (1, ctx, 2 * PAD + NL)):
                    m = (NL, NX)[s]
                    last = dve.scalar_tensor_tensor(hf[:, SEG[s]], src[:, at:at + m], 1.0 / w, hp[:, j, to:to + m],
                                                    ALU.mult, ALU.subtract)
                last.then_inc(d_ready, 1)

            def mods(L):
                with dve.Fori(0, ADA_UNITS // 2) as i:
                    for b in range(2):
                        dve.wait_ge(ada_done, 3 + L * ADA_UNITS + 2 * i + b)
                        for s in range(2):
                            u = bass.ds((2 * i + b) * ADA_CH, ADA_CH)
                            last = dve.tensor_tensor(mod[:, s, u], pv[:, 2 + b, s:2 * ADA_CH:2], par[:, L, u], ALU.add)
                        last.then_inc(ada_out, 1)
                dve.wait_ge(ada_out, 2 + (L + 1) * ADA_UNITS)
                for s in range(2):
                    for k in range(3):
                        dve.scalar_tensor_tensor(amul[:, k, s, :], mod[:, s, (3 * k + 1) * DC:(3 * k + 2) * DC], 1.0,
                                                 par[:, L, C_NORM_G + k * DC:C_NORM_G + (k + 1) * DC], ALU.add, ALU.mult)
                        last = dve.tensor_scalar(gate[:, k, s, :], mod[:, s, (3 * k + 2) * DC:(3 * k + 3) * DC],
                                                 1.0 if k == 1 else 0.5, None, ALU.mult)
                last.then_inc(mod_step, 1)
                dve.wait_ge(mod_step, 2 * L + 1)
                if L == 0:
                    for s in range(2):
                        dve.tensor_tensor(pscl[:, s, :], gate[:, 1, s, :], par[:, 0, C_POOL_S:C_POOL_S + DC], ALU.mult)
                    last = dve.memset(win[:, 0, 0:2], 0.0)
                    last.then_inc(mod_step, 1)
                    dve.wait_ge(mod_step, 2)
                    for s in range(2):
                        last = dve.tensor_tensor(pbia[:, s, :], pscl[:, s, :], par[:, 1, C_POOL_B:C_POOL_B + DC], ALU.mult)
                last.then_inc(mod_ready, 1) if L == 0 else dve.tensor_copy(pbia[:, 0, 0:1], gate[:, 1, 0, 0:1]).then_inc(mod_ready, 1)

            class Steps:

                def __init__(self, sem_, base):
                    self.sem, self.base, self.n = sem_, base, 0

                def __call__(self, i):
                    self.n += 1
                    i.then_inc(self.sem, 1)
                    dve.wait_ge(self.sem, self.base + self.n)

            def sum_squares(h, t):
                n = TT * h + t
                g = 0 if t < QT else 2
                dve.wait_ge(qsq_ready, n + 1)
                if not (isinstance(h, int) and h == 0 and t < 2):
                    dve.wait_ge(rr_ready, n - 1)
                dve.tensor_reduce(ss[:, t % 2, g:4], qk_sq[:, t % 2, g * DH:2 * DV].rearrange("p (g d) -> p g d", d=DH),
                                  AX.X, ALU.add).then_inc(ss_ready, 1)

            def norm_rope(step, h, t):
                g = 0 if t < QT else 2
                v = qkv[:, t, g * DH:2 * DV].rearrange("p (g d) -> p g d", d=DH)
                dve.wait_ge(rr_ready, TT * h + t + 1)
                step(dve.tensor_tensor(v, v, rr[:, t % 2, g:4].unsqueeze(2).broadcast_to((P, 4 - g, DH)), ALU.mult))
                last = dve.tensor_tensor(v, v, gqk[:, g:4, :], ALU.mult)
                if t < QT:
                    step(last)
                    dve.tensor_tensor(qk_c[:].rearrange("p (g d) -> p g d", d=DH), v,
                                      rope_sb[:, t, 0:1, :].broadcast_to((P, 4, DH)), ALU.mult)
                    x5 = qkv[:, t, 0:2 * DV].rearrange("p (g b d) -> p g b d", b=2, d=DH // 4)
                    s5 = qk_s[:].rearrange("p (g b d) -> p g b d", b=2, d=DH // 4)
                    sn = rope_sb[:, t, 1, :].rearrange("p (a b d) -> p a b d", b=2, d=DH // 4)
                    for b in range(2):
                        for ax in range(2):
                            last = dve.tensor_tensor(s5[:, ax::2, b, :], x5[:, ax::2, 1 - b, :],
                                                     sn[:, ax:ax + 1, b, :].broadcast_to((P, 4, DH // 4)), ALU.mult)
                    step(last)
                    last = dve.tensor_tensor(qkv[:, t, 0:2 * DV], qk_c[:], qk_s[:], ALU.add)
                last.then_inc(qk_ready, 1)

            def row_max(step, g, i):
                for c in range(2):
                    n = 2 * (QT * g + i) + c
                    dve.wait_ge(s_done, n + 1)
                    step(dve.tensor_reduce(mx[:, c:c + 1], scores(c), AX.XY, ALU.max))
                    dve.wait_ge(exp_done, n + 1)
                    dve.tensor_scalar(nm[:, i % 2, c:c + 1], mx[:, c:c + 1], -DH ** -0.5, None, ALU.mult).then_inc(nm_ready, 1)

            def weights_lo(g, i):
                for b in range(2):
                    dve.wait_ge(ta_hi, 2 * (QT * g + i) + b + 1)
                    o = (slice(None), slice(3 * b, 3 * b + 3), slice(i * P, (i + 1) * P))
                    dve.tensor_tensor(aT_lo[o], pv[:, 2 + b, 0:3 * P].rearrange("p (k q) -> p k q", k=3),
                                      aT_hi[o].bitcast(F32), ALU.subtract).then_inc(ta_split, 1)

            def combine(step, g, i):
                n = QT * g + i
                dve.wait_ge(exp_done, 2 * n + 6)
                step(dve.reciprocal(rz[:], zz[:, i % 2, :]))
                step(dve.tensor_tensor(rz[:, 1:2], rz[:, 1:2], nlam[:], ALU.mult))
                step(dve.tensor_scalar(e[:, i % 2, 1, :], e[:, i % 2, 1, :], rz[:, 1:2], None, ALU.mult))
                dve.wait_ge(ta_done, 2 * n + 1)
                dve.scalar_tensor_tensor(a[:], e[:, i % 2, 0, :], rz[:, 0:1], e[:, i % 2, 1, :], ALU.mult,
                                         ALU.add).then_inc(a_ready, 1)
                dve.wait_ge(a_ready, n + 3)

            def head_w_lo(h):
                dve.wait_ge(aw_hi, h + 1)
                dve.tensor_tensor(aw[2], aw[0], aw[1].bitcast(F32), ALU.subtract).then_inc(aw_split, 1)

            A_STEPS = 3 * QT + (TT - QT)
            B_STEPS = 5 * QT

            def attn_dve(h, do_a, do_b):
                g = h - 1
                sa, sb_ = Steps(qk_step, A_STEPS * h), Steps(mix_step, B_STEPS * g)
                for s in range(TT):
                    if do_a:
                        sum_squares(h, s)
                        if s:
                            norm_rope(sa, h, s - 1)
                    if do_b and s < QT:
                        row_max(sb_, g, s)
                    if do_b and 1 <= s <= QT:
                        weights_lo(g, s - 1)
                    if do_b and s < QT:
                        combine(sb_, g, s)
                if do_a:
                    norm_rope(sa, h, TT - 1)
                    if not (isinstance(h, int) and h == HEADS - 1):
                        head_w_lo(h + 1)
                    for b, (w, t0, t1) in enumerate(TQ):
                        dve.wait_ge(tq_hi, 3 * h + b + 1)
                        lo, hi = (qT_lo, qT_hi) if w == "q" else (kT_lo, kT_hi)
                        dve.tensor_tensor(lo[:, t0 * P:t1 * P], pv[:, 2 + b % 2, 0:(t1 - t0) * P],
                                          hi[:, t0 * P:t1 * P].bitcast(F32), ALU.subtract).then_inc(tq_split, 1)
                    dve.wait_ge(v_hi, h + 1)
                    dve.tensor_tensor(vs_lo[:], qkv[:, :, 2 * DV:], vs_hi[:].bitcast(F32), ALU.subtract).then_inc(v_split, 1)

            for ch in range(2):
                dve.sem_inc(split_ready[ch], 1)
                dve.sem_inc(psum_used[ch], 1)
                dve.sem_inc(ada_out, 1)
            dve.sem_inc(act_ready, 1)
            dve.sem_inc(a_ready, 2)
            dve.sem_inc(ta_split, 2)
            dve.wait_ge(par_t, 1)
            dve.tensor_copy(par[:], pv[:, 0, 0:2 * P].rearrange("p (t c) -> p t c", t=2)).then_inc(par_ready, 1)
            for j in range(DC):
                dve.wait_ge(xt_done, j + 1)
                dve.tensor_copy(xT[:, j, 0:NL], ps(j % 2, 0))
                dve.tensor_copy(xT[:, j, NL:NT], ps(j % 2, 1)).then_inc(x_ready, 1)
            dve.wait_ge(par_ready, 1)
            dve.tensor_tensor(lam_sb[:, 0::2, :], lam_sb[:, 0::2, :], lam_sb[:, 1::2, :], ALU.mult).then_inc(lam_step, 1)
            dve.wait_ge(lam_step, 1)
            dve.tensor_reduce(lam_s[:, 0:2], lam_sb[:, 0::2, :], AX.X, ALU.add).then_inc(lam_step, 1)
            dve.tensor_scalar(subg[:], par[:, 1, C_SUB_G:C_SUB_G + 1], 1.0 - LAM_INIT, None, ALU.mult)
            mods(0)
            for ch in range(2):
                split_lo(ch, 0, DC)
            norm_dve(0)
            ffn_dve(0, 2)
            norm_dve(1)
            for g in range(4):
                for ch in range(2):
                    split_lo(ch, PAIR_POOL + g + 1, 2 if g < 3 else DC)
                for ch in range(2):
                    m = 2 * g + ch
                    dve.wait_ge(psum_used[ch], PAIR_POOL + g + 2)
                    dve.tensor_tensor(xT[:, m, :], xT[:, m, :], pt[:, 0, :], ALU.add).then_inc(pt_ready, 1)
            dve.wait_ge(pt_ready, 8)
            norm_dve(2)
            ffn_dve(1, None)
            mods(1)
            for ch in range(2):
                split_lo(ch, PAIR_FFN[2], DC)
            norm_dve(3)
            ffn_dve(2, None)
            dve.wait_ge(lam_step, 3)
            dve.tensor_tensor(nlam[:], lam_s[:, 3:4], lam_s[:, 2:3], ALU.subtract).then_inc(lam_step, 1)
            dve.wait_ge(lam_step, 4)
            dve.tensor_scalar(nlam[:], nlam[:], -LAM_INIT, None, ALU.add).then_inc(lam_step, 1)
            dve.wait_ge(lam_step, 5)
            norm_dve(4)
            head_w_lo(0)
            attn_dve(0, True, False)
            with dve.Fori(1, HEADS - 1) as h:
                attn_dve(h, True, True)
            attn_dve(HEADS - 1, True, True)
            attn_dve(HEADS, False, True)
            for ch in range(2):
                split_lo(ch, PAIR_WO, DC)

            def out_lo(h):
                dve.wait_ge(onh_ready, h + 1)
                dve.tensor_tensor(h_lo[:, h, 0:NL], oT[:, h, :], h_hi[:, h, 0:NL].bitcast(F32), ALU.subtract).then_inc(on_split, 1)
            for h in range(HEADS):
                dve.wait_ge(osd_ready, h + 1)
                r = e[:, h % 2, 1, 0:NL]
                dve.reciprocal(r, r).then_inc(orc_ready, 1)
                dve.wait_ge(orc_ready, h + 1)
                dve.scalar_tensor_tensor(oT[:, h, :], oT[:, h, :], subg[:], r, ALU.mult, ALU.mult).then_inc(on_ready, 1)
                if h:
                    out_lo(h - 1)
            out_lo(HEADS - 1)
            for m in range(OUT_PAIRS):
                for ch in range(2):
                    add_out(ch, PAIR_WO + m, slice(2 * m + ch, 2 * m + ch + 1), 1, NL)
                    split_lo(ch, PAIR_WO + m + 1, DC)
            norm_dve(5)
            ffn_dve(3, None)
            for t in range(QT):
                dve.wait_ge(ot_done, 2 * t + 1)
                dve.tensor_copy(xstage[:, t, 0:512], pv[:, 2 * (t % 2), :]).then_inc(o_ready[0], 1)


_INS = ['x', 'ctx', 'c', 'c_ctx', 'ada_w', 'ada_b', 'norm_g', 'ffn_w_in', 'ffn_w_out', 'pool_w', 'pool_b',
        'pool_scale', 'diff_w_qkv', 'diff_qk_g', 'diff_lambda', 'diff_sub_g', 'diff_w_o']


def shape_constants():
    nf = DH // 4
    inv = (10000.0 ** (-np.arange(nf, dtype=np.float32) / np.float32(nf))).astype(np.float32)
    t = np.arange(NL)
    pos = np.stack([t // GRID_W, t % GRID_W], -1).astype(np.float32)
    ang = np.broadcast_to(pos[:, :, None, None] * inv, (NL, 2, 2, nf)).reshape(NL, DH)
    cos, sin = np.cos(ang).astype(np.float32), np.sin(ang).astype(np.float32)
    sin = sin.reshape(NL, 2, 2, nf) * np.array([-1, 1], np.float32)[:, None]
    rope = np.stack([cos, sin.reshape(NL, DH)], 1).reshape(QT, P, 2, DH)
    edge = np.ones((len(WINDOWS), 4, PAD), np.float32)
    for g, w in enumerate(WINDOWS):
        for s, n in enumerate((NL, NX)):
            t = np.arange(n)
            cnt = np.clip(t - w // 2 + w, 0, n) - np.clip(t - w // 2, 0, n)
            edge[g, 2 * s], edge[g, 2 * s + 1] = w / cnt[:PAD], w / cnt[-PAD:]
    return {'rope': rope.astype(np.float32), 'edge': edge, 'ident': np.eye(P, dtype=np.float32)}


def kernel(**inputs):
    import concourse.bacc as _bacc
    from concourse.bass_utils import run_bass_kernel_spmd as _run

    nc = _bacc.Bacc("TRN2", target_bir_lowering=False, num_devices=1)
    arrays, args = {}, []
    named = [(n, np.ascontiguousarray(inputs[n])) for n in _INS] + list(shape_constants().items())
    for name, a in named:
        arrays[f"in_{name}"] = a
        args.append(nc.dram_tensor(f"in_{name}", a.shape, mybir.dt.from_np(a.dtype), kind="ExternalInput").ap())
    out = nc.dram_tensor("out_0", (1, NL, D), F32, kind="ExternalOutput").ap()
    build(nc, *args, out)
    r = _run(nc, [arrays], core_ids=[0])
    return r.results[0]["out_0"]
```

```python
from contextlib import ExitStack

import numpy as np

import concourse.bass as bass
from concourse import mybir

F32 = mybir.dt.float32
F32R = mybir.dt.float32r
ALU = mybir.AluOpType
ACT = mybir.ActivationFunctionType
AX = mybir.AxisListType

P = 128
D = 1024
DC = D // P
NL, NX = 512, 256
NT = NL + NX
GRID_W = 64
D_FF = 2816
FC = D_FF // P
PARTS = 2
FP = FC // PARTS
OUT_PAIRS = DC // 2
PART_PAIRS = FP + OUT_PAIRS
FFN_PAIRS = PARTS * PART_PAIRS
N_MOD = 9
MODC = N_MOD * DC
EPS = 1e-6
WINDOWS = (2, 4, 8, 16)
PAD = max(WINDOWS) // 2
HEADS = 8
DH = D // (2 * HEADS)
DV = 2 * DH
TT = NT // P
QT = NL // P
LAM_INIT = 0.8 - 0.6 * float(np.exp(-0.3 * 1))

PAIR_FFN = (0, FFN_PAIRS + 4, 2 * FFN_PAIRS + 4, 3 * FFN_PAIRS + 8)
PAIR_POOL = FFN_PAIRS
PAIR_WO = 3 * FFN_PAIRS + 4
PAIRS = 4 * FFN_PAIRS + 8

C_ADA_B, C_NORM_G, C_POOL_S, C_COND, C_CTX = 0, 72, 96, 104, 112
C_POOL_B, C_SUB_G = 96, 104
PAR_ROWS = (120, 105)

ADA_CH = 3
ADA_COLS = ADA_CH * P
ADA_N = MODC // ADA_CH
ADA_FIRST = 2 * DC // ADA_CH + 1
ADA_RING = 3
ADA_COUNT = (ADA_N - ADA_FIRST, ADA_N, 0, 0)
ADA_BASE = (0, ADA_COUNT[0])


def ada_split(k, q, pairs, before):
    return max(0, min(pairs, ADA_COUNT[k] - q * PART_PAIRS - before))


def spans(k, q, pairs, before, start, end=None):
    end = pairs if end is None else end
    n = ada_split(k, q, pairs, before)
    runs = ((start, min(n, end), True), (max(n, start), end, False))
    return [r for r in runs if r[1] > r[0]]


def build(nc, x, ctx_in, c, c_ctx, ada_w, ada_b, norm_g, w_in, w_out, pool_w, pool_b, pool_scale,
          w_qkv, qk_g, lam_p, sub_g, w_o, rope, edge, ident_in, out, debug=None):
    stack = ExitStack()
    with stack:
        def sb(name, shape, dt=F32, on=stack):
            return on.enter_context(nc.sbuf_tensor(name, shape, dt))

        def sem(name):
            return stack.enter_context(nc.semaphore(name))

        xT = sb("xT", [P, DC, NT])
        h_hi = sb("h_hi", [P, DC, NT], F32R)
        h_lo = sb("h_lo", [P, DC, NT], F32R)
        KMAX = 12
        w_raw = sb("w_raw", [P, 2, KMAX * P])
        w_hi = sb("w_hi", [P, 2, KMAX * P], F32R)
        w_lo = sb("w_lo", [P, 2, KMAX * P], F32R)
        ident = sb("ident", [P, P])
        ones = sb("ones", [P, P])
        var = sb("var", [P, TT])
        rms = sb("rms", [P, TT])
        par = sb("par", [P, 2, P])
        cs = sb("cs", [P, 2 * DC])
        mod = sb("mod", [P, 2, MODC])
        amul = sb("amul", [P, 3, 2, DC])
        gate = sb("gate", [P, 3, 2, DC])
        pscl = sb("pscl", [P, 2, DC])
        pbia = sb("pbia", [P, 2, DC])
        rope_sb = sb("rope_sb", [P, QT, 2, DH])
        gqk = sb("gqk", [P, 4, DH])
        lam_sb = sb("lam_sb", [P, 4, DH])
        lam_s = sb("lam_s", [P, 4])
        nlam = sb("nlam", [P, 1])
        subg = sb("subg", [P, 1])
        eps4 = sb("eps4", [P, 4])
        nhalf = sb("nhalf", [P, TT])
        ss = sb("ss", [P, 2, 4])
        rr = sb("rr", [P, 2, 4])
        mx = sb("mx", [P, 2])
        nm = sb("nm", [P, 2, 2])
        zz = sb("zz", [P, 2, 2])
        rz = sb("rz", [P, 2])
        edge_sb = sb("edge_sb", [P, len(WINDOWS), 4, PAD])

        ffn = ExitStack()
        a_hi = sb("a_hi", [P, FP, NT], F32R, ffn)
        a_lo = sb("a_lo", [P, FP, NT], F32R, ffn)
        ffn.close()
        a_hi_f32 = a_hi[:].bitcast(F32)
        setup = ExitStack()
        xstage = sb("xstage", [P, TT, D], F32, setup)
        pstage = sb("pstage", [P, 2, P], F32, setup)
        ada_first = sb("ada_first", [P, ADA_RING, DC, ADA_COLS], F32, setup)
        setup.close()
        pool = ExitStack()
        LINE = PAD + NL + PAD + NX + PAD
        hp = sb("hp", [P, DC, LINE], F32, pool)
        win = sb("win", [P, 2, LINE], F32, pool)
        pt = sb("pt", [P, 2, NT], F32, pool)
        pool.close()
        attn = ExitStack()
        oT = sb("oT", [P, HEADS, NL], F32, attn)
        aT_hi = sb("aT_hi", [P, TT, NL], F32R, attn)
        aT_lo = sb("aT_lo", [P, TT, NL], F32R, attn)
        vs_hi = sb("vs_hi", [P, TT, DV], F32R, attn)
        e = sb("e", [P, 2, 2, NT], F32, attn)
        qT_hi = sb("qT_hi", [P, NL], F32R, attn)
        qT_lo = sb("qT_lo", [P, NL], F32R, attn)
        kT_hi = sb("kT_hi", [P, NT], F32R, attn)
        kT_lo = sb("kT_lo", [P, NT], F32R, attn)
        vs_lo = sb("vs_lo", [P, TT, DV], F32R, attn)
        qkv = sb("qkv", [P, TT, 3 * DV], F32, attn)
        a = sb("a", [P, NT], F32, attn)
        qk_sq = sb("qk_sq", [P, 2, 2 * DV], F32, attn)
        qk_c = sb("qk_c", [P, 2 * DV], F32, attn)
        qk_s = sb("qk_s", [P, 2 * DV], F32, attn)
        attn.close()
        over = ExitStack()
        stack.enter_context(over)
        a_hold = sb("a_hold", [P, 2 * FP * NT], F32, over)
        sil = sb("sil", [P, NT])
        prod = sb("prod", [P, NT])
        ada = ExitStack()
        ada_raw = sb("ada_raw", [P, 2, DC // 2, ADA_COLS], F32, ada)
        ada_acc = sb("ada_acc", [P, 2, ADA_COLS], F32, ada)
        ada.close()
        sq = sb("sq", [P, 2, NT])
        sqa = sb("sqa", [P, NT])
        xn = sb("xn", [P, 2, NT])
        diag = sq[:, 0, :].rearrange("p (t c) -> p t c", c=P)
        hf = prod
        attn_hold = sb("attn_hold", [P, P], F32)

        pu = stack.enter_context(nc.psum_tensor("pu", [P, 4, 512], F32))
        pv = stack.enter_context(nc.psum_tensor("pv", [P, 4, 512], F32))

        def ps(ch, s):
            return pu[:, ch, 0:NL] if s == 0 else pu[:, 2 + ch, 0:NX]

        SEG = (slice(0, NL), slice(NL, NT))

        in_x = [sem(f"in_x{t}") for t in range(TT)]
        in_par = sem("in_par")
        in_par2 = sem("in_par2")
        par_z = sem("par_z")
        par_t = sem("par_t")
        par_ready = sem("par_ready")
        cs_ready = sem("cs_ready")
        xt_done = sem("xt_done")
        x_ready = sem("x_ready")
        first_in = [sem(f"first_in{i}") for i in range(ADA_RING)]
        first_done = sem("first_done")
        ada_in = [sem(f"ada_in{i}") for i in range(2)]
        ada_half = [sem(f"ada_half{i}") for i in range(2)]
        ada_step = sem("ada_step")
        ada_red = sem("ada_red")
        mod_step = sem("mod_step")
        raw_ready = [sem(f"raw_ready{i}") for i in range(2)]
        hi_ready = [sem(f"hi_ready{i}") for i in range(2)]
        split_ready = [sem(f"split_ready{i}") for i in range(2)]
        unit_done = [sem(f"unit_done{i}") for i in range(2)]
        psum_used = [sem(f"psum_used{i}") for i in range(2)]
        acthi_ready = sem("acthi_ready")
        act_ready = sem("act_ready")
        sq_ready = sem("sq_ready")
        sqa_step = sem("sqa_step")
        var_done = sem("var_done")
        var_ready = sem("var_ready")
        rms_ready = sem("rms_ready")
        diag_ready = sem("diag_ready")
        rs_done = sem("rs_done")
        xn_ready = sem("xn_ready")
        hf_ready = sem("hf_ready")
        hhi_ready = sem("hhi_ready")
        h_ready = sem("h_ready")
        pad_ready = sem("pad_ready")
        win_step = sem("win_step")
        d_ready = sem("d_ready")
        pt_ready = sem("pt_ready")
        const_ready = sem("const_ready")
        ot_done = sem("ot_done")
        o_ready = [sem(f"o_ready{i}") for i in range(2)]
        out_done = sem("out_done")

        aw_ready = sem("aw_ready")
        aw_hi = sem("aw_hi")
        aw_split = sem("aw_split")
        qkv_done = sem("qkv_done")
        qkv_out = sem("qkv_out")
        qsq_ready = sem("qsq_ready")
        ss_ready = sem("ss_ready")
        rr_ready = sem("rr_ready")
        rr_step = sem("rr_step")
        qk_step = sem("qk_step")
        qk_ready = sem("qk_ready")
        tq_done = sem("tq_done")
        tq_hi = sem("tq_hi")
        tq_split = sem("tq_split")
        v_hi = sem("v_hi")
        v_split = sem("v_split")
        s_done = sem("s_done")
        nm_ready = sem("nm_ready")
        exp_done = sem("exp_done")
        mix_step = sem("mix_step")
        a_ready = sem("a_ready")
        ta_done = sem("ta_done")
        ta_hi = sem("ta_hi")
        ta_split = sem("ta_split")
        pv_done = sem("pv_done")
        oT_ready = sem("oT_ready")
        lam_step = sem("lam_step")
        osq_ready = sem("osq_ready")
        ostat_done = sem("ostat_done")
        ovar_ready = sem("ovar_ready")
        orms_ready = sem("orms_ready")
        odiag_ready = sem("odiag_ready")
        ors_done = sem("ors_done")
        on_ready = sem("on_ready")
        onh_ready = sem("onh_ready")
        on_split = sem("on_split")

        aw = [t[:].rearrange("p a b -> p (a b)").rearrange("p (k c) -> p k c", k=DC) for t in (w_raw, w_hi, w_lo)]
        HK = NT // 2

        def scores(c):
            return pu[:, 2 * c:2 * c + 2, 0:HK]

        N_PAR, N_PAR2 = 10, 7
        TQ = (("q", 0, QT), ("k", 0, QT), ("k", QT, TT))

        def wslot(t, ch, k):
            return t[:, ch, 0:k * P].rearrange("p (k c) -> p k c", k=k)

        NORM_LAYER = (0, 0, 0, 1, 1, 1)
        NORM_K = (0, 1, 2, 0, 1, 2)
        NORM_N = (NT, NT, NT, NT, NT, NL)
        FFN_N = (NT, NT, NT, NL)
        FFN_NORM = (1, 3, 4)

        block = stack.enter_context(nc.Block())

        @block.sync
        def _(sp):
            xr = x.rearrange("b (t p) d -> p (b t) d", p=P)
            cr = ctx_in.rearrange("b (t p) d -> p (b t) d", p=P)
            for t in range(TT):
                sp.dma_start(xstage[:, t, :], xr[:, t] if t < QT else cr[:, t - QT]).then_inc(in_x[t], 16)
            first = ada_w[0].rearrange("(k p) (u n) -> p k u n", p=P, n=ADA_COLS)
            for u in range(ADA_FIRST):
                if u >= ADA_RING:
                    sp.wait_ge(first_done, u - ADA_RING + 1)
                sp.dma_start(ada_first[:, u % ADA_RING], first[:, :, u, :]).then_inc(first_in[u % ADA_RING], 16)

            def load_granule(k, n):
                src = ada_w[k].rearrange("(b k p) (u n) -> p b k u n", p=P, b=2, n=ADA_COLS)
                u = n + ADA_N - ADA_COUNT[k]
                for b in range(2):
                    sp.wait_ge(ada_half[b], ADA_BASE[k] + n + 1)
                    sp.dma_start(ada_raw[:, b], src[:, b, :, u, :]).then_inc(ada_in[b], 16)

            def load_unit(ch, pair, dst, src):
                sp.wait_ge(split_ready[ch], pair + 1)
                sp.dma_start(dst, src).then_inc(raw_ready[ch], 16)

            def load_ffn(n):
                wi = w_in[n // 2, n % 2].rearrange("(k p) (u n) -> p k u n", p=P, n=P)
                wo = w_out[n // 2, n % 2].rearrange("(q k p) (m n) -> p q k m n", p=P, q=PARTS, n=P)
                def in_pair(q, f, ada):
                    for ch in range(2):
                        load_unit(ch, PAIR_FFN[n] + q * PART_PAIRS + f, wslot(w_raw, ch, DC),
                                  wi[:, :, ch * FC + q * FP + f, :])
                    if ada:
                        load_granule(n, q * PART_PAIRS + f)

                def out_pair(q, m, ada):
                    for ch in range(2):
                        load_unit(ch, PAIR_FFN[n] + q * PART_PAIRS + FP + m, wslot(w_raw, ch, FP),
                                  wo[:, q, :, 2 * m + ch, :])
                    if ada:
                        load_granule(n, q * PART_PAIRS + FP + m)
                for q in range(PARTS):
                    if q == 0 and ADA_COUNT[n]:
                        for ch in range(2):
                            load_unit(ch, PAIR_FFN[n], wslot(w_raw, ch, DC), wi[:, :, ch * FC, :])
                        sp.wait_ge(h_ready, DC * (2 * n + 1))
                        load_granule(n, 0)
                    for lo, hi, ada in spans(n, q, FP, 0, 1 if q == 0 and ADA_COUNT[n] else 0):
                        with sp.Fori(lo, hi) as f:
                            in_pair(q, f, ada)
                    for lo, hi, ada in spans(n, q, OUT_PAIRS, FP, 0):
                        with sp.Fori(lo, hi) as m:
                            out_pair(q, m, ada)

            load_ffn(0)
            for g in range(4):
                for ch in range(2):
                    load_unit(ch, PAIR_POOL + g, wslot(w_raw, ch, 2),
                              pool_w[0, g].rearrange("(k p) (o n) -> p k o n", p=P, n=P)[:, :, ch, :])
            load_ffn(1)
            load_ffn(2)
            for ch in range(2):
                sp.wait_ge(split_ready[ch], PAIR_WO + 1)
            wq = w_qkv[0].rearrange("(k p) (j h c) -> p k j h c", p=P, j=3, h=HEADS)
            for h in range(HEADS):
                if h:
                    sp.wait_ge(aw_split, h)
                for j in range(3):
                    sp.dma_start(aw[0][:, :, j * DV:(j + 1) * DV], wq[:, :, j, h, :]).then_inc(aw_ready, 16)
            sp.wait_ge(aw_split, HEADS)
            for m in range(4):
                for ch in range(2):
                    load_unit(ch, PAIR_WO + m, wslot(w_raw, ch, DC),
                              w_o[0].rearrange("(k p) (m n) -> p k m n", p=P, n=P)[:, :, 2 * m + ch, :])
            load_ffn(3)
            for t in range(QT):
                for b in range(2):
                    sp.wait_ge(o_ready[b], t + 1)
                sp.dma_start(out.rearrange("b (t p) d -> p (b t) d", p=P)[:, t], xstage[:, t, :]).then_inc(out_done, 16)
            sp.wait_ge(out_done, 16 * QT)

        @block.gpsimd
        def _(gp):
            nc.gpsimd.memset(pstage[:], 0.0).then_inc(par_z, 1)
            nc.gpsimd.memset(ones[:], 1.0).then_inc(const_ready, 1)
            nc.gpsimd.memset(eps4[:], EPS).then_inc(const_ready, 1)
            nc.gpsimd.memset(nhalf[:], -0.5).then_inc(const_ready, 1)
            gp.wait_ge(const_ready, 3)

            def sum_chunks(i):
                n = NORM_N[i]

                def add(step, x0, x1):
                    gp.wait_ge(sqa_step, 7 * i + step) if i or step else None
                    nc.gpsimd.tensor_tensor(sqa[:, 0:n], x0, x1, ALU.add).then_inc(sqa_step, 1)
                gp.wait_ge(sq_ready, DC * i + 2)
                add(0, sq[:, 0, 0:n], sq[:, 1, 0:n])
                for m in range(1, DC // 2):
                    for ch in range(2):
                        gp.wait_ge(sq_ready, DC * i + 2 * m + ch + 1)
                        add(2 * m - 1 + ch, sqa[:, 0:n], sq[:, ch, 0:n])
                if i == 1:
                    gp.wait_ge(unit_done[1], PAIR_POOL + 1)
                    nc.gpsimd.memset(hp[:, :, 0:PAD], 0.0)
                    nc.gpsimd.memset(hp[:, :, PAD + NL:2 * PAD + NL], 0.0)
                    nc.gpsimd.memset(hp[:, :, LINE - PAD:LINE], 0.0).then_inc(pad_ready, 1)
                gp.wait_ge(var_ready, i + 1)
                nc.gpsimd.tensor_tensor(rms[:, 0:n // P], var[:, 0:n // P], nhalf[:, 0:n // P], ALU.pow).then_inc(rms_ready, 1)
            sum_chunks(0)
            for i in range(1, 5):
                sum_chunks(i)

            def inv_rms(h):
                for t in range(TT):
                    n = TT * h + t
                    g = slice(0, 4) if t < QT else slice(2, 4)
                    gp.wait_ge(ss_ready, n + 1)
                    nc.gpsimd.tensor_tensor(ss[:, t % 2, g], ss[:, t % 2, g], eps4[:, g], ALU.add).then_inc(rr_step, 1)
                    gp.wait_ge(rr_step, n + 1)
                    nc.gpsimd.tensor_tensor(rr[:, t % 2, g], ss[:, t % 2, g], nhalf[:, g], ALU.pow).then_inc(rr_ready, 1)
            with gp.Fori(0, HEADS) as h:
                inv_rms(h)
            for h in range(HEADS):
                gp.wait_ge(ovar_ready, h + 1)
                nc.gpsimd.tensor_tensor(rr[:, h % 2, :], ss[:, h % 2, :], nhalf[:, 0:QT], ALU.pow).then_inc(orms_ready, 1)
            sum_chunks(5)

        @block.scalar
        def _(act):
            def split_hi(ch, pair, k):
                act.wait_ge(raw_ready[ch], 16 * (pair + 1))
                act.wait_ge(unit_done[ch], pair + 1)
                act.activation(w_hi[:, ch, 0:k * P], w_raw[:, ch, 0:k * P], ACT.Copy).then_inc(hi_ready[ch], 1)

            def silu_pair(pair, f, n, nxt):
                act.wait_ge(unit_done[0], pair + 2)
                for s in range(2 if n == NT else 1):
                    i = act.activation(sil[:, SEG[s]], ps(0, s), ACT.Silu)
                i.then_inc(psum_used[0], 1)
                for ch in range(2):
                    split_hi(ch, pair + 1, nxt)
                act.wait_ge(psum_used[1], pair + 2)
                act.activation(a_hi[:, f, 0:n], prod[:, 0:n], ACT.Copy).then_inc(acthi_ready, 1)

            def square(i, m, ch, chunk):
                n = NORM_N[i]
                if not (isinstance(m, int) and m == 0):
                    act.wait_ge(sqa_step, 7 * i + 2 * m - 1)
                act.activation(sq[:, ch, 0:n], xT[:, chunk, 0:n], ACT.Square).then_inc(sq_ready, 1)

            def square_out(i, pair, m):
                for ch in range(2):
                    act.wait_ge(psum_used[ch], pair + 2)
                    square(i, m, ch, 2 * m + ch if isinstance(m, int) else bass.ds(2 * m + ch, 1))

            def ffn_act(k, nxt):
                n = FFN_N[k]
                for q in range(PARTS):
                    b = PAIR_FFN[k] + q * PART_PAIRS
                    with act.Fori(0, FP - 1) as f:
                        silu_pair(b + f, f, n, DC)
                    silu_pair(b + FP - 1, FP - 1, n, FP)
                    last = q == PARTS - 1
                    squares = last and k < 3
                    for ch in range(2):
                        split_hi(ch, b + FP + 1, FP)
                    if squares:
                        square_out(FFN_NORM[k], b + FP, 0)
                    with act.Fori(1, OUT_PAIRS - 1) as m:
                        for ch in range(2):
                            split_hi(ch, b + FP + m + 1, FP)
                        if squares:
                            square_out(FFN_NORM[k], b + FP + m, m)
                    if nxt or not last:
                        for ch in range(2):
                            split_hi(ch, b + PART_PAIRS, nxt if last else DC)
                    if squares:
                        square_out(FFN_NORM[k], b + PART_PAIRS - 1, OUT_PAIRS - 1)

            def norm_act(i):
                L, k, n = NORM_LAYER[i], NORM_K[i], NORM_N[i]
                segs = 2 if n == NT else 1

                def shift(s, j):
                    return mod[:, s, 3 * k * DC + j:3 * k * DC + j + 1]
                for j in range(DC):
                    act.wait_ge(xn_ready, DC * i + j + 1)
                    if i == 1:
                        if j == 0:
                            act.wait_ge(pad_ready, 1)
                        for s, at in ((0, PAD), (1, 2 * PAD + NL)):
                            last = act.activation(hp[:, j, at:at + (NL, NX)[s]], xn[:, j % 2, SEG[s]], ACT.Identity,
                                                  bias=shift(s, j))
                        last.then_inc(hf_ready, 1)
                        act.wait_ge(d_ready, j + 1)
                        last = act.activation(h_hi[:, j, 0:n], hf[:, 0:n], ACT.Copy)
                    else:
                        for s in range(segs):
                            last = act.activation(h_hi[:, j, SEG[s]], xn[:, j % 2, SEG[s]], ACT.Identity, bias=shift(s, j))
                    last.then_inc(hhi_ready, 1)

            def project_act(h, t):
                n = TT * h + t
                act.wait_ge(qkv_done, n + 1)
                if not (isinstance(h, int) and h == 0):
                    act.wait_ge(tq_done, 3 * h)
                    act.wait_ge(v_split, h)
                at = 0 if t < QT else DV
                act.activation(qkv[:, t, at:], pv[:, t % 2, at:3 * DV], ACT.Copy).then_inc(qkv_out, 1)
                act.wait_ge(qkv_out, n + 1)
                if n is not None and not (isinstance(h, int) and h == 0 and t < 2):
                    act.wait_ge(ss_ready, n - 1)
                act.activation(qk_sq[:, t % 2, at:2 * DV], qkv[:, t, at:2 * DV], ACT.Square,
                               scale=DH ** -0.5).then_inc(qsq_ready, 1)

            def exp_act(g, i):
                n = QT * g + i
                act.wait_ge(a_ready, n + 1)
                for c in range(2):
                    act.wait_ge(nm_ready, 2 * n + c + 1)
                    act.activation(e[:, i % 2, c, :].rearrange("p (b k) -> p b k", b=2), scores(c), ACT.Exp,
                                   scale=DH ** -0.5, bias=nm[:, i % 2, c:c + 1],
                                   accum_out=zz[:, i % 2, c:c + 1]).then_inc(exp_done, 1)

            def weights_hi(g, i):
                for b in range(2):
                    act.wait_ge(ta_done, 2 * (QT * g + i) + b + 2)
                    act.activation(aT_hi[:, 3 * b:3 * b + 3, i * P:(i + 1) * P],
                                   pv[:, 2 + b, 0:3 * P].rearrange("p (k q) -> p k q", k=3), ACT.Copy).then_inc(ta_hi, 1)

            def head_w_hi(h):
                act.wait_ge(aw_ready, 48 * (h + 1))
                act.activation(aw[1], aw[0], ACT.Copy).then_inc(aw_hi, 1)

            def attn_act(h, do_a, do_b):
                g = h - 1
                for s in range(TT):
                    if do_a:
                        project_act(h, s)
                    if do_b and 1 <= s <= QT:
                        weights_hi(g, s - 1)
                    if do_b and s < QT:
                        exp_act(g, s)
                if do_a:
                    if not (isinstance(h, int) and h == HEADS - 1):
                        act.wait_ge(qkv_done, TT * (h + 1))
                        head_w_hi(h + 1)
                if do_b:
                    act.wait_ge(pv_done, g + 1)
                    act.activation(oT[:, bass.ds(g, 1), :].rearrange("p o q -> p (o q)"), pu[:, 0, :], ACT.Copy).then_inc(oT_ready, 1)
                if do_a:
                    for b, (w, t0, t1) in enumerate(TQ):
                        act.wait_ge(tq_done, 3 * h + b + 1)
                        dst = qT_hi if w == "q" else kT_hi
                        act.activation(dst[:, t0 * P:t1 * P], pv[:, 2 + b % 2, 0:(t1 - t0) * P], ACT.Copy).then_inc(tq_hi, 1)
                    act.activation(vs_hi[:], qkv[:, :, 2 * DV:], ACT.Copy).then_inc(v_hi, 1)

            act.wait_ge(par_z, 1)

            def rows(t, r, a_):
                act.dma_start(pstage[r:r + a_.shape[0], t, :], a_).then_inc(in_par, 16)
            rows(0, C_COND, c.rearrange("a (r q) -> (a r) q", q=P))
            rows(0, C_CTX, c_ctx.rearrange("(r q) -> r q", q=P))
            for L in range(2):
                rows(L, C_ADA_B, ada_b[L].rearrange("(r q) -> r q", q=P))
                rows(L, C_NORM_G, norm_g[L].rearrange("k (r q) -> (k r) q", q=P))
            rows(0, C_POOL_S, pool_scale.rearrange("a (r q) -> (a r) q", q=P))
            rows(1, C_POOL_B, pool_b.rearrange("a g (r q) -> (a g r) q", q=P))
            rows(1, C_SUB_G, sub_g)
            act.dma_start(ident[:], ident_in).then_inc(in_par, 16)
            act.dma_start(edge_sb[:], edge.rearrange("g s e -> (g s e)").partition_broadcast(P)
                          .rearrange("p (g s e) -> p g s e", g=len(WINDOWS), s=4)).then_inc(in_par2, 16)
            act.dma_start(rope_sb[:], rope.rearrange("t p a d -> p t a d")).then_inc(in_par2, 16)
            for i in range(4):
                act.dma_start(gqk[:, i, :], qk_g[0, i // 2].partition_broadcast(P)).then_inc(in_par2, 16)
            act.dma_start(lam_sb[:], lam_p[0].rearrange("a d -> (a d)").partition_broadcast(P)
                          .rearrange("p (a d) -> p a d", a=4)).then_inc(in_par2, 16)

            act.sem_inc(exp_done, 4)
            act.sem_inc(oT_ready, 1)
            act.wait_ge(par_ready, 1)
            act.activation(cs[:], par[:, 0, C_COND:C_COND + 2 * DC], ACT.Silu).then_inc(cs_ready, 1)
            for ch in range(2):
                split_hi(ch, 0, DC)
            for m in range(DC // 2):
                for ch in range(2):
                    act.wait_ge(x_ready, 2 * m + ch + 1)
                    square(0, m, ch, 2 * m + ch)
            norm_act(0)
            ffn_act(0, 2)
            norm_act(1)
            for g in range(4):
                for ch in range(2):
                    split_hi(ch, PAIR_POOL + g + 1, 2 if g < 3 else DC)
                for ch in range(2):
                    act.wait_ge(unit_done[ch], PAIR_POOL + g + 2)
                    if g or ch:
                        act.wait_ge(pt_ready, 2 * g + ch)
                    m = 2 * g + ch
                    for s in range(2):
                        last = act.activation(pt[:, 0, SEG[s]], ps(ch, s), ACT.Identity,
                                              scale=pscl[:, s, m:m + 1], bias=pbia[:, s, m:m + 1])
                    last.then_inc(psum_used[ch], 1)
                    if m:
                        square(2, (m - 1) // 2, (m - 1) % 2, m - 1)
            act.wait_ge(pt_ready, DC)
            square(2, DC // 2 - 1, 1, DC - 1)
            norm_act(2)
            ffn_act(1, DC)
            norm_act(3)
            ffn_act(2, None)
            act.wait_ge(lam_step, 2)
            act.activation(lam_s[:, 2:4], lam_s[:, 0:2], ACT.Exp).then_inc(lam_step, 1)
            norm_act(4)
            for ch in range(2):
                act.wait_ge(unit_done[ch], PAIR_WO + 1)
            head_w_hi(0)
            attn_act(0, True, False)
            with act.Fori(1, HEADS - 1) as h:
                attn_act(h, True, True)
            attn_act(HEADS - 1, True, True)
            attn_act(HEADS, False, True)
            for h in range(HEADS + 1):
                if h < HEADS:
                    act.wait_ge(oT_ready, h + 2)
                    if h >= 2:
                        act.wait_ge(ostat_done, h - 1)
                    act.activation(e[:, h % 2, 0, 0:NL], oT[:, h, :], ACT.Square).then_inc(osq_ready, 1)
                if h:
                    act.wait_ge(on_ready, h)
                    act.activation(h_hi[:, h - 1, 0:NL], oT[:, h - 1, :], ACT.Copy).then_inc(onh_ready, 1)
                if h == 1:
                    for ch in range(2):
                        split_hi(ch, PAIR_WO, DC)
            for m in range(OUT_PAIRS):
                for ch in range(2):
                    split_hi(ch, PAIR_WO + m + 1, DC)
                square_out(5, PAIR_WO + m, m)
            norm_act(5)
            ffn_act(3, None)
            for t in range(QT):
                act.wait_ge(ot_done, 2 * t + 2)
                act.activation(xstage[:, t, 512:1024], pv[:, 2 * (t % 2) + 1, :], ACT.Copy).then_inc(o_ready[1], 1)

        @block.tensor
        def _(pe):
            def chunk(ch, j, k, x_hi, x_lo, n):
                hi, lo = wslot(w_hi, ch, k), wslot(w_lo, ch, k)
                for i, (w, r) in enumerate(((hi, x_hi), (hi, x_lo), (lo, x_hi))):
                    for s_ in range(2 if n == NT else 1):
                        last = pe.matmul(ps(ch, s_), w[:, j, :], r[:, SEG[s_]], start=(j == 0 and i == 0),
                                         stop=(j == k - 1 and i == 2))
                return last

            def unit(ch, pair, k, rhs_hi, rhs_lo, n, acts=None):
                pe.wait_ge(split_ready[ch], pair + 2)
                pe.wait_ge(psum_used[ch], pair + 1)
                if acts is not None:
                    pe.wait_ge(act_ready, acts)
                for j in range(k):
                    if acts is not None and j == k - 1:
                        pe.wait_ge(act_ready, acts + 1)
                    last = chunk(ch, j, k, rhs_hi(j), rhs_lo(j), n)
                last.then_inc(unit_done[ch], 1)

            def reduce_granule(k, n):
                c = ADA_BASE[k] + n
                pe.wait_ge(ada_step, DC * c + DC + 1)
                for m in range(ADA_CH):
                    for s_ in range(2):
                        col = 2 * (ADA_CH * (n + ADA_N - ADA_COUNT[k]) + m) + s_
                        last = pe.matmul(pv[:, 2, bass.ds(col, 1)], ada_acc[:, s_, m * P:(m + 1) * P], ones[:, 0:1],
                                         start=True, stop=True)
                last.then_inc(ada_red, 1)

            def ffn_pe(k):
                n = FFN_N[k]
                for q in range(PARTS):
                    b = PAIR_FFN[k] + q * PART_PAIRS
                    first = 0
                    if q == 0:
                        i = (0, 2, 3, 5)[k]
                        for ch in range(2):
                            pe.wait_ge(split_ready[ch], b + 2)
                            pe.wait_ge(psum_used[ch], b + 1)
                        for j in range(DC):
                            pe.wait_ge(h_ready, DC * i + j + 1)
                            for ch in range(2):
                                last = chunk(ch, j, DC, h_hi[:, j], h_lo[:, j], n)
                                if j == DC - 1:
                                    last.then_inc(unit_done[ch], 1)
                        if ADA_COUNT[k]:
                            reduce_granule(k, 0)
                        first = 1
                    for lo, hi, ada in spans(k, q, FP, 0, first):
                        with pe.Fori(lo, hi) as f:
                            for ch in range(2):
                                unit(ch, b + f, DC, lambda j: h_hi[:, j], lambda j: h_lo[:, j], n)
                            if ada:
                                reduce_granule(k, q * PART_PAIRS + f)
                    for lo, hi, ada in spans(k, q, OUT_PAIRS, FP, 0):
                        with pe.Fori(lo, hi) as m:
                            for ch in range(2):
                                unit(ch, b + FP + m, FP, lambda j: a_hi[:, j], lambda j: a_lo[:, j], n,
                                     acts=k * FC + q * FP + FP)
                            if ada:
                                reduce_granule(k, q * PART_PAIRS + FP + m)

            def norm_pe(i):
                n = NORM_N[i]
                pe.wait_ge(sqa_step, 7 * i + 7)
                for t in range(n // P):
                    last = pe.matmul(pv[:, 0, t:t + 1], sqa[:, t * P:(t + 1) * P], ones[:, 0:1], start=True, stop=True)
                last.then_inc(var_done, 1)
                pe.wait_ge(diag_ready, i + 1)
                for s_ in range(2 if n == NT else 1):
                    last = pe.matmul((pv[:, 0, 0:NL], pv[:, 1, 0:NX])[s_], ones[:], sq[:, 0, SEG[s_]], start=True, stop=True)
                last.then_inc(rs_done, 1)

            def ada_first_pe():
                for u in range(ADA_FIRST):
                    pe.wait_ge(first_in[u % ADA_RING], 16 * (u // ADA_RING + 1))
                    for m in range(ADA_CH):
                        for j in range(DC):
                            c0 = 2 * (ADA_CH * u + m)
                            last = pe.matmul(pv[:, 2, c0:c0 + 2], ada_first[:, u % ADA_RING, j, m * P:(m + 1) * P],
                                             cs[:, j::DC], start=(j == 0), stop=(j == DC - 1))
                    last.then_inc(first_done, 1)

            def project(h, t):
                at = 0 if t < QT else DV
                if t == 0:
                    pe.wait_ge(aw_split, h + 1)
                if not (isinstance(h, int) and h == 0 and t < 2):
                    pe.wait_ge(qkv_out, TT * h + t - 1)
                for j in range(DC):
                    for i, (x_, w_) in enumerate(((h_hi, 1), (h_hi, 2), (h_lo, 1))):
                        last = pe.matmul(pv[:, t % 2, at:3 * DV], x_[:, j, t * P:(t + 1) * P], aw[w_][:, j, at:],
                                         start=(j == 0 and i == 0), stop=(j == DC - 1 and i == 2))
                last.then_inc(qkv_done, 1)

            def score(g, i):
                for c in range(2):
                    pe.wait_ge(exp_done, 2 * (QT * g + i) + c + 3)
                    if i == 0:
                        pe.wait_ge(oT_ready, g + 1)
                    if i == 0:
                        pe.wait_ge(tq_split, 3 * (g + 1))
                    d = slice(c * DH, (c + 1) * DH)
                    for b in range(2):
                        ks = slice(b * HK, (b + 1) * HK)
                        for n, (q_, k_) in enumerate(((qT_hi, kT_hi), (qT_hi, kT_lo), (qT_lo, kT_hi))):
                            last = pe.matmul(pu[:, 2 * c + b, 0:HK], q_[d, i * P:(i + 1) * P], k_[d, ks],
                                             start=(n == 0), stop=(n == 2))
                    last.then_inc(s_done, 1)

            def turn_weights(g, i):
                pe.wait_ge(a_ready, QT * g + i + 3)
                for b in range(2):
                    pe.wait_ge(ta_split, 2 * (QT * g + i) + b + 1)
                    for k in range(3):
                        last = pe.transpose(pv[:, 2 + b, k * P:(k + 1) * P], a[:, (3 * b + k) * P:(3 * b + k + 1) * P], ident[:])
                    last.then_inc(ta_done, 1)

            def values(g):
                pe.wait_ge(ta_split, 2 * QT * (g + 1) + 2)
                pe.wait_ge(v_split, g + 1)
                pe.wait_ge(exp_done, 2 * QT * (g + 1) + 4)
                for k in range(TT):
                    for n, (v_, a_) in enumerate(((vs_hi, aT_hi), (vs_hi, aT_lo), (vs_lo, aT_hi))):
                        last = pe.matmul(pu[:, 0, :], v_[:, k, :], a_[:, k, :], start=(k == 0 and n == 0),
                                         stop=(k == TT - 1 and n == 2))
                last.then_inc(pv_done, 1)

            def turn_qk(h):
                for b, (w, t0, t1) in enumerate(TQ):
                    pe.wait_ge(qk_ready, TT * h + t1)
                    if b == 2:
                        pe.wait_ge(tq_split, 3 * h + 1)
                    for t in range(t0, t1):
                        c0 = 0 if w == "q" else DV
                        last = pe.transpose(pv[:, 2 + b % 2, (t - t0) * P:(t - t0 + 1) * P], qkv[:, t, c0:c0 + DV], ident[:])
                    last.then_inc(tq_done, 1)

            def attn_pe(h, do_a, do_b):
                g = h - 1
                for s in range(TT):
                    if do_a:
                        project(h, s)
                    if do_b and s < QT:
                        score(g, s)
                    if do_b and 1 <= s <= QT:
                        turn_weights(g, s - 1)
                if do_b:
                    values(g)
                if do_a:
                    turn_qk(h)

            for ch in range(2):
                pe.sem_inc(unit_done[ch], 1)
            pe.sem_inc(ta_done, 1)
            pe.sem_inc(ada_red, 1)
            pe.wait_ge(in_par, N_PAR * 16)
            for t in range(2):
                last = pe.transpose(pv[:, 0, t * P:(t + 1) * P], pstage[:, t, :], ident[:])
            last.then_inc(par_t, 1)
            for j in range(DC):
                if j >= 2:
                    pe.wait_ge(x_ready, j - 1)
                for t in range(TT):
                    if j == 0:
                        pe.wait_ge(in_x[t], 16)
                    o = ps(j % 2, 0)[:, t * P:(t + 1) * P] if t < QT else ps(j % 2, 1)[:, (t - QT) * P:(t - QT + 1) * P]
                    last = pe.transpose(o, xstage[:, t, j * P:(j + 1) * P], ident[:])
                last.then_inc(xt_done, 1)
            pe.wait_ge(x_ready, DC)
            pe.wait_ge(cs_ready, 1)
            ada_first_pe()
            norm_pe(0)
            ffn_pe(0)
            norm_pe(1)
            pe.wait_ge(h_ready, 2 * DC)
            for g in range(4):
                for ch in range(2):
                    unit(ch, PAIR_POOL + g, 2, lambda j: h_hi[:, 2 * g + j], lambda j: h_lo[:, 2 * g + j], NT)
            norm_pe(2)
            ffn_pe(1)
            norm_pe(3)
            ffn_pe(2)
            norm_pe(4)
            pe.wait_ge(h_ready, 5 * DC)
            attn_pe(0, True, False)
            with pe.Fori(1, HEADS) as h:
                attn_pe(h, True, True)
            attn_pe(HEADS, False, True)
            pe.wait_ge(oT_ready, HEADS + 1)
            for h in range(HEADS + 1):
                if h < HEADS:
                    pe.wait_ge(osq_ready, h + 1)
                    for t in range(QT):
                        last = pe.matmul(pv[:, h % 2, t:t + 1], e[:, h % 2, 0, t * P:(t + 1) * P], ones[:, 0:1],
                                         start=True, stop=True)
                    last.then_inc(ostat_done, 1)
                if h:
                    pe.wait_ge(odiag_ready, h)
                    if h > 2:
                        pe.wait_ge(on_ready, h - 2)
                    pe.matmul(pu[:, (h - 1) % 2, :], ones[:], e[:, (h - 1) % 2, 1, 0:NL], start=True,
                              stop=True).then_inc(ors_done, 1)
            pe.wait_ge(on_ready, HEADS)
            pe.wait_ge(on_split, HEADS)
            for m in range(OUT_PAIRS):
                for ch in range(2):
                    unit(ch, PAIR_WO + m, DC, lambda j: h_hi[:, j], lambda j: h_lo[:, j], NL)
            norm_pe(5)
            ffn_pe(3)
            for ch in range(2):
                pe.wait_ge(psum_used[ch], PAIRS + 1)
            for t in range(QT):
                for b in range(2):
                    if t >= 2:
                        pe.wait_ge(o_ready[b], t - 1)
                    for j in range(4):
                        last = pe.transpose(pv[:, 2 * (t % 2) + b, j * P:(j + 1) * P], xT[:, 4 * b + j, t * P:(t + 1) * P], ident[:])
                    last.then_inc(ot_done, 1)

        @block.vector
        def _(dve):
            def split_lo(ch, pair, k):
                dve.wait_ge(hi_ready[ch], pair + 1)
                dve.tensor_tensor(w_lo[:, ch, 0:k * P], w_raw[:, ch, 0:k * P], w_hi[:, ch, 0:k * P].bitcast(F32),
                                  ALU.subtract).then_inc(split_ready[ch], 1)

            def half_granule(k, n, b):
                c = ADA_BASE[k] + n
                dve.wait_ge(ada_in[b], 16 * (c + 1))
                for i in range(DC // 2):
                    j = b * DC // 2 + i
                    if j == 0:
                        dve.wait_ge(ada_red, c + 1)
                    dve.wait_ge(ada_step, DC * c + j + 1)
                    for s_ in range(2):
                        w = cs[:, s_ * DC + j:s_ * DC + j + 1]
                        if j == 0:
                            last = dve.tensor_scalar(ada_acc[:, s_, :], ada_raw[:, b, i, :], w, None, ALU.mult)
                        else:
                            last = dve.scalar_tensor_tensor(ada_acc[:, s_, :], ada_raw[:, b, i, :], w, ada_acc[:, s_, :],
                                                            ALU.mult, ALU.add)
                    last.then_inc(ada_step, 1)
                dve.wait_ge(ada_step, DC * c + (b + 1) * DC // 2 + 1)
                dve.sem_inc(ada_half[b], 1)

            def mul_pair(k, pair, count, f, n, nxt, granule=None):
                if granule is not None:
                    half_granule(k, granule, 0)
                split_lo(0, pair + 1, nxt)
                if granule is not None:
                    half_granule(k, granule, 1)
                dve.wait_ge(unit_done[1], pair + 2)
                dve.wait_ge(psum_used[0], pair + 2)
                dve.wait_ge(act_ready, count + 1)
                for s in range(2 if n == NT else 1):
                    last = dve.tensor_tensor(prod[:, SEG[s]], ps(1, s), sil[:, SEG[s]], ALU.mult)
                last.then_inc(psum_used[1], 1)
                split_lo(1, pair + 1, nxt)
                dve.wait_ge(acthi_ready, count + 1)
                dve.tensor_tensor(a_lo[:, f, 0:n], prod[:, 0:n], a_hi_f32[:, f, 0:n],
                                  ALU.subtract).then_inc(act_ready, 1)

            def add_out(ch, pair, m, gk, n):
                dve.wait_ge(unit_done[ch], pair + 2)
                for s in range(2 if n == NT else 1):
                    last = dve.scalar_tensor_tensor(xT[:, m, SEG[s]], ps(ch, s), gate[:, gk, s, m],
                                                    xT[:, m, SEG[s]], ALU.mult, ALU.add)
                last.then_inc(psum_used[ch], 1)

            def ffn_dve(k, nxt):
                n, gk = FFN_N[k], 2 * (k % 2)
                for q in range(PARTS):
                    b = PAIR_FFN[k] + q * PART_PAIRS
                    a_ = k * FC + q * FP
                    for lo, hi, ada in spans(k, q, FP, 0, 0, FP - 1):
                        with dve.Fori(lo, hi) as f:
                            mul_pair(k, b + f, a_ + f, f, n, DC, q * PART_PAIRS + f if ada else None)
                    ada = ada_split(k, q, FP, 0) == FP
                    if k == 0 and q == 0:
                        dve.wait_ge(ada_red, FP)
                        add_bias(0, ADA_CH * ADA_FIRST, ADA_CH * (ADA_FIRST + FP - 1))
                        mod_link(gates(0, (0,)))
                    mul_pair(k, b + FP - 1, a_ + FP - 1, FP - 1, n, FP, q * PART_PAIRS + FP - 1 if ada else None)
                    for lo, hi, ada in spans(k, q, OUT_PAIRS, FP, 0, OUT_PAIRS - 1):
                        with dve.Fori(lo, hi) as m:
                            out_pair(k, q, b, m, [bass.ds(2 * m + ch, 1) for ch in range(2)], gk, n, FP, ada)
                    last = q == PARTS - 1
                    ada = ada_split(k, q, OUT_PAIRS, FP) == OUT_PAIRS
                    out_pair(k, q, b, OUT_PAIRS - 1, [slice(DC - 2 + ch, DC - 1 + ch) for ch in range(2)], gk, n,
                             nxt if last else DC, ada)

            def out_pair(k, q, b, m, chunks, gk, n, nxt, ada):
                if ada:
                    half_granule(k, q * PART_PAIRS + FP + m, 0)
                    half_granule(k, q * PART_PAIRS + FP + m, 1)
                for ch in range(2):
                    add_out(ch, b + FP + m, chunks[ch], gk, n)
                    if nxt:
                        split_lo(ch, b + FP + m + 1, nxt)

            def norm_dve(i):
                L, k, n = NORM_LAYER[i], NORM_K[i], NORM_N[i]
                tt = n // P
                dve.wait_ge(var_done, i + 1)
                dve.tensor_scalar(var[:, 0:tt], pv[:, 0, 0:tt], 1.0 / D, EPS, ALU.mult, ALU.add).then_inc(var_ready, 1)
                dve.wait_ge(rms_ready, i + 1)
                dve.tensor_tensor(diag[:, 0:tt], ident[:].unsqueeze(1).broadcast_to((P, tt, P)),
                                  rms[:, 0:tt].unsqueeze(2).broadcast_to((P, tt, P)), ALU.mult).then_inc(diag_ready, 1)
                dve.wait_ge(rs_done, i + 1)
                segs = 2 if n == NT else 1

                def scale(j):
                    if j >= 2:
                        dve.wait_ge(h_ready, DC * i + j - 1)
                    for s_ in range(segs):
                        last = dve.scalar_tensor_tensor(xn[:, j % 2, SEG[s_]], xT[:, j, SEG[s_]], amul[:, k, s_, j:j + 1],
                                                        (pv[:, 0, 0:NL], pv[:, 1, 0:NX])[s_], ALU.mult, ALU.mult)
                    last.then_inc(xn_ready, 1)
                scale(0)
                for j in range(DC):
                    if j + 1 < DC:
                        scale(j + 1)
                    if i == 1:
                        pool_chunk(j)
                    dve.wait_ge(hhi_ready, DC * i + j + 1)
                    if i == 1:
                        last = dve.tensor_tensor(h_lo[:, j, 0:n], hf[:, 0:n], h_hi[:, j, 0:n].bitcast(F32), ALU.subtract)
                    else:
                        for s_ in range(segs):
                            sh = 3 * k * DC + j
                            last = dve.scalar_tensor_tensor(h_lo[:, j, SEG[s_]], xn[:, j % 2, SEG[s_]],
                                                            mod[:, s_, sh:sh + 1], h_hi[:, j, SEG[s_]].bitcast(F32),
                                                            ALU.add, ALU.subtract)
                    last.then_inc(h_ready, 1)

            steps = [0]

            def pool_chunk(j):
                g = j // 2
                w = WINDOWS[g]
                dve.wait_ge(hf_ready, j + 1)

                def step(i):
                    steps[0] += 1
                    i.then_inc(win_step, 1)
                    dve.wait_ge(win_step, steps[0])
                src, size, length, b = hp[:, j, :], 1, LINE, 0
                while size < w:
                    length -= size
                    step(dve.tensor_tensor(win[:, b, 0:length], src[:, 0:length], src[:, size:size + length], ALU.add))
                    src, b, size = win[:, b, :], 1 - b, 2 * size
                lat, ctx = PAD - w // 2, 2 * PAD + NL - w // 2
                for e, at in enumerate((lat, lat + NL - PAD, ctx, ctx + NX - PAD)):
                    last = dve.tensor_tensor(src[:, at:at + PAD], src[:, at:at + PAD], edge_sb[:, g, e, :], ALU.mult)
                step(last)
                for s, at, to in ((0, lat, PAD), (1, ctx, 2 * PAD + NL)):
                    m = (NL, NX)[s]
                    last = dve.scalar_tensor_tensor(hf[:, SEG[s]], src[:, at:at + m], 1.0 / w, hp[:, j, to:to + m],
                                                    ALU.mult, ALU.subtract)
                last.then_inc(d_ready, 1)

            def add_bias(L, c0, c1):
                for s_ in range(2):
                    last = dve.tensor_tensor(mod[:, s_, c0:c1], pv[:, 2, 2 * c0 + s_:2 * c1:2], par[:, L, c0:c1], ALU.add)
                last.then_inc(mod_step, 1)
                mod_steps[0] += 1
                dve.wait_ge(mod_step, mod_steps[0])

            def gates(L, ks):
                for s_ in range(2):
                    for k in ks:
                        last = dve.tensor_scalar(gate[:, k, s_, :], mod[:, s_, (3 * k + 2) * DC:(3 * k + 3) * DC],
                                                 1.0 if k == 1 else 0.5, None, ALU.mult)
                return last

            def scales(L, ks):
                for s_ in range(2):
                    for k in ks:
                        last = dve.scalar_tensor_tensor(amul[:, k, s_, :], mod[:, s_, (3 * k + 1) * DC:(3 * k + 2) * DC], 1.0,
                                                        par[:, L, C_NORM_G + k * DC:C_NORM_G + (k + 1) * DC], ALU.add, ALU.mult)
                return last

            mod_steps = [0]

            def mod_link(i):
                i.then_inc(mod_step, 1)
                mod_steps[0] += 1
                dve.wait_ge(mod_step, mod_steps[0])

            class Steps:

                def __init__(self, sem_, base):
                    self.sem, self.base, self.n = sem_, base, 0

                def __call__(self, i):
                    self.n += 1
                    i.then_inc(self.sem, 1)
                    dve.wait_ge(self.sem, self.base + self.n)

            def sum_squares(h, t):
                n = TT * h + t
                g = 0 if t < QT else 2
                dve.wait_ge(qsq_ready, n + 1)
                if not (isinstance(h, int) and h == 0 and t < 2):
                    dve.wait_ge(rr_ready, n - 1)
                dve.tensor_reduce(ss[:, t % 2, g:4], qk_sq[:, t % 2, g * DH:2 * DV].rearrange("p (g d) -> p g d", d=DH),
                                  AX.X, ALU.add).then_inc(ss_ready, 1)

            def norm_rope(step, h, t):
                g = 0 if t < QT else 2
                v = qkv[:, t, g * DH:2 * DV].rearrange("p (g d) -> p g d", d=DH)
                dve.wait_ge(rr_ready, TT * h + t + 1)
                step(dve.tensor_tensor(v, v, rr[:, t % 2, g:4].unsqueeze(2).broadcast_to((P, 4 - g, DH)), ALU.mult))
                last = dve.tensor_tensor(v, v, gqk[:, g:4, :], ALU.mult)
                if t < QT:
                    step(last)
                    dve.tensor_tensor(qk_c[:].rearrange("p (g d) -> p g d", d=DH), v,
                                      rope_sb[:, t, 0:1, :].broadcast_to((P, 4, DH)), ALU.mult)
                    x5 = qkv[:, t, 0:2 * DV].rearrange("p (g b d) -> p g b d", b=2, d=DH // 4)
                    s5 = qk_s[:].rearrange("p (g b d) -> p g b d", b=2, d=DH // 4)
                    sn = rope_sb[:, t, 1, :].rearrange("p (a b d) -> p a b d", b=2, d=DH // 4)
                    for b in range(2):
                        for ax in range(2):
                            last = dve.tensor_tensor(s5[:, ax::2, b, :], x5[:, ax::2, 1 - b, :],
                                                     sn[:, ax:ax + 1, b, :].broadcast_to((P, 4, DH // 4)), ALU.mult)
                    step(last)
                    last = dve.tensor_tensor(qkv[:, t, 0:2 * DV], qk_c[:], qk_s[:], ALU.add)
                last.then_inc(qk_ready, 1)

            def row_max(step, g, i):
                for c in range(2):
                    n = 2 * (QT * g + i) + c
                    dve.wait_ge(s_done, n + 1)
                    step(dve.tensor_reduce(mx[:, c:c + 1], scores(c), AX.XY, ALU.max))
                    dve.wait_ge(exp_done, n + 1)
                    dve.tensor_scalar(nm[:, i % 2, c:c + 1], mx[:, c:c + 1], -DH ** -0.5, None, ALU.mult).then_inc(nm_ready, 1)

            def weights_lo(g, i):
                for b in range(2):
                    dve.wait_ge(ta_hi, 2 * (QT * g + i) + b + 1)
                    o = (slice(None), slice(3 * b, 3 * b + 3), slice(i * P, (i + 1) * P))
                    dve.tensor_tensor(aT_lo[o], pv[:, 2 + b, 0:3 * P].rearrange("p (k q) -> p k q", k=3),
                                      aT_hi[o].bitcast(F32), ALU.subtract).then_inc(ta_split, 1)

            def combine(step, g, i):
                n = QT * g + i
                dve.wait_ge(exp_done, 2 * n + 6)
                step(dve.reciprocal(rz[:], zz[:, i % 2, :]))
                step(dve.tensor_tensor(rz[:, 1:2], rz[:, 1:2], nlam[:], ALU.mult))
                step(dve.tensor_scalar(e[:, i % 2, 1, :], e[:, i % 2, 1, :], rz[:, 1:2], None, ALU.mult))
                dve.wait_ge(ta_done, 2 * n + 1)
                dve.scalar_tensor_tensor(a[:], e[:, i % 2, 0, :], rz[:, 0:1], e[:, i % 2, 1, :], ALU.mult,
                                         ALU.add).then_inc(a_ready, 1)
                dve.wait_ge(a_ready, n + 3)

            def head_w_lo(h):
                dve.wait_ge(aw_hi, h + 1)
                dve.tensor_tensor(aw[2], aw[0], aw[1].bitcast(F32), ALU.subtract).then_inc(aw_split, 1)

            A_STEPS = 3 * QT + (TT - QT)
            B_STEPS = 5 * QT

            def attn_dve(h, do_a, do_b):
                g = h - 1
                sa, sb_ = Steps(qk_step, A_STEPS * h), Steps(mix_step, B_STEPS * g)
                for s in range(TT):
                    if do_a:
                        sum_squares(h, s)
                        if s:
                            norm_rope(sa, h, s - 1)
                    if do_b and s < QT:
                        row_max(sb_, g, s)
                    if do_b and 1 <= s <= QT:
                        weights_lo(g, s - 1)
                    if do_b and s < QT:
                        combine(sb_, g, s)
                if do_a:
                    norm_rope(sa, h, TT - 1)
                    if not (isinstance(h, int) and h == HEADS - 1):
                        head_w_lo(h + 1)
                    for b, (w, t0, t1) in enumerate(TQ):
                        dve.wait_ge(tq_hi, 3 * h + b + 1)
                        lo, hi = (qT_lo, qT_hi) if w == "q" else (kT_lo, kT_hi)
                        dve.tensor_tensor(lo[:, t0 * P:t1 * P], pv[:, 2 + b % 2, 0:(t1 - t0) * P],
                                          hi[:, t0 * P:t1 * P].bitcast(F32), ALU.subtract).then_inc(tq_split, 1)
                    dve.wait_ge(v_hi, h + 1)
                    dve.tensor_tensor(vs_lo[:], qkv[:, :, 2 * DV:], vs_hi[:].bitcast(F32), ALU.subtract).then_inc(v_split, 1)

            for ch in range(2):
                dve.sem_inc(split_ready[ch], 1)
                dve.sem_inc(psum_used[ch], 1)
                dve.sem_inc(ada_half[ch], 1)
            dve.sem_inc(ada_step, 1)
            dve.sem_inc(act_ready, 1)
            dve.sem_inc(a_ready, 2)
            dve.sem_inc(ta_split, 2)
            dve.wait_ge(par_t, 1)
            dve.tensor_copy(par[:], pv[:, 0, 0:2 * P].rearrange("p (t c) -> p t c", t=2)).then_inc(par_ready, 1)
            for j in range(DC):
                dve.wait_ge(xt_done, j + 1)
                dve.tensor_copy(xT[:, j, 0:NL], ps(j % 2, 0))
                dve.tensor_copy(xT[:, j, NL:NT], ps(j % 2, 1)).then_inc(x_ready, 1)
            dve.wait_ge(par_ready, 1)
            dve.wait_ge(first_done, ADA_FIRST)
            add_bias(0, 0, ADA_CH * ADA_FIRST)
            mod_link(scales(0, (0,)))
            for ch in range(2):
                split_lo(ch, 0, DC)
            norm_dve(0)
            ffn_dve(0, 2)
            dve.wait_ge(ada_red, ADA_COUNT[0] + 1)
            add_bias(0, ADA_CH * (ADA_FIRST + FP - 1), MODC)
            mod_link(scales(0, (1, 2)))
            mod_link(gates(0, (1, 2)))
            for s_ in range(2):
                last = dve.tensor_tensor(pscl[:, s_, :], gate[:, 1, s_, :], par[:, 0, C_POOL_S:C_POOL_S + DC], ALU.mult)
            mod_link(last)
            for s_ in range(2):
                last = dve.tensor_tensor(pbia[:, s_, :], pscl[:, s_, :], par[:, 1, C_POOL_B:C_POOL_B + DC], ALU.mult)
            mod_link(last)
            dve.wait_ge(in_par2, 16 * N_PAR2)
            dve.tensor_tensor(lam_sb[:, 0::2, :], lam_sb[:, 0::2, :], lam_sb[:, 1::2, :], ALU.mult).then_inc(lam_step, 1)
            dve.wait_ge(lam_step, 1)
            dve.tensor_reduce(lam_s[:, 0:2], lam_sb[:, 0::2, :], AX.X, ALU.add).then_inc(lam_step, 1)
            dve.tensor_scalar(subg[:], par[:, 1, C_SUB_G:C_SUB_G + 1], 1.0 - LAM_INIT, None, ALU.mult)
            norm_dve(1)
            for g in range(4):
                for ch in range(2):
                    split_lo(ch, PAIR_POOL + g + 1, 2 if g < 3 else DC)
                for ch in range(2):
                    m = 2 * g + ch
                    dve.wait_ge(psum_used[ch], PAIR_POOL + g + 2)
                    dve.tensor_tensor(xT[:, m, :], xT[:, m, :], pt[:, 0, :], ALU.add).then_inc(pt_ready, 1)
            dve.wait_ge(pt_ready, 8)
            norm_dve(2)
            ffn_dve(1, DC)
            dve.wait_ge(ada_red, ADA_COUNT[0] + ADA_COUNT[1] + 1)
            add_bias(1, 0, MODC)
            mod_link(scales(1, (0, 1, 2)))
            mod_link(gates(1, (0, 1, 2)))
            norm_dve(3)
            ffn_dve(2, None)
            dve.wait_ge(lam_step, 3)
            dve.tensor_tensor(nlam[:], lam_s[:, 3:4], lam_s[:, 2:3], ALU.subtract).then_inc(lam_step, 1)
            dve.wait_ge(lam_step, 4)
            dve.tensor_scalar(nlam[:], nlam[:], -LAM_INIT, None, ALU.add).then_inc(lam_step, 1)
            dve.wait_ge(lam_step, 5)
            norm_dve(4)
            head_w_lo(0)
            attn_dve(0, True, False)
            with dve.Fori(1, HEADS - 1) as h:
                attn_dve(h, True, True)
            attn_dve(HEADS - 1, True, True)
            attn_dve(HEADS, False, True)
            def out_stat(h):
                dve.wait_ge(ostat_done, h + 1)
                dve.tensor_scalar(ss[:, h % 2, :], pv[:, h % 2, 0:QT], 1.0 / DV, EPS, ALU.mult, ALU.add).then_inc(ovar_ready, 1)

            def out_diag(h):
                dve.wait_ge(orms_ready, h + 1)
                if h >= 2:
                    dve.wait_ge(ors_done, h - 1)
                dve.tensor_tensor(e[:, h % 2, 1, 0:NL].rearrange("p (t c) -> p t c", c=P),
                                  ident[:].unsqueeze(1).broadcast_to((P, QT, P)),
                                  rr[:, h % 2, :].unsqueeze(2).broadcast_to((P, QT, P)), ALU.mult).then_inc(odiag_ready, 1)

            def out_norm(h):
                dve.wait_ge(ors_done, h + 1)
                dve.scalar_tensor_tensor(oT[:, h, :], oT[:, h, :], subg[:], pu[:, h % 2, :], ALU.mult,
                                         ALU.mult).then_inc(on_ready, 1)

            def out_lo(h):
                dve.wait_ge(onh_ready, h + 1)
                dve.tensor_tensor(h_lo[:, h, 0:NL], oT[:, h, :], h_hi[:, h, 0:NL].bitcast(F32), ALU.subtract).then_inc(on_split, 1)
            for h in range(HEADS + 2):
                for step, n in ((out_stat, h), (out_diag, h - 1), (out_norm, h - 1), (out_lo, h - 2)):
                    if 0 <= n < HEADS:
                        step(n)
                if h == 2:
                    for ch in range(2):
                        split_lo(ch, PAIR_WO, DC)
            for m in range(OUT_PAIRS):
                for ch in range(2):
                    add_out(ch, PAIR_WO + m, slice(2 * m + ch, 2 * m + ch + 1), 1, NL)
                    split_lo(ch, PAIR_WO + m + 1, DC)
            norm_dve(5)
            ffn_dve(3, None)
            for t in range(QT):
                dve.wait_ge(ot_done, 2 * t + 1)
                dve.tensor_copy(xstage[:, t, 0:512], pv[:, 2 * (t % 2), :]).then_inc(o_ready[0], 1)


_INS = ['x', 'ctx', 'c', 'c_ctx', 'ada_w', 'ada_b', 'norm_g', 'ffn_w_in', 'ffn_w_out', 'pool_w', 'pool_b',
        'pool_scale', 'diff_w_qkv', 'diff_qk_g', 'diff_lambda', 'diff_sub_g', 'diff_w_o']


def shape_constants():
    nf = DH // 4
    inv = (10000.0 ** (-np.arange(nf, dtype=np.float32) / np.float32(nf))).astype(np.float32)
    t = np.arange(NL)
    pos = np.stack([t // GRID_W, t % GRID_W], -1).astype(np.float32)
    ang = np.broadcast_to(pos[:, :, None, None] * inv, (NL, 2, 2, nf)).reshape(NL, DH)
    cos, sin = np.cos(ang).astype(np.float32), np.sin(ang).astype(np.float32)
    sin = sin.reshape(NL, 2, 2, nf) * np.array([-1, 1], np.float32)[:, None]
    rope = np.stack([cos, sin.reshape(NL, DH)], 1).reshape(QT, P, 2, DH)
    edge = np.ones((len(WINDOWS), 4, PAD), np.float32)
    for g, w in enumerate(WINDOWS):
        for s, n in enumerate((NL, NX)):
            t = np.arange(n)
            cnt = np.clip(t - w // 2 + w, 0, n) - np.clip(t - w // 2, 0, n)
            edge[g, 2 * s], edge[g, 2 * s + 1] = w / cnt[:PAD], w / cnt[-PAD:]
    return {'rope': rope.astype(np.float32), 'edge': edge, 'ident': np.eye(P, dtype=np.float32)}


def kernel(**inputs):
    import concourse.bacc as _bacc
    from concourse.bass_utils import run_bass_kernel_spmd as _run

    nc = _bacc.Bacc("TRN2", target_bir_lowering=False, num_devices=1)
    arrays, args = {}, []
    named = [(n, np.ascontiguousarray(inputs[n])) for n in _INS] + list(shape_constants().items())
    for name, a in named:
        arrays[f"in_{name}"] = a
        args.append(nc.dram_tensor(f"in_{name}", a.shape, mybir.dt.from_np(a.dtype), kind="ExternalInput").ap())
    out = nc.dram_tensor("out_0", (1, NL, D), F32, kind="ExternalOutput").ap()
    build(nc, *args, out)
    r = _run(nc, [arrays], core_ids=[0])
    return r.results[0]["out_0"]
```

```python
from contextlib import ExitStack

import numpy as np

import concourse.bass as bass
from concourse import mybir

F32 = mybir.dt.float32
F32R = mybir.dt.float32r
BF16 = mybir.dt.bfloat16
ALU = mybir.AluOpType
ACT = mybir.ActivationFunctionType
AX = mybir.AxisListType

P = 128
D = 1024
DC = D // P
NL, NX = 512, 256
NT = NL + NX
GRID_W = 64
D_FF = 2816
FC = D_FF // P
PARTS = 2
FP = FC // PARTS
OUT_PAIRS = DC // 2
PART_PAIRS = FP + OUT_PAIRS
FFN_PAIRS = PARTS * PART_PAIRS
N_MOD = 9
MODC = N_MOD * DC
EPS = 1e-6
WINDOWS = (2, 4, 8, 16)
PAD = max(WINDOWS) // 2
HEADS = 8
DH = D // (2 * HEADS)
DV = 2 * DH
TT = NT // P
QT = NL // P
LAM_INIT = 0.8 - 0.6 * float(np.exp(-0.3 * 1))

PAIR_FFN = (0, FFN_PAIRS + 4, 2 * FFN_PAIRS + 4, 3 * FFN_PAIRS + 8)
PAIR_POOL = FFN_PAIRS
PAIR_WO = 3 * FFN_PAIRS + 4
PAIRS = 4 * FFN_PAIRS + 8

C_ADA_B, C_NORM_G, C_POOL_S = 0, 72, 96
C_POOL_B, C_SUB_G = 96, 104

ADA_CH = 3
ADA_COLS = ADA_CH * P
ADA_N = MODC // ADA_CH
ADA_FIRST = 2 * DC // ADA_CH + 1
FIRST_DVE = ((1, 0), (3, 0), (5, 0), (4, 2))
FIRST_PE = ((0, ADA_CH), (2, ADA_CH), (4, 2))
ADA_OWN = 2
ADA_COUNT = (ADA_N - ADA_FIRST, ADA_N, 0, 0)
ADA_BASE = (0, ADA_COUNT[0])
PARTS3 = 3
SUM_LAG = 2


def beside(k, pair, lag=1):
    return lag <= pair < lag + ADA_COUNT[k]


def spans(k, before, start, end, lag=1):
    def flags(t):
        return tuple(beside(k, before + t, n) for n in lag) if isinstance(lag, tuple) else beside(k, before + t, lag)
    cuts = [start] + [t for t in range(start + 1, end) if flags(t) != flags(t - 1)] + [end]
    return [(a, b, flags(a)) for a, b in zip(cuts, cuts[1:])]


def build(nc, x, ctx_in, c, c_ctx, ada_w, ada_b, norm_g, w_in, w_out, pool_w, pool_b, pool_scale,
          w_qkv, qk_g, lam_p, sub_g, w_o, rope, edge, ident_in, out):
    stack = ExitStack()
    with stack:
        def sb(name, shape, dt=F32, on=stack):
            return on.enter_context(nc.sbuf_tensor(name, shape, dt))

        def sem(name):
            return stack.enter_context(nc.semaphore(name))

        xT = sb("xT", [P, DC, NT])
        early = ExitStack()
        first_h = sb("first_h", [P, ADA_FIRST - ADA_OWN, DC, ADA_COLS], F32, early)
        early.close()
        late = ExitStack()
        ostage = sb("ostage", [P, QT, D], F32, late)
        late.close()
        h_hi = sb("h_hi", [P, DC, NT], F32R)
        h_lo = sb("h_lo", [P, DC, NT], F32R)
        KMAX = 12
        w_raw = sb("w_raw", [P, 2, KMAX * P])
        w_hi = sb("w_hi", [P, 2, KMAX * P], F32R)
        w_lo = sb("w_lo", [P, 2, KMAX * P], F32R)
        ident = sb("ident", [P, P])
        ones = sb("ones", [P, P])
        ones_bf = sb("ones_bf", [P, 2], BF16)
        var = sb("var", [P, 2, TT])
        rms = sb("rms", [P, TT])
        par = sb("par", [P, 2, P])
        cs = sb("cs", [P, 2 * DC])
        mod = sb("mod", [P, 2, MODC])
        amul = sb("amul", [P, 3, 2, DC])
        gate = sb("gate", [P, 3, 2, DC])
        pscl = sb("pscl", [P, 2, DC])
        pbia = sb("pbia", [P, 2, DC])
        rope_sb = sb("rope_sb", [P, QT, 2, DH])
        gqk = sb("gqk", [P, 4, DH])
        lam_sb = sb("lam_sb", [P, 4, DH])
        lam_s = sb("lam_s", [P, 4])
        nlam = sb("nlam", [P, 1])
        subg = sb("subg", [P, 1])
        eps4 = sb("eps4", [P, 4])
        nhalf = sb("nhalf", [P, TT])
        ss = sb("ss", [P, 2, 4])
        rr = sb("rr", [P, 2, 4])
        mx = sb("mx", [P, 2])
        nm = sb("nm", [P, 2, 2])
        zz = sb("zz", [P, 2, 2])
        rz = sb("rz", [P, 2])
        ovar = sb("ovar", [P, QT])
        orms = sb("orms", [P, QT])
        edge_sb = sb("edge_sb", [P, len(WINDOWS), 4, PAD])

        ffn = ExitStack()
        a_hi = sb("a_hi", [P, FP, NT], F32R, ffn)
        a_lo = sb("a_lo", [P, FP, NT], F32R, ffn)
        ffn.close()
        a_hi_f32 = a_hi[:].bitcast(F32)
        setup = ExitStack()
        xstage = sb("xstage", [P, TT, D], F32, setup)
        pstage = sb("pstage", [P, 2, P], F32, setup)
        cstage = sb("cstage", [2 * DC, P], F32, setup)
        first_own = sb("first_own", [P, ADA_OWN, DC, ADA_COLS], F32, setup)
        first_acc = sb("first_acc", [P, len(FIRST_DVE), 2, ADA_COLS], F32, setup)
        setup.close()
        pool = ExitStack()
        LINE = PAD + NL + PAD + NX + PAD
        hp = sb("hp", [P, DC, LINE], F32, pool)
        win = sb("win", [P, 2, 2, LINE], F32, pool)
        pt = sb("pt", [P, 2, NT], F32, pool)
        po = sb("po", [P, 2, NT], F32, pool)
        pool.close()
        attn = ExitStack()
        oT = sb("oT", [P, HEADS, NL], F32, attn)
        rope_g = sb("rope_g", [P, 2, QT, 2, DH], F32, attn)
        aT_hi = sb("aT_hi", [P, TT, NL], F32R, attn)
        aT_lo = sb("aT_lo", [P, TT, NL], F32R, attn)
        vs_hi = sb("vs_hi", [P, TT, DV], F32R, attn)
        e = sb("e", [P, 2, 2, NT], F32, attn)
        qT_hi = sb("qT_hi", [P, NL], F32R, attn)
        qT_lo = sb("qT_lo", [P, NL], F32R, attn)
        kT_hi = sb("kT_hi", [P, NT], F32R, attn)
        kT_lo = sb("kT_lo", [P, NT], F32R, attn)
        vs_lo = sb("vs_lo", [P, TT, DV], F32R, attn)
        qkv = sb("qkv", [P, TT, 3 * DV], F32, attn)
        a = sb("a", [P, NT], F32, attn)
        qk_sq = sb("qk_sq", [P, 2, 2 * DV], F32, attn)
        qk_c = sb("qk_c", [P, 2 * DV], F32, attn)
        qk_s = sb("qk_s", [P, 2 * DV], F32, attn)
        ob = sb("ob", [P, NL], F32, attn)
        attn.close()
        over = ExitStack()
        stack.enter_context(over)
        a_hold = sb("a_hold", [P, 2 * FP * NT], F32, over)
        sil = sb("sil", [P, NT])
        prod = sb("prod", [P, NT])
        ada = ExitStack()
        ada_raw = sb("ada_raw", [P, 2, DC // 2, ADA_COLS], F32, ada)
        ada_acc = sb("ada_acc", [P, 2, ADA_COLS], F32, ada)
        ada.close()
        sq = sb("sq", [P, 2, NT])
        sqa = sb("sqa", [P, NT])
        xn = sb("xn", [P, 2, NT])
        ada_parts = sb("ada_parts", [P, PARTS3, 2 * ADA_COLS], BF16)
        diag = sq[:, 0, :].rearrange("p (t c) -> p t c", c=P)

        first_raw = [first_own[:, u] for u in range(ADA_OWN)] + [first_h[:, u] for u in range(ADA_FIRST - ADA_OWN)]

        pu = stack.enter_context(nc.psum_tensor("pu", [P, 4, 512], F32))
        pv = stack.enter_context(nc.psum_tensor("pv", [P, 4, 512], F32))

        def ps(ch, s):
            return pu[:, ch, 0:NL] if s == 0 else pu[:, 2 + ch, 0:NX]

        def wo_banks(ch, s):
            return pv[:, ch, 0:NL]

        SEG = (slice(0, NL), slice(NL, NT))

        class Steps:

            def __init__(self, engine, sem_, base):
                self.engine, self.sem, self.base, self.n = engine, sem_, base, 0

            def __call__(self, i):
                self.n += 1
                i.then_inc(self.sem, 1)
                self.engine.wait_ge(self.sem, self.base + self.n)

        SUMS_TO = (1, 3, 6, 10)

        def window_sums(engine, who, step, j):
            src, size, length, b = hp[:, j, :], 1, LINE, 0
            while size < WINDOWS[j // 2]:
                length -= size
                step(engine.tensor_tensor(win[:, who, b, 0:length], src[:, 0:length], src[:, size:size + length], ALU.add))
                src, b, size = win[:, who, b, :], 1 - b, 2 * size
            return src

        def norm_rope(engine, step, t):
            g = 0 if t < QT else 2
            v = qkv[:, t, g * DH:2 * DV].rearrange("p (g d) -> p g d", d=DH)
            step(engine.tensor_tensor(v, v, rr[:, t % 2, g:4].unsqueeze(2).broadcast_to((P, 4 - g, DH)), ALU.mult))
            if t >= QT:
                engine.tensor_tensor(v, v, gqk[:, g:4, :], ALU.mult).then_inc(qk_ready, 1)
                return
            for w in range(2):
                c_ = qk_c[:, w * DV:(w + 1) * DV].rearrange("p (c d) -> p c d", d=DH)
                engine.tensor_tensor(c_, v[:, 2 * w:2 * w + 2, :], rope_g[:, w, t, 0:1, :].broadcast_to((P, 2, DH)), ALU.mult)
                x_ = qkv[:, t, w * DV:(w + 1) * DV].rearrange("p (c a b d) -> p c a b d", c=2, a=2, b=2)
                o_ = qk_s[:, w * DV:(w + 1) * DV].rearrange("p (c a b d) -> p c a b d", c=2, a=2, b=2)
                sn = rope_g[:, w, t, 1:2, :].rearrange("p c (a b d) -> p c a b d", a=2, b=2)
                for b in range(2):
                    last = engine.tensor_tensor(o_[:, :, :, b, :], x_[:, :, :, 1 - b, :],
                                                sn[:, :, :, b, :].broadcast_to((P, 2, 2, DH // 4)), ALU.mult)
            step(last)
            engine.tensor_tensor(qkv[:, t, 0:2 * DV], qk_c[:], qk_s[:], ALU.add).then_inc(qk_ready, 1)

        def copy_out(engine, done, run, t):
            j0, j1 = OUT_RUNS[run]
            engine.wait_ge(ot_done, QT * run + t + 1)
            src, dst = pv[:, t, 0:(j1 - j0) * P], ostage[:, t, j0 * P:j1 * P]
            i = engine.activation(dst, src, ACT.Copy) if done is not o_late[0] else engine.tensor_copy(dst, src)
            i.then_inc(done, 1)

        A_STEPS = 2 * QT + (TT - QT)
        B_STEPS = 5 * QT

        in_x = [sem(f"in_x{t}") for t in range(TT)]
        in_cond = sem("in_cond")
        in_par = sem("in_par")
        in_par2 = sem("in_par2")
        par_z = sem("par_z")
        par_t = sem("par_t")
        par_ready = sem("par_ready")
        cond_t = sem("cond_t")
        cs_ready = sem("cs_ready")
        xt_done = sem("xt_done")
        x_ready = sem("x_ready")
        first_in = [sem(f"first_in{i}") for i in range(ADA_FIRST)]
        first_step = sem("first_step")
        first_done = sem("first_done")
        ada_in = [sem(f"ada_in{i}") for i in range(2)]
        ada_half = [sem(f"ada_half{i}") for i in range(2)]
        ada_step = sem("ada_step")
        part_ready = sem("part_ready")
        rest_ready = sem("rest_ready")
        ada_red = sem("ada_red")
        mod_step = sem("mod_step")
        raw_ready = [sem(f"raw_ready{i}") for i in range(2)]
        hi_ready = [sem(f"hi_ready{i}") for i in range(2)]
        split_ready = [sem(f"split_ready{i}") for i in range(2)]
        unit_done = [sem(f"unit_done{i}") for i in range(2)]
        psum_used = [sem(f"psum_used{i}") for i in range(2)]
        acthi_ready = sem("acthi_ready")
        act_ready = sem("act_ready")
        sq_ready = sem("sq_ready")
        sqa_step = sem("sqa_step")
        psq_done = sem("psq_done")
        var_done = sem("var_done")
        var_part = sem("var_part")
        var_ready = sem("var_ready")
        rms_ready = sem("rms_ready")
        diag_ready = sem("diag_ready")
        rs_done = sem("rs_done")
        xn_ready = sem("xn_ready")
        hf_ready = sem("hf_ready")
        hhi_ready = sem("hhi_ready")
        h_ready = sem("h_ready")
        pad_ready = sem("pad_ready")
        win_step = sem("win_step")
        gp_win = sem("gp_win")
        d_ready = sem("d_ready")
        pt_ready = sem("pt_ready")
        const_ready = sem("const_ready")
        ot_done = sem("ot_done")
        o_early = sem("o_early")
        o_late = [sem(f"o_late{i}") for i in range(2)]
        out_done = sem("out_done")

        aw_ready = sem("aw_ready")
        aw_hi = sem("aw_hi")
        aw_split = sem("aw_split")
        qkv_done = sem("qkv_done")
        qkv_out = sem("qkv_out")
        qsq_ready = sem("qsq_ready")
        ss_ready = sem("ss_ready")
        rr_ready = sem("rr_ready")
        rr_step = sem("rr_step")
        rope_ready = sem("rope_ready")
        rope_step = sem("rope_step")
        qk_step = sem("qk_step")
        qk_ready = sem("qk_ready")
        tq_done = sem("tq_done")
        tq_hi = sem("tq_hi")
        tq_split = sem("tq_split")
        v_hi = sem("v_hi")
        v_split = sem("v_split")
        s_done = sem("s_done")
        nm_ready = sem("nm_ready")
        exp_done = sem("exp_done")
        mix_step = sem("mix_step")
        a_ready = sem("a_ready")
        ta_done = sem("ta_done")
        ta_hi = sem("ta_hi")
        ta_split = sem("ta_split")
        pv_done = sem("pv_done")
        oT_ready = sem("oT_ready")
        lam_step = sem("lam_step")
        osq_ready = sem("osq_ready")
        ostat_done = sem("ostat_done")
        ovar_ready = sem("ovar_ready")
        orms_ready = sem("orms_ready")
        odiag_ready = sem("odiag_ready")
        ors_done = sem("ors_done")
        on_ready = sem("on_ready")
        onh_ready = sem("onh_ready")
        on_split = sem("on_split")

        FIRST_BANK = [pu[:, b] for b in range(4)] + [pv[:, b] for b in (2, 3)]
        aw = [t[:].rearrange("p a b -> p (a b)").rearrange("p (k c) -> p k c", k=DC) for t in (w_raw, w_hi, w_lo)]
        HK = NT // 2

        def scores(c):
            return pu[:, 2 * c:2 * c + 2, 0:HK]

        OUT_RUNS = ((0, DC - 4), (DC - 4, DC - 2), (DC - 2, DC))
        EARLY = (DC - 2) * P
        N_COND, N_PAR, N_PAR2 = 3, 7, 7
        TQ = (("q", 0, QT, pv[:, 2]), ("k", 0, QT, pv[:, 3]), ("k", QT, TT, pu[:, 1]))

        def wslot(t, ch, k):
            return t[:, ch, 0:k * P].rearrange("p (k c) -> p k c", k=k)

        SQ_SUMS = DC - 2
        POOL_NORM = 2

        def sums_before(i):
            return SQ_SUMS * (i - (i > POOL_NORM))

        NORM_LAYER = (0, 0, 0, 1, 1, 1)
        NORM_K = (0, 1, 2, 0, 1, 2)
        NORM_N = (NT, NT, NT, NT, NT, NL)
        FFN_N = (NT, NT, NT, NL)
        FFN_NORM = (1, 3, 4)

        block = stack.enter_context(nc.Block())

        @block.sync
        def _(sp):
            xr = x.rearrange("b (t p) d -> p (b t) d", p=P)
            cr = ctx_in.rearrange("b (t p) d -> p (b t) d", p=P)
            for t in range(TT):
                sp.dma_start(xstage[:, t, :], xr[:, t] if t < QT else cr[:, t - QT]).then_inc(in_x[t], 16)
            first = ada_w[0].rearrange("(k p) (u n) -> p k u n", p=P, n=ADA_COLS)
            for u in range(ADA_FIRST):
                sp.dma_start(first_raw[u], first[:, :, u, :]).then_inc(first_in[u], 16)

            def load_granule(k, n):
                src = ada_w[k].rearrange("(b k p) (u n) -> p b k u n", p=P, b=2, n=ADA_COLS)
                u = n + ADA_N - ADA_COUNT[k]
                for b in range(2):
                    sp.wait_ge(ada_half[b], ADA_BASE[k] + n + 1)
                    sp.dma_start(ada_raw[:, b], src[:, b, :, u, :]).then_inc(ada_in[b], 16)

            def load_unit(ch, pair, dst, src):
                sp.wait_ge(split_ready[ch], pair + 1)
                sp.dma_start(dst, src).then_inc(raw_ready[ch], 16)

            def load_ffn(n):
                wi = w_in[n // 2, n % 2].rearrange("(k p) (u n) -> p k u n", p=P, n=P)
                wo = w_out[n // 2, n % 2].rearrange("(q k p) (m n) -> p q k m n", p=P, q=PARTS, n=P)
                def in_pair(q, f, ada):
                    for ch in range(2):
                        load_unit(ch, PAIR_FFN[n] + q * PART_PAIRS + f, wslot(w_raw, ch, DC),
                                  wi[:, :, ch * FC + q * FP + f, :])
                    if ada:
                        load_granule(n, q * PART_PAIRS + f - 1)

                def out_pair(q, m, ada):
                    for ch in range(2):
                        load_unit(ch, PAIR_FFN[n] + q * PART_PAIRS + FP + m, wslot(w_raw, ch, FP),
                                  wo[:, q, :, 2 * m + ch, :])
                    if ada:
                        load_granule(n, q * PART_PAIRS + FP + m - 1)
                for q in range(PARTS):
                    if q == 0 and ADA_COUNT[n]:
                        for f in range(2):
                            in_pair(0, f, False)
                        sp.wait_ge(h_ready, DC * (2 * n + 1))
                        load_granule(n, 0)
                    for lo, hi, ada in spans(n, q * PART_PAIRS, 2 if q == 0 and ADA_COUNT[n] else 0, FP):
                        with sp.Fori(lo, hi) as f:
                            in_pair(q, f, ada)
                    for lo, hi, ada in spans(n, q * PART_PAIRS + FP, 0, OUT_PAIRS):
                        with sp.Fori(lo, hi) as m:
                            out_pair(q, m, ada)

            load_ffn(0)
            for g in range(4):
                for ch in range(2):
                    load_unit(ch, PAIR_POOL + g, wslot(w_raw, ch, 2),
                              pool_w[0, g].rearrange("(k p) (o n) -> p k o n", p=P, n=P)[:, :, ch, :])
            load_ffn(1)
            load_ffn(2)
            for ch in range(2):
                sp.wait_ge(split_ready[ch], PAIR_WO + 1)
            wq = w_qkv[0].rearrange("(k p) (j h c) -> p k j h c", p=P, j=3, h=HEADS)
            for h in range(HEADS):
                if h:
                    sp.wait_ge(aw_split, 2 * h)
                for j in range(3):
                    sp.dma_start(aw[0][:, :, j * DV:(j + 1) * DV], wq[:, :, j, h, :]).then_inc(aw_ready, 16)
            sp.wait_ge(aw_split, 2 * HEADS)
            for m in range(4):
                for ch in range(2):
                    load_unit(ch, PAIR_WO + m, wslot(w_raw, ch, DC),
                              w_o[0].rearrange("(k p) (m n) -> p k m n", p=P, n=P)[:, :, 2 * m + ch, :])
            load_ffn(3)
            o = out.rearrange("b (t p) d -> p (b t) d", p=P)
            for t in range(QT):
                sp.wait_ge(o_early, QT + t + 1)
                sp.dma_start(o[:, t, 0:EARLY], ostage[:, t, 0:EARLY]).then_inc(out_done, 16)
            for t in range(QT):
                sp.wait_ge(o_late[t % 2], t // 2 + 1)
                sp.dma_start(o[:, t, EARLY:D], ostage[:, t, EARLY:D]).then_inc(out_done, 16)
            sp.wait_ge(out_done, 16 * 2 * QT)

        @block.gpsimd
        def _(gp):
            nc.gpsimd.memset(pstage[:], 0.0).then_inc(par_z, 1)
            nc.gpsimd.memset(ones[:], 1.0).then_inc(const_ready, 1)
            nc.gpsimd.memset(eps4[:], EPS).then_inc(const_ready, 1)
            nc.gpsimd.memset(nhalf[:], -0.5).then_inc(const_ready, 1)
            nc.gpsimd.memset(ones_bf[:], 1.0).then_inc(const_ready, 1)
            gp.wait_ge(const_ready, 4)

            def sum_chunks(i):
                n = NORM_N[i]

                def add(step, x0, x1):
                    if i or step:
                        gp.wait_ge(sqa_step, sums_before(i) + step)
                    nc.gpsimd.tensor_tensor(sqa[:, 0:n], x0, x1, ALU.add).then_inc(sqa_step, 1)
                gp.wait_ge(sq_ready, DC * i + 2)
                add(0, sq[:, 0, 0:n], sq[:, 1, 0:n])
                for m in range(1, DC // 2):
                    for ch in range(2 if m < DC // 2 - 1 else 1):
                        gp.wait_ge(sq_ready, DC * i + 2 * m + ch + 1)
                        add(2 * m - 1 + ch, sqa[:, 0:n], sq[:, ch, 0:n])
                if i == 1:
                    gp.wait_ge(unit_done[1], PAIR_POOL + 1)
                    nc.gpsimd.memset(hp[:, :, 0:PAD], 0.0)
                    nc.gpsimd.memset(hp[:, :, PAD + NL:2 * PAD + NL], 0.0)
                    nc.gpsimd.memset(hp[:, :, LINE - PAD:LINE], 0.0).then_inc(pad_ready, 1)
                inv_rms_tokens(i)

            def inv_rms_tokens(i):
                n = NORM_N[i]
                gp.wait_ge(var_ready, i + 1)
                nc.gpsimd.tensor_tensor(rms[:, 0:n // P], var[:, 1, 0:n // P], nhalf[:, 0:n // P], ALU.pow).then_inc(rms_ready, 1)

            def granule_rests(k):
                rest = ada_acc[:].rearrange("p s n -> p (s n)")
                with gp.Fori(0, ADA_COUNT[k]) as n:
                    c = ADA_BASE[k] + n
                    for i in range(PARTS3 - 1):
                        gp.wait_ge(part_ready, PARTS3 * c + i + 2)
                        nc.gpsimd.tensor_tensor(rest, rest, ada_parts[:, i, :], ALU.subtract).then_inc(rest_ready, 1)
            sum_chunks(0)
            granule_rests(0)
            sum_chunks(1)
            step = Steps(gp, gp_win, 0)
            for j in range(1, DC, 2):
                gp.wait_ge(hf_ready, j + 1)
                if j > 1:
                    gp.wait_ge(d_ready, j - 1)
                window_sums(nc.gpsimd, 1, step, j)
                for i in (j - 1, j):
                    gp.wait_ge(hhi_ready, DC + i + 1)
                    nc.gpsimd.tensor_tensor(h_lo[:, i, :], pt[:, i % 2, :], h_hi[:, i, :].bitcast(F32),
                                            ALU.subtract).then_inc(h_ready, 1)
            inv_rms_tokens(POOL_NORM)
            granule_rests(1)
            sum_chunks(3)
            sum_chunks(4)

            gp.wait_ge(in_par2, 16 * N_PAR2)
            gp.wait_ge(unit_done[1], PAIR_WO + 1)

            def halves(t):
                return t.rearrange("p t (a b d) -> p t a b d", a=2, b=2)
            for w in range(2):
                gain = gqk[:, 2 * w:2 * w + 1, :].broadcast_to((P, QT, DH))
                nc.gpsimd.tensor_tensor(rope_g[:, w, :, 0, :], rope_sb[:, :, 0, :], gain, ALU.mult).then_inc(rope_ready, 1)
                gain = gqk[:, 2 * w:2 * w + 1, :].rearrange("p t (a b d) -> p t a b d", a=2, b=2)
                for b in range(2):
                    nc.gpsimd.tensor_tensor(halves(rope_g[:, w, :, 1, :])[:, :, :, b, :],
                                            halves(rope_sb[:, :, 1, :])[:, :, :, b, :],
                                            gain[:, :, :, 1 - b, :].broadcast_to((P, QT, 2, DH // 4)),
                                            ALU.mult).then_inc(rope_ready, 1)
            gp.wait_ge(rope_ready, 6)

            def inv_rms(h, t):
                n = TT * h + t
                g = slice(0, 4) if t < QT else slice(2, 4)
                gp.wait_ge(ss_ready, n + 1)
                nc.gpsimd.tensor_tensor(ss[:, t % 2, g], ss[:, t % 2, g], eps4[:, g], ALU.add).then_inc(rr_step, 1)
                gp.wait_ge(rr_step, n + 1)
                nc.gpsimd.tensor_tensor(rr[:, t % 2, g], ss[:, t % 2, g], nhalf[:, g], ALU.pow).then_inc(rr_ready, 1)
                gp.wait_ge(rr_ready, n + 1)

            def out_rms(g):
                gp.wait_ge(ovar_ready, g + 1)
                nc.gpsimd.tensor_tensor(orms[:], ovar[:], nhalf[:, 0:QT], ALU.pow).then_inc(orms_ready, 1)

            def attn_pool(h, do_c):
                step = Steps(gp, qk_step, A_STEPS * h)
                for t in range(TT):
                    if t == TT - 1 and do_c:
                        out_rms(h - 2)
                    inv_rms(h, t)
                    norm_rope(nc.gpsimd, step, t)
            step = Steps(gp, qk_step, A_STEPS - (TT - QT))
            for t in range(TT):
                if t >= 2:
                    gp.wait_ge(rope_step, 2 * (min(t, QT + 1) - 1))
                inv_rms(0, t)
                if t >= QT:
                    norm_rope(nc.gpsimd, step, t)
            attn_pool(1, False)
            with gp.Fori(2, HEADS) as h:
                attn_pool(h, True)
            out_rms(HEADS - 2)
            out_rms(HEADS - 1)
            sum_chunks(5)

        @block.scalar
        def _(act):
            def split_hi(ch, pair, k):
                act.wait_ge(raw_ready[ch], 16 * (pair + 1))
                act.wait_ge(unit_done[ch], pair + 1)
                act.activation(w_hi[:, ch, 0:k * P], w_raw[:, ch, 0:k * P], ACT.Copy).then_inc(hi_ready[ch], 1)

            def first_part(k, n):
                c = ADA_BASE[k] + n
                act.wait_ge(ada_step, DC * (c + 1) + 1)
                act.wait_ge(ada_red, c + 1)
                act.activation(ada_parts[:, 0, :], ada_acc[:].rearrange("p s n -> p (s n)"), ACT.Copy).then_inc(part_ready, 1)

            def other_parts(k, n):
                for i in range(1, PARTS3):
                    act.wait_ge(rest_ready, 2 * (ADA_BASE[k] + n) + i)
                    act.activation(ada_parts[:, i, :], ada_acc[:].rearrange("p s n -> p (s n)"), ACT.Copy).then_inc(part_ready, 1)

            def silu_pair(pair, f, n, nxt, k, p, ada):
                if ada[1]:
                    other_parts(k, p - SUM_LAG)
                act.wait_ge(unit_done[0], pair + 2)
                for s in range(2 if n == NT else 1):
                    i = act.activation(sil[:, SEG[s]], ps(0, s), ACT.Silu)
                i.then_inc(psum_used[0], 1)
                split_hi(0, pair + 1, nxt)
                if ada[0]:
                    first_part(k, p - 1)
                split_hi(1, pair + 1, nxt)
                act.wait_ge(psum_used[1], pair + 2)
                act.activation(a_hi[:, f, 0:n], prod[:, 0:n], ACT.Copy).then_inc(acthi_ready, 1)

            def square(i, m, ch, chunk):
                n = NORM_N[i]
                if not (isinstance(m, int) and m == 0):
                    act.wait_ge(sqa_step, sums_before(i) + 2 * m - 1)
                act.activation(sq[:, ch, 0:n], xT[:, chunk, 0:n], ACT.Square).then_inc(sq_ready, 1)

            def square_out(i, pair, m):
                for ch in range(2):
                    act.wait_ge(psum_used[ch], pair + 2)
                    square(i, m, ch, 2 * m + ch if isinstance(m, int) else bass.ds(2 * m + ch, 1))

            def ffn_act(k, nxt):
                n = FFN_N[k]
                for q in range(PARTS):
                    b = PAIR_FFN[k] + q * PART_PAIRS
                    p0 = q * PART_PAIRS
                    for lo, hi, ada in spans(k, p0, 0, FP - 1, (1, SUM_LAG)):
                        with act.Fori(lo, hi) as f:
                            silu_pair(b + f, f, n, DC, k, p0 + f, ada)
                    silu_pair(b + FP - 1, FP - 1, n, FP, k, p0 + FP - 1, [beside(k, p0 + FP - 1, lag) for lag in (1, SUM_LAG)])
                    last = q == PARTS - 1
                    squares = last and k < 3

                    def out_pair(m, nxt_, ada):
                        p = p0 + FP + m
                        if ada[1]:
                            other_parts(k, p - SUM_LAG)
                        for ch in range(2):
                            if nxt_:
                                split_hi(ch, PAIR_FFN[k] + p + 1, nxt_)
                            if ada[0] and ch == 0:
                                first_part(k, p - 1)
                        if squares:
                            square_out(FFN_NORM[k], PAIR_FFN[k] + p, m)
                    out_pair(0, FP, [beside(k, p0 + FP, lag) for lag in (1, SUM_LAG)])
                    for lo, hi, ada in spans(k, p0 + FP, 1, OUT_PAIRS - 1, (1, SUM_LAG)):
                        with act.Fori(lo, hi) as m:
                            out_pair(m, FP, ada)
                    if k == 3 and last:
                        for run in range(2):
                            for t in range(QT):
                                copy_out(act, o_early, run, t)
                    out_pair(OUT_PAIRS - 1, nxt if last else DC, [beside(k, p0 + PART_PAIRS - 1, lag) for lag in (1, SUM_LAG)])

            def norm_act(i):
                L, k, n = NORM_LAYER[i], NORM_K[i], NORM_N[i]
                segs = 2 if n == NT else 1

                def shift(s, j):
                    return mod[:, s, 3 * k * DC + j:3 * k * DC + j + 1]
                for j in range(DC):
                    act.wait_ge(xn_ready, DC * i + j + 1)
                    for s in range(segs):
                        last = act.activation(h_hi[:, j, SEG[s]], xn[:, j % 2, SEG[s]], ACT.Identity, bias=shift(s, j))
                    last.then_inc(hhi_ready, 1)

            def pool_act():
                act.wait_ge(pad_ready, 1)
                for j in range(-2, DC):
                    if j + 2 < DC:
                        act.wait_ge(xn_ready, DC + j + 3)
                        for s, at in ((0, PAD), (1, 2 * PAD + NL)):
                            last = act.activation(hp[:, j + 2, at:at + (NL, NX)[s]], xn[:, j % 2, SEG[s]], ACT.Identity,
                                                  bias=mod[:, s, 3 * DC + j + 2:3 * DC + j + 3])
                        last.then_inc(hf_ready, 1)
                    if j >= 0:
                        act.wait_ge(d_ready, j + 1)
                        act.activation(h_hi[:, j, :], pt[:, j % 2, :], ACT.Copy).then_inc(hhi_ready, 1)
                    if j >= 3 and j % 2:
                        out_group(j // 2 - 1)

            def pool_squares(g):
                for m in (2 * g, 2 * g + 1):
                    act.wait_ge(pt_ready, m + 1)
                    if m >= 2:
                        act.wait_ge(psq_done, m - 1)
                    act.activation(sq[:, m % 2, :], xT[:, m, :], ACT.Square).then_inc(sq_ready, 1)

            def out_group(g):
                if g:
                    pool_squares(g - 1)
                for ch in range(2):
                    split_hi(ch, PAIR_POOL + g + 1, 2 if g < 3 else DC)
                for ch in range(2):
                    act.wait_ge(unit_done[ch], PAIR_POOL + g + 2)
                    m = 2 * g + ch
                    for s in range(2):
                        last = act.activation(po[:, ch, SEG[s]], ps(ch, s), ACT.Identity,
                                              scale=pscl[:, s, m:m + 1], bias=pbia[:, s, m:m + 1])
                    last.then_inc(psum_used[ch], 1)

            def project_act(h, t):
                n = TT * h + t
                act.wait_ge(qkv_done, n + 1)
                if not (isinstance(h, int) and h == 0):
                    act.wait_ge(tq_done, 3 * h)
                    act.wait_ge(v_split, h)
                at = 0 if t < QT else DV
                bank = FIRST_BANK[t] if isinstance(h, int) and h == 0 else pv[:, t % 2]
                act.activation(qkv[:, t, at:], bank[:, at:3 * DV], ACT.Copy).then_inc(qkv_out, 1)
                act.wait_ge(qkv_out, n + 1)
                if not (isinstance(h, int) and h == 0 and t < 2):
                    act.wait_ge(ss_ready, n - 1)
                act.activation(qk_sq[:, t % 2, at:2 * DV], qkv[:, t, at:2 * DV], ACT.Square,
                               scale=DH ** -0.5).then_inc(qsq_ready, 1)

            def exp_act(g, i):
                n = QT * g + i
                act.wait_ge(a_ready, n + 1)
                for c in range(2):
                    act.wait_ge(nm_ready, 2 * n + c + 1)
                    act.activation(e[:, i % 2, c, :].rearrange("p (b k) -> p b k", b=2), scores(c), ACT.Exp,
                                   scale=DH ** -0.5, bias=nm[:, i % 2, c:c + 1],
                                   accum_out=zz[:, i % 2, c:c + 1]).then_inc(exp_done, 1)

            def weights_hi(g, i):
                for b in range(2):
                    act.wait_ge(ta_done, 2 * (QT * g + i) + b + 2)
                    act.activation(aT_hi[:, 3 * b:3 * b + 3, i * P:(i + 1) * P],
                                   pv[:, 2 + b, 0:3 * P].rearrange("p (k q) -> p k q", k=3), ACT.Copy).then_inc(ta_hi, 1)

            def head_w_hi(h):
                act.wait_ge(aw_ready, 48 * (h + 1))
                for b in range(2):
                    k = slice(b * DC // 2, (b + 1) * DC // 2)
                    act.activation(aw[1][:, k, :], aw[0][:, k, :], ACT.Copy).then_inc(aw_hi, 1)

            def out_square(g):
                act.wait_ge(oT_ready, g + 2)
                act.wait_ge(ors_done, g + 1)
                act.activation(ob[:], oT[:, bass.ds(g, 1), :].rearrange("p o q -> p (o q)"), ACT.Square).then_inc(osq_ready, 1)

            def out_hi(g):
                act.wait_ge(on_ready, g + 3)
                act.activation(h_hi[:, g, 0:NL], oT[:, g, :], ACT.Copy).then_inc(onh_ready, 1)

            def attn_act(h, do_a, do_b, do_c):
                g = h - 1
                if do_c:
                    out_square(h - 2)
                if not do_a:
                    act.wait_ge(qkv_done, TT * HEADS)
                for s in range(TT):
                    if do_a:
                        project_act(h, s)
                    if do_b and 1 <= s <= QT:
                        weights_hi(g, s - 1)
                    if do_b and s < QT:
                        exp_act(g, s)
                    if not do_a and s < 2:
                        split_hi(s, PAIR_WO, DC)
                    if not do_a:
                        out_hi(s)
                if do_a:
                    if not (isinstance(h, int) and h == HEADS - 1):
                        act.wait_ge(qkv_done, TT * (h + 1))
                        head_w_hi(h + 1)
                if do_b:
                    act.wait_ge(pv_done, g + 1)
                    act.activation(oT[:, bass.ds(g, 1), :].rearrange("p o q -> p (o q)"), pu[:, 0, :],
                                   ACT.Copy).then_inc(oT_ready, 1)
                if do_a:
                    for b, (w, t0, t1, bank) in enumerate(TQ):
                        act.wait_ge(tq_done, 3 * h + b + 1)
                        dst = qT_hi if w == "q" else kT_hi
                        act.activation(dst[:, t0 * P:t1 * P], bank[:, 0:(t1 - t0) * P], ACT.Copy).then_inc(tq_hi, 1)
                    act.activation(vs_hi[:], qkv[:, :, 2 * DV:], ACT.Copy).then_inc(v_hi, 1)

            act.dma_start(ident[:], ident_in).then_inc(in_cond, 16)
            act.dma_start(cstage[0:DC, :], c.rearrange("a (r q) -> (a r) q", q=P)).then_inc(in_cond, 16)
            act.dma_start(cstage[DC:2 * DC, :], c_ctx.rearrange("(r q) -> r q", q=P)).then_inc(in_cond, 16)
            act.wait_ge(par_z, 1)

            def rows(t, r, a_):
                act.dma_start(pstage[r:r + a_.shape[0], t, :], a_).then_inc(in_par, 16)
            for L in range(2):
                rows(L, C_ADA_B, ada_b[L].rearrange("(r q) -> r q", q=P))
                rows(L, C_NORM_G, norm_g[L].rearrange("k (r q) -> (k r) q", q=P))
            rows(0, C_POOL_S, pool_scale.rearrange("a (r q) -> (a r) q", q=P))
            rows(1, C_POOL_B, pool_b.rearrange("a g (r q) -> (a g r) q", q=P))
            rows(1, C_SUB_G, sub_g)
            act.wait_ge(cond_t, 1)
            act.activation(cs[:], pv[:, 3, 0:2 * DC], ACT.Silu).then_inc(cs_ready, 1)
            act.dma_start(edge_sb[:], edge.rearrange("g s e -> (g s e)").partition_broadcast(P)
                          .rearrange("p (g s e) -> p g s e", g=len(WINDOWS), s=4)).then_inc(in_par2, 16)
            act.dma_start(rope_sb[:], rope.rearrange("t p a d -> p t a d")).then_inc(in_par2, 16)
            for i in range(4):
                act.dma_start(gqk[:, i, :], qk_g[0, i // 2].partition_broadcast(P)).then_inc(in_par2, 16)
            act.dma_start(lam_sb[:], lam_p[0].rearrange("a d -> (a d)").partition_broadcast(P)
                          .rearrange("p (a d) -> p a d", a=4)).then_inc(in_par2, 16)

            act.sem_inc(exp_done, 4)
            act.sem_inc(oT_ready, 1)
            for m in range(DC // 2):
                for ch in range(2):
                    act.wait_ge(x_ready, 2 * m + ch + 1)
                    square(0, m, ch, 2 * m + ch)
            for ch in range(2):
                split_hi(ch, 0, DC)
            norm_act(0)
            ffn_act(0, 2)
            pool_act()
            out_group(3)
            pool_squares(3)
            norm_act(2)
            ffn_act(1, DC)
            norm_act(3)
            ffn_act(2, None)
            act.wait_ge(lam_step, 2)
            act.activation(lam_s[:, 2:4], lam_s[:, 0:2], ACT.Exp).then_inc(lam_step, 1)
            for ch in range(2):
                act.wait_ge(unit_done[ch], PAIR_WO + 1)
            head_w_hi(0)
            norm_act(4)
            attn_act(0, True, False, False)
            attn_act(1, True, True, False)
            with act.Fori(2, HEADS - 1) as h:
                attn_act(h, True, True, True)
            attn_act(HEADS - 1, True, True, True)
            attn_act(HEADS, False, True, True)
            out_square(HEADS - 1)
            out_hi(TT)
            out_hi(TT + 1)
            for m in range(OUT_PAIRS):
                for ch in range(2):
                    split_hi(ch, PAIR_WO + m + 1, DC)
                square_out(5, PAIR_WO + m, m)
            norm_act(5)
            ffn_act(3, None)
            for t in range(1, QT, 2):
                copy_out(act, o_late[1], 2, t)

        @block.tensor
        def _(pe):
            def chunk(ch, j, k, x_hi, x_lo, n, banks=ps):
                hi, lo = wslot(w_hi, ch, k), wslot(w_lo, ch, k)
                for i, (w, r) in enumerate(((hi, x_hi), (hi, x_lo), (lo, x_hi))):
                    for s_ in range(2 if n == NT else 1):
                        last = pe.matmul(banks(ch, s_), w[:, j, :], r[:, SEG[s_]], start=(j == 0 and i == 0),
                                         stop=(j == k - 1 and i == 2))
                return last

            def unit(ch, pair, k, rhs_hi, rhs_lo, n, acts=None):
                pe.wait_ge(split_ready[ch], pair + 2)
                pe.wait_ge(psum_used[ch], pair + 1)
                if acts is not None:
                    pe.wait_ge(act_ready, acts)
                for j in range(k):
                    if acts is not None and j == k - 1:
                        pe.wait_ge(act_ready, acts + 1)
                    last = chunk(ch, j, k, rhs_hi(j), rhs_lo(j), n)
                last.then_inc(unit_done[ch], 1)

            def reduce_granule(k, n):
                pe.wait_ge(part_ready, PARTS3 * (ADA_BASE[k] + n + 1) + 1)
                for m in range(ADA_CH):
                    for s_ in range(2):
                        col = 2 * (ADA_CH * (n + ADA_N - ADA_COUNT[k]) + m) + s_
                        for i in range(PARTS3):
                            part = ada_parts[:, i, (ADA_CH * s_ + m) * P:(ADA_CH * s_ + m + 1) * P]
                            last = pe.matmul(pv[:, 2, bass.ds(col, 1)], part,
                                             ones_bf[:, 0:1], start=(i == 0), stop=(i == PARTS3 - 1))
                last.then_inc(ada_red, 1)

            def turn_out(run):
                j0, j1 = OUT_RUNS[run]
                for ch in range(2):
                    pe.wait_ge(psum_used[ch], PAIRS - 1 + run)
                for t in range(QT):
                    if run:
                        pe.wait_ge(o_early, QT * (run - 1) + t + 1)
                    for j in range(j0, j1):
                        last = pe.transpose(pv[:, t, (j - j0) * P:(j - j0 + 1) * P], xT[:, j, t * P:(t + 1) * P], ident[:])
                    last.then_inc(ot_done, 1)

            def ffn_pe(k):
                n = FFN_N[k]
                for q in range(PARTS):
                    b = PAIR_FFN[k] + q * PART_PAIRS
                    first = 0
                    if q == 0:
                        i = (0, 2, 3, 5)[k]
                        for ch in range(2):
                            pe.wait_ge(split_ready[ch], b + 2)
                            pe.wait_ge(psum_used[ch], b + 1)
                        for j in range(DC):
                            pe.wait_ge(h_ready, DC * i + j + 1)
                            for ch in range(2):
                                last = chunk(ch, j, DC, h_hi[:, j], h_lo[:, j], n)
                                if j == DC - 1:
                                    last.then_inc(unit_done[ch], 1)
                        first = 1
                    for lo, hi, ada in spans(k, q * PART_PAIRS, first, FP, SUM_LAG):
                        with pe.Fori(lo, hi) as f:
                            for ch in range(2):
                                unit(ch, b + f, DC, lambda j: h_hi[:, j], lambda j: h_lo[:, j], n)
                            if ada:
                                reduce_granule(k, q * PART_PAIRS + f - SUM_LAG)
                    def out_pair(m, ada, wait_mod=0, amid=None):
                        for ch in range(2):
                            if ch and amid:
                                amid()
                            unit(ch, b + FP + m, FP, lambda j: a_hi[:, j], lambda j: a_lo[:, j], n,
                                 acts=k * FC + q * FP + FP)
                        if wait_mod:
                            pe.wait_ge(mod_step, wait_mod)
                        if ada:
                            reduce_granule(k, q * PART_PAIRS + FP + m - SUM_LAG)
                    first = k == 0 and q == 0
                    if first:
                        out_pair(0, beside(k, FP, SUM_LAG), 3)
                    final = k == 3 and q == PARTS - 1
                    for lo, hi, ada in spans(k, q * PART_PAIRS + FP, int(first), OUT_PAIRS - int(final), SUM_LAG):
                        with pe.Fori(lo, hi) as m:
                            out_pair(m, ada)
                    if final:
                        turn_out(0)
                        out_pair(OUT_PAIRS - 1, False, amid=lambda: turn_out(1))
                        turn_out(2)

            def norm_pe(i):
                norm_sums(i)
                norm_spread(i)

            def norm_sums(i):
                n = NORM_N[i]
                pe.wait_ge(sqa_step, sums_before(i) + SQ_SUMS)
                for t in range(n // P):
                    pe.matmul(pv[:, 0, t:t + 1], sqa[:, t * P:(t + 1) * P], ones[:, 0:1], start=True, stop=True)
                pe.wait_ge(sq_ready, DC * (i + 1))
                for t in range(n // P):
                    last = pe.matmul(pv[:, 0, TT + t:TT + t + 1], sq[:, 1, t * P:(t + 1) * P], ones[:, 0:1], start=True, stop=True)
                last.then_inc(var_done, 1)

            def norm_spread(i):
                n = NORM_N[i]
                for s_ in range(2 if n == NT else 1):
                    pe.wait_ge(diag_ready, 2 * i + s_ + 1)
                    pe.matmul((pv[:, 0, 0:NL], pv[:, 1, 0:NX])[s_], ones[:], sq[:, 0, SEG[s_]], start=True,
                              stop=True).then_inc(rs_done, 1)

            def first_products(i):
                u, m1 = FIRST_PE[i]
                pe.wait_ge(first_in[u], 16)
                for m in range(m1):
                    c0 = 2 * (ADA_CH * u + m)
                    for j in range(DC):
                        last = pe.matmul(pv[:, 2, c0:c0 + 2], first_raw[u][:, j, m * P:(m + 1) * P],
                                         cs[:, j::DC], start=(j == 0), stop=(j == DC - 1))
                last.then_inc(first_done, 1)

            def first_sums(i):
                u, m0 = FIRST_DVE[i]
                pe.wait_ge(first_step, DC * (i + 1))
                for m in range(m0, ADA_CH):
                    c0 = 2 * (ADA_CH * u + m)
                    for s_ in range(2):
                        last = pe.matmul(pv[:, 2, c0 + s_:c0 + s_ + 1], first_acc[:, i, s_, m * P:(m + 1) * P],
                                         ones[:, 0:1], start=True, stop=True)
                last.then_inc(first_done, 1)

            def project_first():
                for j in range(DC):
                    pe.wait_ge(h_ready, 4 * DC + j + 1)
                    if j % (DC // 2) == 0:
                        pe.wait_ge(aw_split, 1 + j // (DC // 2))
                    for t in range(TT):
                        at = 0 if t < QT else DV
                        for i, (x_, w_) in enumerate(((h_hi, 1), (h_hi, 2), (h_lo, 1))):
                            last = pe.matmul(FIRST_BANK[t][:, at:3 * DV], x_[:, j, t * P:(t + 1) * P], aw[w_][:, j, at:],
                                             start=(j == 0 and i == 0), stop=(j == DC - 1 and i == 2))
                        if j == DC - 1:
                            last.then_inc(qkv_done, 1)

            def project(h, t, j0=0, j1=DC):
                at = 0 if t < QT else DV
                if j0 == 0:
                    pe.wait_ge(qkv_out, TT * h + t - 1)
                for j in range(j0, j1):
                    if t == 0 and j % (DC // 2) == 0:
                        pe.wait_ge(aw_split, 2 * h + 1 + j // (DC // 2))
                    for i, (x_, w_) in enumerate(((h_hi, 1), (h_hi, 2), (h_lo, 1))):
                        last = pe.matmul(pv[:, t % 2, at:3 * DV], x_[:, j, t * P:(t + 1) * P], aw[w_][:, j, at:],
                                         start=(j == 0 and i == 0), stop=(j == DC - 1 and i == 2))
                if j1 == DC:
                    last.then_inc(qkv_done, 1)

            def score(g, i):
                for c in range(2):
                    pe.wait_ge(exp_done, 2 * (QT * g + i) + c + 3)
                    if i == 0:
                        pe.wait_ge(oT_ready, g + 1)
                        pe.wait_ge(on_ready, g + 1)
                        pe.wait_ge(tq_split, 3 * (g + 1))
                    d = slice(c * DH, (c + 1) * DH)
                    for b in range(2):
                        ks = slice(b * HK, (b + 1) * HK)
                        for n, (q_, k_) in enumerate(((qT_hi, kT_hi), (qT_hi, kT_lo), (qT_lo, kT_hi))):
                            last = pe.matmul(pu[:, 2 * c + b, 0:HK], q_[d, i * P:(i + 1) * P], k_[d, ks],
                                             start=(n == 0), stop=(n == 2))
                    last.then_inc(s_done, 1)

            def turn_weights(g, i):
                pe.wait_ge(a_ready, QT * g + i + 3)
                for b in range(2):
                    pe.wait_ge(ta_split, 2 * (QT * g + i) + b + 1)
                    for k in range(3):
                        last = pe.transpose(pv[:, 2 + b, k * P:(k + 1) * P], a[:, (3 * b + k) * P:(3 * b + k + 1) * P], ident[:])
                    last.then_inc(ta_done, 1)

            def values(g):
                pe.wait_ge(ta_split, 2 * QT * (g + 1) + 2)
                pe.wait_ge(v_split, g + 1)
                pe.wait_ge(exp_done, 2 * QT * (g + 1) + 4)
                for k in range(TT):
                    for n, (v_, a_) in enumerate(((vs_hi, aT_hi), (vs_hi, aT_lo), (vs_lo, aT_hi))):
                        last = pe.matmul(pu[:, 0, :], v_[:, k, :], a_[:, k, :], start=(k == 0 and n == 0),
                                         stop=(k == TT - 1 and n == 2))
                last.then_inc(pv_done, 1)

            def turn_qk(h):
                for b, (w, t0, t1, bank) in enumerate(TQ):
                    pe.wait_ge(qk_ready, TT if isinstance(h, int) and h == 0 else TT * h + t1)
                    for t in range(t0, t1):
                        c0 = 0 if w == "q" else DV
                        last = pe.transpose(bank[:, (t - t0) * P:(t - t0 + 1) * P], qkv[:, t, c0:c0 + DV], ident[:])
                    last.then_inc(tq_done, 1)

            def out_sums(g):
                pe.wait_ge(osq_ready, g + 1)
                pe.wait_ge(exp_done, 2 * QT * (h_of(g) + 1) + 4)
                for t in range(QT):
                    last = pe.matmul(pu[:, 3, t:t + 1], ob[:, t * P:(t + 1) * P], ones[:, 0:1], start=True, stop=True)
                last.then_inc(ostat_done, 1)

            def h_of(g):
                return g if isinstance(g, int) and g == HEADS - 1 else g + 1

            def out_spread(g):
                pe.wait_ge(odiag_ready, g + 1)
                pe.matmul(pu[:, 2, :], ones[:], ob[:], start=True, stop=True).then_inc(ors_done, 1)

            WO_BESIDE = ((), (), (0, 1), (2,), (3,))

            def out_chunk(j):
                if j == 0:
                    pe.wait_ge(qkv_out, TT * HEADS)
                    for ch in range(2):
                        pe.wait_ge(split_ready[ch], PAIR_WO + 2)
                pe.wait_ge(on_split, j + 1)
                for ch in range(2):
                    last = chunk(ch, j, DC, h_hi[:, j], h_lo[:, j], NL, wo_banks)
                    if j == HEADS - 1:
                        last.then_inc(unit_done[ch], 1)

            def attn_pe(h, do_b, do_a, do_c):
                g = h - 1
                for s in range(TT - 1):
                    if do_a:
                        project(h, s)
                    if do_c and s == QT:
                        out_sums(h - 2)
                    if do_a and s == QT:
                        project(h, TT - 1, 0, DC // 2)
                    if do_b and s < QT:
                        score(g, s)
                    if do_b and 1 <= s <= QT:
                        turn_weights(g, s - 1)
                    if not do_a:
                        for j in WO_BESIDE[s]:
                            out_chunk(j)
                if do_a:
                    project(h, TT - 1, DC // 2, DC)
                if do_b:
                    values(g)
                if do_c:
                    out_spread(h - 2)
                if do_a:
                    turn_qk(h)

            pe.sem_inc(ors_done, 1)
            for ch in range(2):
                pe.sem_inc(unit_done[ch], 1)
            pe.sem_inc(ta_done, 1)
            pe.sem_inc(ada_red, 1)
            pe.wait_ge(in_cond, N_COND * 16)
            pe.transpose(pv[:, 3, 0:2 * DC], cstage[:], ident[0:2 * DC, 0:2 * DC]).then_inc(cond_t, 1)
            for j in range(DC):
                if j >= 2:
                    pe.wait_ge(x_ready, j - 1)
                for t in range(TT):
                    if j == 0:
                        pe.wait_ge(in_x[t], 16)
                    o = ps(j % 2, 0)[:, t * P:(t + 1) * P] if t < QT else ps(j % 2, 1)[:, (t - QT) * P:(t - QT + 1) * P]
                    last = pe.transpose(o, xstage[:, t, j * P:(j + 1) * P], ident[:])
                last.then_inc(xt_done, 1)
            pe.wait_ge(cs_ready, 1)
            pe.wait_ge(const_ready, 4)
            first_products(0)
            pe.wait_ge(in_par, N_PAR * 16)
            for t in range(2):
                last = pe.transpose(pv[:, 3, t * P:(t + 1) * P], pstage[:, t, :], ident[:])
            last.then_inc(par_t, 1)
            first_sums(0)
            first_products(1)
            norm_sums(0)
            first_sums(1)
            first_products(2)
            norm_spread(0)
            first_sums(2)
            first_sums(3)
            ffn_pe(0)
            norm_pe(1)
            for g in range(5):
                if g < 4:
                    pe.wait_ge(h_ready, DC + 2 * g + 2)
                    for ch in range(2):
                        unit(ch, PAIR_POOL + g, 2, lambda j: h_hi[:, 2 * g + j], lambda j: h_lo[:, 2 * g + j], NT)
                for m in (2 * g - 2, 2 * g - 1) if g else ():
                    pe.wait_ge(sq_ready, DC * POOL_NORM + m + 1)
                    for t in range(TT):
                        last = pe.matmul(pv[:, 3, TT * m + t:TT * m + t + 1], sq[:, m % 2, t * P:(t + 1) * P], ones[:, 0:1],
                                         start=True, stop=True)
                    last.then_inc(psq_done, 1)
            norm_spread(POOL_NORM)
            ffn_pe(1)
            norm_pe(3)
            ffn_pe(2)
            norm_pe(4)
            project_first()
            pe.wait_ge(qkv_out, TT)
            turn_qk(0)
            attn_pe(1, True, True, False)
            with pe.Fori(2, HEADS) as h:
                attn_pe(h, True, True, True)
            attn_pe(HEADS, True, False, True)
            out_chunk(4)
            out_sums(HEADS - 1)
            out_chunk(5)
            out_chunk(6)
            out_spread(HEADS - 1)
            out_chunk(7)
            for m in range(1, OUT_PAIRS):
                for ch in range(2):
                    unit(ch, PAIR_WO + m, DC, lambda j: h_hi[:, j], lambda j: h_lo[:, j], NL)
            norm_pe(5)
            ffn_pe(3)

        @block.vector
        def _(dve):
            def split_lo(ch, pair, k):
                dve.wait_ge(hi_ready[ch], pair + 1)
                dve.tensor_tensor(w_lo[:, ch, 0:k * P], w_raw[:, ch, 0:k * P], w_hi[:, ch, 0:k * P].bitcast(F32),
                                  ALU.subtract).then_inc(split_ready[ch], 1)

            def half_granule(k, n, b):
                c = ADA_BASE[k] + n
                dve.wait_ge(ada_in[b], 16 * (c + 1))
                for i in range(DC // 2):
                    j = b * DC // 2 + i
                    if j == 0:
                        dve.wait_ge(part_ready, PARTS3 * c + 1)
                    dve.wait_ge(ada_step, DC * c + j + 1)
                    for s_ in range(2):
                        w = cs[:, s_ * DC + j:s_ * DC + j + 1]
                        if j == 0:
                            last = dve.tensor_scalar(ada_acc[:, s_, :], ada_raw[:, b, i, :], w, None, ALU.mult)
                        else:
                            last = dve.scalar_tensor_tensor(ada_acc[:, s_, :], ada_raw[:, b, i, :], w, ada_acc[:, s_, :],
                                                            ALU.mult, ALU.add)
                    last.then_inc(ada_step, 1)
                dve.wait_ge(ada_step, DC * c + (b + 1) * DC // 2 + 1)
                dve.sem_inc(ada_half[b], 1)

            def mul_pair(k, pair, count, f, n, nxt, granule=None):
                if granule is not None:
                    half_granule(k, granule, 0)
                split_lo(0, pair + 1, nxt)
                if granule is not None:
                    half_granule(k, granule, 1)
                dve.wait_ge(unit_done[1], pair + 2)
                dve.wait_ge(psum_used[0], pair + 2)
                dve.wait_ge(act_ready, count + 1)
                for s in range(2 if n == NT else 1):
                    last = dve.tensor_tensor(prod[:, SEG[s]], ps(1, s), sil[:, SEG[s]], ALU.mult)
                last.then_inc(psum_used[1], 1)
                split_lo(1, pair + 1, nxt)
                dve.wait_ge(acthi_ready, count + 1)
                dve.tensor_tensor(a_lo[:, f, 0:n], prod[:, 0:n], a_hi_f32[:, f, 0:n],
                                  ALU.subtract).then_inc(act_ready, 1)

            def add_out(ch, pair, m, gk, n, banks=ps):
                dve.wait_ge(unit_done[ch], pair + 2)
                for s in range(2 if n == NT else 1):
                    last = dve.scalar_tensor_tensor(xT[:, m, SEG[s]], banks(ch, s), gate[:, gk, s, m],
                                                    xT[:, m, SEG[s]], ALU.mult, ALU.add)
                last.then_inc(psum_used[ch], 1)

            def ffn_dve(k, nxt):
                n, gk = FFN_N[k], 2 * (k % 2)
                for q in range(PARTS):
                    b = PAIR_FFN[k] + q * PART_PAIRS
                    a_ = k * FC + q * FP
                    for lo, hi, ada in spans(k, q * PART_PAIRS, 0, FP - 1):
                        with dve.Fori(lo, hi) as f:
                            mul_pair(k, b + f, a_ + f, f, n, DC, q * PART_PAIRS + f - 1 if ada else None)
                    ada = beside(k, q * PART_PAIRS + FP - 1)
                    mul_pair(k, b + FP - 1, a_ + FP - 1, FP - 1, n, FP, q * PART_PAIRS + FP - 2 if ada else None)
                    if k == 0 and q == 0:
                        dve.wait_ge(ada_red, FP - 2 + 1)
                        add_bias(0, ADA_CH * ADA_FIRST, ADA_CH * (ADA_FIRST + FP - 2))
                        mod_link(gates(0, (0,)))
                    for lo, hi, ada in spans(k, q * PART_PAIRS + FP, 0, OUT_PAIRS - 1):
                        with dve.Fori(lo, hi) as m:
                            out_pair(k, q, b, m, [bass.ds(2 * m + ch, 1) for ch in range(2)], gk, n, FP, ada)
                    last = q == PARTS - 1
                    ada = beside(k, (q + 1) * PART_PAIRS - 1)
                    out_pair(k, q, b, OUT_PAIRS - 1, [slice(DC - 2 + ch, DC - 1 + ch) for ch in range(2)], gk, n,
                             nxt if last else DC, ada)

            def out_pair(k, q, b, m, chunks, gk, n, nxt, ada):
                if ada:
                    half_granule(k, q * PART_PAIRS + FP + m - 1, 0)
                    half_granule(k, q * PART_PAIRS + FP + m - 1, 1)
                for ch in range(2):
                    add_out(ch, b + FP + m, chunks[ch], gk, n)
                    if nxt:
                        split_lo(ch, b + FP + m + 1, nxt)

            def norm_dve(i):
                norm_rms(i)
                norm_chunks(i)

            def norm_rms(i):
                tt = NORM_N[i] // P
                dve.wait_ge(var_done, i + 1 - (i > POOL_NORM))
                dve.tensor_scalar(var[:, 0, 0:tt], pv[:, 0, 0:tt], 1.0 / D, EPS, ALU.mult, ALU.add).then_inc(var_part, 1)
                dve.wait_ge(var_part, i + 1)
                dve.scalar_tensor_tensor(var[:, 1, 0:tt], pv[:, 0, TT:TT + tt], 1.0 / D, var[:, 0, 0:tt], ALU.mult,
                                         ALU.add).then_inc(var_ready, 1)
                spread_rms(i)

            def spread_rms(i):
                tt = NORM_N[i] // P
                dve.wait_ge(rms_ready, i + 1)
                for t0, t1 in ((0, QT), (QT, tt))[:1 + (tt > QT)]:
                    dve.tensor_tensor(diag[:, t0:t1], ident[:].unsqueeze(1).broadcast_to((P, t1 - t0, P)),
                                      rms[:, t0:t1].unsqueeze(2).broadcast_to((P, t1 - t0, P)), ALU.mult).then_inc(diag_ready, 1)

            def norm_chunks(i):
                L, k, n = NORM_LAYER[i], NORM_K[i], NORM_N[i]
                segs = 2 if n == NT else 1

                def scale(j):
                    if j >= 2 and i == 1:
                        dve.wait_ge(hf_ready, j - 1)
                    elif j >= 2:
                        dve.wait_ge(h_ready, DC * i + j - 1)
                    for s_ in range(segs):
                        if j == 0:
                            dve.wait_ge(rs_done, 2 * i + s_ + 1)
                        last = dve.scalar_tensor_tensor(xn[:, j % 2, SEG[s_]], xT[:, j, SEG[s_]], amul[:, k, s_, j:j + 1],
                                                        (pv[:, 0, 0:NL], pv[:, 1, 0:NX])[s_], ALU.mult, ALU.mult)
                    last.then_inc(xn_ready, 1)
                scale(0)
                if i == 1:
                    scale(1)
                    for j in range(DC):
                        if j + 2 < DC:
                            scale(j + 2)
                        pool_chunk(j)
                        if j in (4, 6):
                            add_group(j // 2 - 2)
                    return
                for j in range(DC):
                    if j + 1 < DC:
                        scale(j + 1)
                    dve.wait_ge(hhi_ready, DC * i + j + 1)
                    for s_ in range(segs):
                        sh = 3 * k * DC + j
                        last = dve.scalar_tensor_tensor(h_lo[:, j, SEG[s_]], xn[:, j % 2, SEG[s_]],
                                                        mod[:, s_, sh:sh + 1], h_hi[:, j, SEG[s_]].bitcast(F32),
                                                        ALU.add, ALU.subtract)
                    last.then_inc(h_ready, 1)

            def add_group(g):
                for ch in range(2):
                    split_lo(ch, PAIR_POOL + g + 1, 2 if g < 3 else DC)
                for ch in range(2):
                    m = 2 * g + ch
                    dve.wait_ge(psum_used[ch], PAIR_POOL + g + 2)
                    dve.tensor_tensor(xT[:, m, :], xT[:, m, :], po[:, ch, :], ALU.add).then_inc(pt_ready, 1)

            win_sum = Steps(dve, win_step, 0)

            def pool_chunk(j):
                g = j // 2
                w = WINDOWS[g]
                if j % 2 == 0:
                    dve.wait_ge(hf_ready, j + 1)
                    src = window_sums(dve, 0, win_sum, j)
                else:
                    dve.wait_ge(gp_win, SUMS_TO[g])
                    src = win[:, 1, g % 2, :]
                lat, ctx = PAD - w // 2, 2 * PAD + NL - w // 2
                for e, at in enumerate((lat, lat + NL - PAD, ctx, ctx + NX - PAD)):
                    last = dve.tensor_tensor(src[:, at:at + PAD], src[:, at:at + PAD], edge_sb[:, g, e, :], ALU.mult)
                win_sum(last)
                if j >= 2:
                    dve.wait_ge(h_ready, DC + j - 1)
                for s, at, to in ((0, lat, PAD), (1, ctx, 2 * PAD + NL)):
                    m = (NL, NX)[s]
                    last = dve.scalar_tensor_tensor(pt[:, j % 2, SEG[s]], src[:, at:at + m], 1.0 / w, hp[:, j, to:to + m],
                                                    ALU.mult, ALU.subtract)
                last.then_inc(d_ready, 1)

            def add_bias(L, c0, c1):
                for s_ in range(2):
                    last = dve.tensor_tensor(mod[:, s_, c0:c1], pv[:, 2, 2 * c0 + s_:2 * c1:2], par[:, L, c0:c1], ALU.add)
                last.then_inc(mod_step, 1)
                mod_steps[0] += 1
                dve.wait_ge(mod_step, mod_steps[0])

            def gates(L, ks):
                for s_ in range(2):
                    for k in ks:
                        last = dve.tensor_scalar(gate[:, k, s_, :], mod[:, s_, (3 * k + 2) * DC:(3 * k + 3) * DC],
                                                 1.0 if k == 1 else 0.5, None, ALU.mult)
                return last

            def scales(L, ks):
                for s_ in range(2):
                    for k in ks:
                        last = dve.scalar_tensor_tensor(amul[:, k, s_, :], mod[:, s_, (3 * k + 1) * DC:(3 * k + 2) * DC], 1.0,
                                                        par[:, L, C_NORM_G + k * DC:C_NORM_G + (k + 1) * DC], ALU.add, ALU.mult)
                return last

            mod_steps = [0]

            def mod_link(i):
                i.then_inc(mod_step, 1)
                mod_steps[0] += 1
                dve.wait_ge(mod_step, mod_steps[0])

            def sum_squares(h, t):
                n = TT * h + t
                g = 0 if t < QT else 2
                dve.wait_ge(qsq_ready, n + 1)
                if not (isinstance(h, int) and h == 0 and t < 2):
                    dve.wait_ge(rr_ready, n - 1)
                dve.tensor_reduce(ss[:, t % 2, g:4], qk_sq[:, t % 2, g * DH:2 * DV].rearrange("p (g d) -> p g d", d=DH),
                                  AX.X, ALU.add).then_inc(ss_ready, 1)

            def row_max(step, g, i):
                for c in range(2):
                    n = 2 * (QT * g + i) + c
                    dve.wait_ge(s_done, n + 1)
                    step(dve.tensor_reduce(mx[:, c:c + 1], scores(c), AX.XY, ALU.max))
                    dve.wait_ge(exp_done, n + 1)
                    dve.tensor_scalar(nm[:, i % 2, c:c + 1], mx[:, c:c + 1], -DH ** -0.5, None, ALU.mult).then_inc(nm_ready, 1)

            def weights_lo(g, i):
                for b in range(2):
                    dve.wait_ge(ta_hi, 2 * (QT * g + i) + b + 1)
                    o = (slice(None), slice(3 * b, 3 * b + 3), slice(i * P, (i + 1) * P))
                    dve.tensor_tensor(aT_lo[o], pv[:, 2 + b, 0:3 * P].rearrange("p (k q) -> p k q", k=3),
                                      aT_hi[o].bitcast(F32), ALU.subtract).then_inc(ta_split, 1)

            def combine(step, g, i):
                n = QT * g + i
                dve.wait_ge(exp_done, 2 * n + 6)
                step(dve.reciprocal(rz[:], zz[:, i % 2, :]))
                step(dve.tensor_tensor(rz[:, 1:2], rz[:, 1:2], nlam[:], ALU.mult))
                step(dve.tensor_scalar(e[:, i % 2, 1, :], e[:, i % 2, 1, :], rz[:, 1:2], None, ALU.mult))
                dve.wait_ge(ta_done, 2 * n + 1)
                dve.scalar_tensor_tensor(a[:], e[:, i % 2, 0, :], rz[:, 0:1], e[:, i % 2, 1, :], ALU.mult,
                                         ALU.add).then_inc(a_ready, 1)
                dve.wait_ge(a_ready, n + 3)

            def head_w_lo(h, b):
                dve.wait_ge(aw_hi, 2 * h + b + 1)
                k = slice(b * DC // 2, (b + 1) * DC // 2)
                dve.tensor_tensor(aw[2][:, k, :], aw[0][:, k, :], aw[1].bitcast(F32)[:, k, :],
                                  ALU.subtract).then_inc(aw_split, 1)

            def out_var(g):
                dve.wait_ge(ostat_done, g + 1)
                dve.tensor_scalar(ovar[:], pu[:, 3, 0:QT], 1.0 / DV, EPS, ALU.mult, ALU.add).then_inc(ovar_ready, 1)

            def out_diag(g):
                dve.wait_ge(orms_ready, g + 1)
                dve.tensor_tensor(ob[:].rearrange("p (t c) -> p t c", c=P), ident[:].unsqueeze(1).broadcast_to((P, QT, P)),
                                  orms[:].unsqueeze(2).broadcast_to((P, QT, P)), ALU.mult).then_inc(odiag_ready, 1)

            def out_norm(g):
                dve.wait_ge(ors_done, g + 2)
                o = oT[:, bass.ds(g, 1), :].rearrange("p o q -> p (o q)")
                dve.scalar_tensor_tensor(o, o, subg[:], pu[:, 2, :], ALU.mult, ALU.mult).then_inc(on_ready, 1)

            def out_lo(g):
                dve.wait_ge(onh_ready, g + 1)
                dve.tensor_tensor(h_lo[:, g, 0:NL], oT[:, g, :], h_hi[:, g, 0:NL].bitcast(F32), ALU.subtract).then_inc(on_split, 1)

            rope_link = Steps(dve, rope_step, 0)

            def attn_dve(h, do_a, do_b, do_c):
                g = h - 1
                step = Steps(dve, mix_step, B_STEPS * g)
                for s in range(TT):
                    if isinstance(h, int) and h == 0 and 2 <= s:
                        dve.wait_ge(rr_ready, s - 1)
                        norm_rope(dve, rope_link, s - 2)
                    if do_c and s == TT - 1:
                        out_diag(h - 2)
                    if do_a:
                        sum_squares(h, s)
                    if do_c and s == QT:
                        out_var(h - 2)
                    if do_b and s < QT:
                        row_max(step, g, s)
                    if do_b and 1 <= s <= QT:
                        weights_lo(g, s - 1)
                    if do_b and s < QT:
                        combine(step, g, s)
                    if not do_a and s < 2:
                        split_lo(s, PAIR_WO, DC)
                    if not do_a and s < QT:
                        out_lo(s)
                more = do_a and not (isinstance(h, int) and h == HEADS - 1)
                if more:
                    head_w_lo(h + 1, 0)
                if do_c:
                    out_norm(h - 2)
                if more:
                    head_w_lo(h + 1, 1)
                if do_a:
                    for b, (w, t0, t1, bank) in enumerate(TQ):
                        dve.wait_ge(tq_hi, 3 * h + b + 1)
                        lo, hi = (qT_lo, qT_hi) if w == "q" else (kT_lo, kT_hi)
                        dve.tensor_tensor(lo[:, t0 * P:t1 * P], bank[:, 0:(t1 - t0) * P],
                                          hi[:, t0 * P:t1 * P].bitcast(F32), ALU.subtract).then_inc(tq_split, 1)
                    dve.wait_ge(v_hi, h + 1)
                    dve.tensor_tensor(vs_lo[:], qkv[:, :, 2 * DV:], vs_hi[:].bitcast(F32), ALU.subtract).then_inc(v_split, 1)

            for ch in range(2):
                dve.sem_inc(split_ready[ch], 1)
                dve.sem_inc(psum_used[ch], 1)
                dve.sem_inc(ada_half[ch], 1)
            dve.sem_inc(ada_step, 1)
            dve.sem_inc(part_ready, 1)
            dve.sem_inc(act_ready, 1)
            dve.sem_inc(a_ready, 2)
            dve.sem_inc(ta_split, 2)
            dve.sem_inc(on_ready, 2)
            dve.sem_inc(qk_step, A_STEPS - (TT - QT))
            for j in range(DC):
                dve.wait_ge(xt_done, j + 1)
                dve.tensor_copy(xT[:, j, 0:NL], ps(j % 2, 0))
                dve.tensor_copy(xT[:, j, NL:NT], ps(j % 2, 1)).then_inc(x_ready, 1)
            def first_share(i):
                u, m0 = FIRST_DVE[i]
                dve.wait_ge(first_in[u], 16)
                for j in range(DC):
                    if j:
                        dve.wait_ge(first_step, DC * i + j)
                    for s_ in range(2):
                        w, acc = cs[:, s_ * DC + j:s_ * DC + j + 1], first_acc[:, i, s_, m0 * P:]
                        raw = first_raw[u][:, j, m0 * P:]
                        if j == 0:
                            last = dve.tensor_scalar(acc, raw, w, None, ALU.mult)
                        else:
                            last = dve.scalar_tensor_tensor(acc, raw, w, acc, ALU.mult, ALU.add)
                    last.then_inc(first_step, 1)
            dve.wait_ge(cs_ready, 1)
            first_share(0)
            first_share(1)
            first_share(2)
            norm_rms(0)
            first_share(3)
            dve.wait_ge(par_t, 1)
            dve.tensor_copy(par[:], pv[:, 3, 0:2 * P].rearrange("p (t c) -> p t c", t=2)).then_inc(par_ready, 1)
            for ch in range(2):
                split_lo(ch, 0, DC)
            dve.wait_ge(par_ready, 1)
            dve.wait_ge(first_done, len(FIRST_DVE) + len(FIRST_PE))
            add_bias(0, 0, ADA_CH * ADA_FIRST)
            mod_link(scales(0, (0,)))
            norm_chunks(0)
            ffn_dve(0, 2)
            dve.wait_ge(ada_red, ADA_COUNT[0] + 1)
            add_bias(0, ADA_CH * (ADA_FIRST + FP - 2), MODC)
            mod_link(scales(0, (1, 2)))
            mod_link(gates(0, (1, 2)))
            for s_ in range(2):
                last = dve.tensor_tensor(pscl[:, s_, :], gate[:, 1, s_, :], par[:, 0, C_POOL_S:C_POOL_S + DC], ALU.mult)
            mod_link(last)
            for s_ in range(2):
                last = dve.tensor_tensor(pbia[:, s_, :], pscl[:, s_, :], par[:, 1, C_POOL_B:C_POOL_B + DC], ALU.mult)
            mod_link(last)
            dve.wait_ge(in_par2, 16 * N_PAR2)
            dve.tensor_tensor(lam_sb[:, 0::2, :], lam_sb[:, 0::2, :], lam_sb[:, 1::2, :], ALU.mult).then_inc(lam_step, 1)
            dve.wait_ge(lam_step, 1)
            dve.tensor_reduce(lam_s[:, 0:2], lam_sb[:, 0::2, :], AX.X, ALU.add).then_inc(lam_step, 1)
            dve.tensor_scalar(subg[:], par[:, 1, C_SUB_G:C_SUB_G + 1], 1.0 - LAM_INIT, None, ALU.mult)
            norm_dve(1)
            add_group(2)
            add_group(3)
            dve.wait_ge(psq_done, DC)
            dve.tensor_reduce(var[:, 0, :], pv[:, 3, 0:DC * TT].rearrange("p (m t) -> p t m", t=TT), AX.X,
                              ALU.add).then_inc(var_part, 1)
            dve.wait_ge(var_part, POOL_NORM + 1)
            dve.tensor_scalar(var[:, 1, :], var[:, 0, :], 1.0 / D, EPS, ALU.mult, ALU.add).then_inc(var_ready, 1)
            spread_rms(POOL_NORM)
            norm_chunks(POOL_NORM)
            ffn_dve(1, DC)
            dve.wait_ge(ada_red, ADA_COUNT[0] + ADA_COUNT[1] + 1)
            add_bias(1, 0, MODC)
            mod_link(scales(1, (0, 1, 2)))
            mod_link(gates(1, (0, 1, 2)))
            norm_dve(3)
            ffn_dve(2, None)
            dve.wait_ge(lam_step, 3)
            dve.tensor_tensor(nlam[:], lam_s[:, 3:4], lam_s[:, 2:3], ALU.subtract).then_inc(lam_step, 1)
            dve.wait_ge(lam_step, 4)
            dve.tensor_scalar(nlam[:], nlam[:], -LAM_INIT, None, ALU.add).then_inc(lam_step, 1)
            dve.wait_ge(lam_step, 5)
            norm_rms(4)
            for b in range(2):
                head_w_lo(0, b)
            norm_chunks(4)
            attn_dve(0, True, False, False)
            attn_dve(1, True, True, False)
            with dve.Fori(2, HEADS - 1) as h:
                attn_dve(h, True, True, True)
            attn_dve(HEADS - 1, True, True, True)
            attn_dve(HEADS, False, True, True)
            for j in range(QT, TT):
                out_lo(j)
            out_var(HEADS - 1)
            out_lo(TT)
            out_diag(HEADS - 1)
            out_norm(HEADS - 1)
            out_lo(TT + 1)
            for m in range(OUT_PAIRS):
                for ch in range(2):
                    add_out(ch, PAIR_WO + m, slice(2 * m + ch, 2 * m + ch + 1), 1, NL, ps if m else wo_banks)
                    split_lo(ch, PAIR_WO + m + 1, DC)
            norm_dve(5)
            ffn_dve(3, None)
            for t in range(0, QT, 2):
                copy_out(dve, o_late[0], 2, t)


_INS = ['x', 'ctx', 'c', 'c_ctx', 'ada_w', 'ada_b', 'norm_g', 'ffn_w_in', 'ffn_w_out', 'pool_w', 'pool_b',
        'pool_scale', 'diff_w_qkv', 'diff_qk_g', 'diff_lambda', 'diff_sub_g', 'diff_w_o']


def shape_constants():
    nf = DH // 4
    inv = (10000.0 ** (-np.arange(nf, dtype=np.float32) / np.float32(nf))).astype(np.float32)
    t = np.arange(NL)
    pos = np.stack([t // GRID_W, t % GRID_W], -1).astype(np.float32)
    ang = np.broadcast_to(pos[:, :, None, None] * inv, (NL, 2, 2, nf)).reshape(NL, DH)
    cos, sin = np.cos(ang).astype(np.float32), np.sin(ang).astype(np.float32)
    sin = sin.reshape(NL, 2, 2, nf) * np.array([-1, 1], np.float32)[:, None]
    rope = np.stack([cos, sin.reshape(NL, DH)], 1).reshape(QT, P, 2, DH)
    edge = np.ones((len(WINDOWS), 4, PAD), np.float32)
    for g, w in enumerate(WINDOWS):
        for s, n in enumerate((NL, NX)):
            t = np.arange(n)
            cnt = np.clip(t - w // 2 + w, 0, n) - np.clip(t - w // 2, 0, n)
            edge[g, 2 * s], edge[g, 2 * s + 1] = w / cnt[:PAD], w / cnt[-PAD:]
    return {'rope': rope.astype(np.float32), 'edge': edge, 'ident': np.eye(P, dtype=np.float32)}


def kernel(**inputs):
    import concourse.bacc as _bacc
    from concourse.bass_utils import run_bass_kernel_spmd as _run

    nc = _bacc.Bacc("TRN2", target_bir_lowering=False, num_devices=1)
    arrays, args = {}, []
    named = [(n, np.ascontiguousarray(inputs[n])) for n in _INS] + list(shape_constants().items())
    for name, a in named:
        arrays[f"in_{name}"] = a
        args.append(nc.dram_tensor(f"in_{name}", a.shape, mybir.dt.from_np(a.dtype), kind="ExternalInput").ap())
    out = nc.dram_tensor("out_0", (1, NL, D), F32, kind="ExternalOutput").ap()
    build(nc, *args, out)
    r = _run(nc, [arrays], core_ids=[0])
    return r.results[0]["out_0"]
```
